# Optimizing a Trainium2 kernel written in Bass

```python
import math
import jax, jax.numpy as jnp
from jax import lax
import numpy as np

D_MODEL = 1024
BATCH = 1
SEQ = 256
DEPTH = 2

CHUNK = 64
POOL_WIDTH = D_MODEL // 2
POOL_WINDOWS = (2, 4, 8, 16)
N_POOL_GROUPS = len(POOL_WINDOWS)
POOL_GROUP = POOL_WIDTH // N_POOL_GROUPS
SB_WIDTH = D_MODEL - POOL_WIDTH
SB_HEAD_DIM = 64
SB_HEADS = SB_WIDTH // SB_HEAD_DIM
Q_BLOCK = 128
IN_WIDTH = POOL_WIDTH + 3 * SB_WIDTH
D_FF = 2816
N_EXPERTS = 8
TOP_K = 2
EXPERT_FF = 2816
MOE_BLOCK = 256
N_DENSE = (DEPTH + 1) // 2
N_MOE = DEPTH // 2
DN_ALPHA = (2 * DEPTH) ** 0.25
DN_BETA = (8 * DEPTH) ** -0.25
LN_EPS = 1e-5


def layer_norm(x, g, b):
    xf = x.astype(jnp.float32)
    mu = jnp.mean(xf, axis=-1, keepdims=True)
    xc = xf - mu
    var = jnp.mean(xc * xc, axis=-1, keepdims=True)
    y = xc * lax.rsqrt(var + LN_EPS) * g.astype(jnp.float32) + b.astype(jnp.float32)
    return y.astype(x.dtype)

def pool_mixer(u, pool_w, pool_scale):
    B, S, _ = u.shape
    ug = u.astype(jnp.float32).reshape(B, S, N_POOL_GROUPS, POOL_GROUP)
    cs = jnp.cumsum(ug, axis=1)
    pos = jnp.arange(S)
    outs = []
    for gi, w in enumerate(POOL_WINDOWS):
        c = cs[:, :, gi]
        lagged = jnp.pad(c, ((0, 0), (w, 0), (0, 0)))[:, :S]
        cnt = jnp.minimum(pos + 1, w).astype(jnp.float32)[None, :, None]
        outs.append((c - lagged) / cnt - ug[:, :, gi])
    d = jnp.stack(outs, axis=2)
    y = jnp.einsum('bsgc,gcd->bsgd', d, pool_w.astype(jnp.float32))
    y = y.reshape(B, S, POOL_WIDTH) * pool_scale.astype(jnp.float32)
    return y.astype(u.dtype)

def stick_breaking_attention(q, k, v):
    S = q.shape[2]
    scale = 1.0 / math.sqrt(SB_HEAD_DIM)
    outs = []
    for blk in range(S // Q_BLOCK):
        start = blk * Q_BLOCK
        end = start + Q_BLOCK
        qb = q[:, :, start:end].astype(jnp.float32)
        kb = k[:, :, :end].astype(jnp.float32)
        vb = v[:, :, :end].astype(jnp.float32)
        z = jnp.einsum('bhtd,bhsd->bhts', qb, kb) * scale
        t_idx = start + jnp.arange(Q_BLOCK)[:, None]
        s_idx = jnp.arange(end)[None, :]
        mask = s_idx < t_idx
        log_1m_beta = jnp.where(mask, jax.nn.log_sigmoid(-z), 0.0)
        between = lax.cumsum(log_1m_beta, axis=3, reverse=True) - log_1m_beta
        att = jnp.where(mask, jnp.exp(jax.nn.log_sigmoid(z) + between), 0.0)
        outs.append(jnp.einsum('bhts,bhsd->bhtd', att, vb))
    return jnp.concatenate(outs, axis=2).astype(q.dtype)

def swiglu(x, wg, wu, wd):
    return (jax.nn.silu(x @ wg) * (x @ wu)) @ wd

def moe_ffn(x, router, wg, wu, wd):
    B, S, D = x.shape
    T = B * S
    A = T * TOP_K
    xf = x.reshape(T, D)
    logits = xf.astype(jnp.float32) @ router.astype(jnp.float32)
    top_logits, top_idx = lax.top_k(logits, TOP_K)
    gates = jax.nn.softmax(top_logits, axis=-1)
    flat_e = top_idx.reshape(-1)
    flat_tok = jnp.repeat(jnp.arange(T, dtype=jnp.int32), TOP_K)
    flat_g = gates.reshape(-1)
    order = jnp.argsort(flat_e)
    sorted_e = flat_e[order]
    counts = jnp.zeros((N_EXPERTS,), jnp.int32).at[flat_e].add(1)
    padded = ((counts + MOE_BLOCK - 1) // MOE_BLOCK) * MOE_BLOCK
    start = jnp.cumsum(counts) - counts
    pend = jnp.cumsum(padded)
    pstart = pend - padded
    rank = jnp.arange(A, dtype=jnp.int32) - start[sorted_e]
    dest = pstart[sorted_e] + rank
    n_slots = ((A + MOE_BLOCK - 1) // MOE_BLOCK) * MOE_BLOCK + N_EXPERTS * MOE_BLOCK
    n_blocks = n_slots // MOE_BLOCK
    slot_tok = jnp.zeros((n_slots,), jnp.int32).at[dest].set(flat_tok[order])
    slot_g = jnp.zeros((n_slots,), jnp.float32).at[dest].set(flat_g[order])
    block_e = jnp.minimum(
        jnp.searchsorted(pend, jnp.arange(n_blocks, dtype=jnp.int32) * MOE_BLOCK, side='right'),
        N_EXPERTS - 1)
    xs = xf[slot_tok].reshape(n_blocks, MOE_BLOCK, D)

    def expert_block(args):
        xb, e = args
        return swiglu(xb, wg[e], wu[e], wd[e])

    ys = lax.map(expert_block, (xs, block_e)).reshape(n_slots, D)
    out = jnp.zeros((T, D), jnp.float32).at[slot_tok].add(ys.astype(jnp.float32) * slot_g[:, None])
    return out.astype(x.dtype).reshape(B, S, D)

def first_inputs(seed: int = 0) -> dict:
    key = jax.random.key(seed)
    ks = jax.random.split(key, 24)
    f32 = jnp.float32
    nrm = lambda k, shape, s: jax.random.normal(k, shape, f32) * s
    x = jax.random.normal(ks[0], (BATCH, SEQ, D_MODEL), f32)
    ln_in_g = 1.0 + nrm(ks[1], (D_MODEL,), 0.02)
    ln_in_b = nrm(ks[2], (D_MODEL,), 0.02)
    w_in = nrm(ks[3], (DEPTH, D_MODEL, IN_WIDTH), D_MODEL ** -0.5)
    w_in = w_in.at[:, :, POOL_WIDTH + 2 * SB_WIDTH:].multiply(DN_BETA)
    pool_w = nrm(ks[4], (DEPTH, N_POOL_GROUPS, POOL_GROUP, POOL_GROUP), POOL_GROUP ** -0.5)
    pool_scale = 1.0 + nrm(ks[5], (DEPTH, POOL_WIDTH), 0.1)
    w_out = nrm(ks[6], (DEPTH, D_MODEL, D_MODEL), D_MODEL ** -0.5) * DN_BETA
    ln1_g = 1.0 + nrm(ks[7], (DEPTH, D_MODEL), 0.02)
    ln1_b = nrm(ks[8], (DEPTH, D_MODEL), 0.02)
    ffn_wg = nrm(ks[9], (N_DENSE, D_MODEL, D_FF), D_MODEL ** -0.5)
    ffn_wu = nrm(ks[10], (N_DENSE, D_MODEL, D_FF), D_MODEL ** -0.5)
    ffn_wd = nrm(ks[11], (N_DENSE, D_FF, D_MODEL), D_FF ** -0.5) * DN_BETA
    moe_router = nrm(ks[12], (N_MOE, D_MODEL, N_EXPERTS), D_MODEL ** -0.5)
    moe_wg = nrm(ks[13], (N_MOE, N_EXPERTS, D_MODEL, EXPERT_FF), D_MODEL ** -0.5)
    moe_wu = nrm(ks[14], (N_MOE, N_EXPERTS, D_MODEL, EXPERT_FF), D_MODEL ** -0.5)
    moe_wd = nrm(ks[15], (N_MOE, N_EXPERTS, EXPERT_FF, D_MODEL), EXPERT_FF ** -0.5) * DN_BETA
    ln2_g = 1.0 + nrm(ks[16], (DEPTH, D_MODEL), 0.02)
    ln2_b = nrm(ks[17], (DEPTH, D_MODEL), 0.02)
    return {"x": x, "ln_in_g": ln_in_g, "ln_in_b": ln_in_b, "w_in": w_in, "pool_w": pool_w,
            "pool_scale": pool_scale, "w_out": w_out, "ln1_g": ln1_g, "ln1_b": ln1_b,
            "ffn_wg": ffn_wg, "ffn_wu": ffn_wu, "ffn_wd": ffn_wd, "moe_router": moe_router,
            "moe_wg": moe_wg, "moe_wu": moe_wu, "moe_wd": moe_wd, "ln2_g": ln2_g, "ln2_b": ln2_b}

def first_block(x, ln_in_g, ln_in_b, w_in, pool_w, pool_scale, w_out, ln1_g, ln1_b,
              ffn_wg, ffn_wu, ffn_wd, moe_router, moe_wg, moe_wu, moe_wd, ln2_g, ln2_b):
    B, S, _ = x.shape
    h = layer_norm(x, ln_in_g, ln_in_b)
    for layer in range(DEPTH):
        proj = h @ w_in[layer]
        u_pool = proj[..., :POOL_WIDTH]
        qkv = proj[..., POOL_WIDTH:].reshape(B, S, 3, SB_HEADS, SB_HEAD_DIM)
        qkv = jnp.transpose(qkv, (2, 0, 3, 1, 4))
        y_pool = pool_mixer(u_pool, pool_w[layer], pool_scale[layer])
        y_sb = stick_breaking_attention(qkv[0], qkv[1], qkv[2])
        y_sb = jnp.transpose(y_sb, (0, 2, 1, 3)).reshape(B, S, SB_WIDTH)
        mix = jnp.concatenate([y_pool, y_sb], axis=-1) @ w_out[layer]
        h = layer_norm(DN_ALPHA * h + mix, ln1_g[layer], ln1_b[layer])
        if layer % 2 == 0:
            i = layer // 2
            f = swiglu(h, ffn_wg[i], ffn_wu[i], ffn_wd[i])
        else:
            i = layer // 2
            f = moe_ffn(h, moe_router[i], moe_wg[i], moe_wu[i], moe_wd[i])
        h = layer_norm(DN_ALPHA * h + f, ln2_g[layer], ln2_b[layer])
    return h


HG_HEADS = 4
HG_KDIM = 128
HG_VDIM = 128
HG_CHUNK = 64
ATT_GROUPS = ((128, 1), (512, 4), (2048, 16))
N_GROUPS = 3
ATT_HEADS = 4
ATT_DIM = 128
ROPE_THETA = 500000.0
ROPE_DIM = ATT_DIM // 4
D_FF_2 = 4 * D_MODEL
EPS = 1e-6

HG_QK_W = HG_HEADS * HG_KDIM
HG_V_W = HG_HEADS * HG_VDIM
ATT_W = ATT_HEADS * ATT_DIM
ATT_QKV_W = 3 * N_GROUPS * ATT_W
SPLITS = (HG_QK_W, HG_QK_W, HG_V_W, HG_V_W, ATT_QKV_W, D_MODEL, D_MODEL)
N_IN = HG_QK_W + HG_QK_W + HG_V_W + HG_V_W + ATT_QKV_W + D_MODEL + D_MODEL


def rms_norm(x, g):
    xf = x.astype(jnp.float32)
    y = xf * lax.rsqrt(jnp.mean(xf * xf, axis=-1, keepdims=True) + EPS)
    return (y * g.astype(jnp.float32)).astype(x.dtype)

def partial_rope(t, cos, sin):
    tf = t.astype(jnp.float32)
    c = cos[:, None, :]
    s = sin[:, None, :]
    half = ROPE_DIM // 2
    r1 = tf[..., :half]
    r2 = tf[..., half:ROPE_DIM]
    out = jnp.concatenate([r1 * c - r2 * s, r2 * c + r1 * s, tf[..., ROPE_DIM:]], axis=-1)
    return out.astype(t.dtype)

def hgrn2_chunked(q, log_f, k, v):
    B, S, H, K = q.shape
    V = v.shape[-1]
    C = HG_CHUNK
    nc = S // C

    def chunks(t):
        return t.reshape(B, nc, C, H, t.shape[-1]).swapaxes(0, 1)

    causal = jnp.tril(jnp.ones((C, C), dtype=bool))[None, :, :, None, None]

    def step(state, xs):
        qc, gc, kc, vc = xs
        b = jnp.cumsum(gc, axis=1)
        rel = jnp.where(causal, b[:, :, None] - b[:, None, :], -jnp.inf)
        attn = jnp.einsum('bthk,btshk,bshk->bhts', qc, jnp.exp(rel), kc)
        o = (jnp.einsum('bhts,bshv->bthv', attn, vc)
             + jnp.einsum('bthk,bhkv->bthv', qc * jnp.exp(b), state))
        b_last = b[:, -1]
        k_dec = kc * jnp.exp(b_last[:, None] - b)
        state = state * jnp.exp(b_last)[..., None] + jnp.einsum('bshk,bshv->bhkv', k_dec, vc)
        return state, o

    state0 = jnp.zeros((B, H, K, V), jnp.float32)
    _, o = lax.scan(step, state0, (chunks(q), chunks(log_f), chunks(k), chunks(v)))
    return o.swapaxes(0, 1).reshape(B, S, H, V)

def dilated_window_attention(q, k, v, window, dilation):
    B, S, H, Dh = q.shape
    L = window // dilation
    period = dilation * L
    Sp = -(-S // period) * period
    M = Sp // dilation
    nb = M // L
    pad = Sp - S

    def to_blocks(t):
        t = jnp.pad(t, ((0, 0), (0, pad), (0, 0), (0, 0)))
        t = t.reshape(B, M, dilation, H, Dh)
        t = t.transpose(0, 2, 3, 1, 4)
        return t.reshape(B, dilation, H, nb, L, Dh)

    def with_prev(t):
        prev = jnp.pad(t, ((0, 0), (0, 0), (0, 0), (1, 0), (0, 0), (0, 0)))[:, :, :, :-1]
        return jnp.concatenate([prev, t], axis=4)

    qb = to_blocks(q).astype(jnp.float32)
    kw = with_prev(to_blocks(k)).astype(jnp.float32)
    vw = with_prev(to_blocks(v)).astype(jnp.float32)

    scores = jnp.einsum('bzhnqd,bzhnkd->bzhnqk', qb, kw) * (Dh ** -0.5)
    i = jnp.arange(L)[:, None]
    j = jnp.arange(2 * L)[None, :]
    delta = L + i - j
    band = (delta >= 0) & (delta <= L)
    n = jnp.arange(nb)[:, None, None]
    mask = band[None] & ((n > 0) | (j[None] >= L))
    scores = jnp.where(mask, scores, -jnp.inf)
    m = jnp.max(scores, axis=-1, keepdims=True)
    p = jnp.exp(scores - m)
    den = jnp.sum(p, axis=-1, keepdims=True)
    o = jnp.einsum('bzhnqk,bzhnkd->bzhnqd', p, vw) / den
    lse = (m + jnp.log(den))[..., 0]

    o = o.reshape(B, dilation, H, M, Dh).transpose(0, 3, 1, 2, 4).reshape(B, Sp, H, Dh)[:, :S]
    lse = lse.reshape(B, dilation, H, M).transpose(0, 3, 1, 2).reshape(B, Sp, H)[:, :S]
    return o, lse

def second_inputs(seed: int = 0) -> dict:
    key = jax.random.key(seed)
    ks = jax.random.split(key, 13)
    f32 = jnp.float32
    nrm = lambda k, shape, scale: jax.random.normal(k, shape, f32) * scale
    return {
        "x": nrm(ks[0], (BATCH, SEQ, D_MODEL), 1.0),
        "norm1_g": 1.0 + nrm(ks[1], (DEPTH, D_MODEL), 0.02),
        "w_in": nrm(ks[2], (DEPTH, D_MODEL, N_IN), D_MODEL ** -0.5),
        "hg_lower_bounds": nrm(ks[3], (DEPTH, HG_QK_W), 1.0),
        "hg_norm_g": 1.0 + nrm(ks[4], (DEPTH, HG_V_W), 0.02),
        "w_branch_a": nrm(ks[5], (DEPTH, HG_V_W, D_MODEL), HG_V_W ** -0.5),
        "w_branch_b": nrm(ks[6], (DEPTH, ATT_W, D_MODEL), ATT_W ** -0.5),
        "w_out": nrm(ks[7], (DEPTH, D_MODEL, D_MODEL), D_MODEL ** -0.5),
        "norm2_g": 1.0 + nrm(ks[8], (DEPTH, D_MODEL), 0.02),
        "w_up": nrm(ks[9], (DEPTH, D_MODEL, D_FF_2), D_MODEL ** -0.5),
        "w_down": nrm(ks[10], (DEPTH, D_FF_2, D_MODEL), D_FF_2 ** -0.5),
        "final_norm_g": 1.0 + nrm(ks[11], (D_MODEL,), 0.02),
    }

def second_block(x, norm1_g, w_in, hg_lower_bounds, hg_norm_g, w_branch_a, w_branch_b,
              w_out, norm2_g, w_up, w_down, final_norm_g):
    B, S, _ = x.shape
    f32 = jnp.float32
    split_idx = [int(c) for c in np.cumsum(SPLITS)[:-1]]

    pos = jnp.arange(S, dtype=f32)
    inv_freq = ROPE_THETA ** (-jnp.arange(0, ROPE_DIM, 2, dtype=f32) / ROPE_DIM)
    ang = pos[:, None] * inv_freq[None, :]
    cos, sin = jnp.cos(ang), jnp.sin(ang)

    lb_all = jnp.cumsum(jax.nn.softmax(hg_lower_bounds.astype(f32), axis=0), axis=0)
    lb_all = lb_all - lb_all[0:1]

    for l in range(DEPTH):
        h = rms_norm(x, norm1_g[l])
        z = h @ w_in[l]
        zq, zf, zi, zg, zatt, za, zb = jnp.split(z, split_idx, axis=-1)

        q_hg = jax.nn.silu(zq.astype(f32)).reshape(B, S, HG_HEADS, HG_KDIM)
        lb = lb_all[l]
        log_f = jnp.logaddexp(jnp.log(lb), jnp.log1p(-lb) + jax.nn.log_sigmoid(zf.astype(f32)))
        log_f = log_f.reshape(B, S, HG_HEADS, HG_KDIM)
        k_hg = -jnp.expm1(log_f)
        v_hg = zi.astype(f32).reshape(B, S, HG_HEADS, HG_VDIM)
        o_hg = hgrn2_chunked(q_hg, log_f, k_hg, v_hg)
        o_hg = rms_norm(o_hg, hg_norm_g[l].reshape(HG_HEADS, HG_VDIM))
        o_hg = o_hg * jax.nn.sigmoid(zg.astype(f32)).reshape(B, S, HG_HEADS, HG_VDIM)
        o_hg = o_hg.reshape(B, S, HG_V_W).astype(x.dtype)

        qkv = zatt.reshape(B, S, 3, N_GROUPS, ATT_HEADS, ATT_DIM)
        outs, lses = [], []
        for g, (window, dilation) in enumerate(ATT_GROUPS):
            qg = partial_rope(qkv[:, :, 0, g], cos, sin)
            kg = partial_rope(qkv[:, :, 1, g], cos, sin)
            vg = qkv[:, :, 2, g]
            o_g, lse_g = dilated_window_attention(qg, kg, vg, window, dilation)
            outs.append(o_g)
            lses.append(lse_g)
        w_grp = jax.nn.softmax(jnp.stack(lses, axis=0), axis=0)
        o_att = jnp.sum(w_grp[..., None] * jnp.stack(outs, axis=0), axis=0)
        o_att = o_att.reshape(B, S, ATT_W).astype(x.dtype)

        y = (jax.nn.sigmoid(za) * (o_hg @ w_branch_a[l])
             + jax.nn.sigmoid(zb) * (o_att @ w_branch_b[l]))
        x = x + y @ w_out[l]

        h2 = rms_norm(x, norm2_g[l])
        x = x + jnp.square(jax.nn.relu(h2 @ w_up[l])) @ w_down[l]

    return rms_norm(x, final_norm_g)


def setup_inputs(seed=0):
    out = dict(first_inputs(seed))
    for name, value in second_inputs(seed + 1).items():
        if name != "x":
            out[name + "_2"] = value
    return out


def reference(
    x, ln_in_g, ln_in_b, w_in, pool_w, pool_scale, w_out, ln1_g, ln1_b, ffn_wg, ffn_wu, ffn_wd,
    moe_router, moe_wg, moe_wu, moe_wd, ln2_g, ln2_b, norm1_g_2, w_in_2, hg_lower_bounds_2,
    hg_norm_g_2, w_branch_a_2, w_branch_b_2, w_out_2, norm2_g_2, w_up_2, w_down_2,
    final_norm_g_2,
):
    x = first_block(
        x, ln_in_g, ln_in_b, w_in, pool_w, pool_scale, w_out, ln1_g, ln1_b, ffn_wg, ffn_wu,
        ffn_wd, moe_router, moe_wg, moe_wu, moe_wd, ln2_g, ln2_b,
    )
    return second_block(
        x, norm1_g_2, w_in_2, hg_lower_bounds_2, hg_norm_g_2, w_branch_a_2, w_branch_b_2,
        w_out_2, norm2_g_2, w_up_2, w_down_2, final_norm_g_2,
    )


_drawn_inputs = setup_inputs


def setup_inputs(seed=0):
    import zlib

    import numpy as np

    out = dict(_drawn_inputs(seed))
    spreads = {}
    factors = {'norm1_g_2': 5.761, 'hg_lower_bounds_2': 3.783, 'hg_norm_g_2': 7.642}
    for name, (base, spread) in spreads.items():
        noise = np.random.default_rng([zlib.crc32(name.encode()), seed]).standard_normal(out[name].shape)
        drawn = base * np.exp(spread * noise) if base else spread * noise
        out[name] = __import__('jax').numpy.asarray(drawn.astype(out[name].dtype))
    for name, factor in factors.items():
        out[name] = (out[name] * factor).astype(out[name].dtype)
    return out
```

```python
from contextlib import ExitStack, contextmanager

import numpy as np

import concourse.bass as bass
from concourse import mybir

F32 = mybir.dt.float32
I32 = mybir.dt.int32
ALU = mybir.AluOpType
ACT = mybir.ActivationFunctionType
AX = mybir.AxisListType.X

P = 128
D = 1024
S = 256
TT = S // P
KT = D // P
DEPTH = 2
ALPHA = (2 * DEPTH) ** 0.25
LN_EPS = 1e-5
RMS_EPS = 1e-6

POOL_W = 512
POOL_WINDOWS = (2, 4, 8, 16)
SB_HEADS = 8
SB_DIM = 64
FF = 2816
FT = FF // P
E = 8
SLOTS = 128

HG_HEADS = 4
ATT_HEADS = 4
ATT_GROUPS = 3
DILATIONS = (1, 4, 16)
ROPE_DIM = 32
ROPE_THETA = 500000.0
FF2 = 4096
NT2 = FF2 // P
BIG = 30000.0

CHUNK = 2048
RING = 8

HG_LEVELS = (64, 32, 16, 8, 4, 2, 1)



def shape_constants():
    i = np.arange(P)
    part, free = i[:, None], i[None, :]
    f = np.float32
    c = {}
    c["ident"] = np.eye(P, dtype=f)
    c["ones"] = np.ones((P, P), f)
    c["neg_ge"] = -(part >= free).astype(f)
    c["neg_ones"] = -np.ones((P, P), f)
    c["before"] = (part < free).astype(f)
    c["before_bias"] = np.where(part < free, 0.0, -BIG).astype(f)
    c["upto"] = (part <= free).astype(f)
    c["iota"] = np.broadcast_to(free, (P, P)).astype(f)
    t = np.arange(S)
    c["inv_count"] = np.broadcast_to(
        np.concatenate([1.0 / np.minimum(t + 1, w) for w in POOL_WINDOWS])[None], (P, 4 * S)).astype(f)
    first = {k: v.copy() for k, v in c.items() if k not in ("ident", "ones")}
    shared = {k: c[k] for k in ("ident", "ones")}
    second = {}
    for name, gap in (("own_mask", 0), ("prev_mask", P)):
        delta = part + gap - free
        ok = [(delta >= 0) & (delta % dil == 0) & (delta <= P * dil) for dil in DILATIONS]
        second[name] = np.concatenate([np.where(o, 0.0, -BIG * 1e26) for o in ok], 1).astype(f)
    lv = [(part // (2 * m) == free // (2 * m)) & (part % (2 * m) < m) & (free % (2 * m) >= m) for m in HG_LEVELS]
    second["hg_levels"] = np.concatenate(lv + [part == free], 1).astype(f)
    second["scan_keep"] = np.broadcast_to((np.arange(HG_HEADS * S) % P != 0)[None], (P, HG_HEADS * S)).astype(f)
    inv = ROPE_THETA ** (-np.arange(0, ROPE_DIM, 2, dtype=f) / f(ROPE_DIM))
    ang = np.arange(S, dtype=f)[None, :] * inv.astype(f)[:, None]
    pad = np.zeros((P - ROPE_DIM, S), f)
    second["rope_cos"] = np.concatenate([np.cos(ang), np.cos(ang), pad]).astype(f)
    second["rope_sin"] = np.concatenate([np.sin(ang), np.sin(ang), pad]).astype(f)
    half = ROPE_DIM // 2
    swap = np.zeros((P, ROPE_DIM), f)
    for m in range(half):
        swap[m + half, m] = -1.0
        swap[m, m + half] = 1.0
    second["rope_swap"] = swap
    return shared, first, second


def packed(parts):
    where, at = {}, 0
    for k, v in parts.items():
        where[k] = (at, v.shape[1])
        at += v.shape[1]
    return np.ascontiguousarray(np.concatenate(list(parts.values()), 1)), where



class Sem:

    def __init__(self, handle, name):
        self.handle, self.name, self.count = handle, name, 0


class Tok:

    def __init__(self, sem, count, loop):
        self.sem, self.count, self.loop = sem, count, loop


class Loop:
    def __init__(self, name, index, trips, start):
        self.name, self.index, self.trips, self.start, self.open = name, index, trips, start, True


class Counters:

    def __init__(self, nc, ctx, plan):
        self.nc, self.ctx, self.plan, self.seen = nc, ctx, plan, {}
        self.loop, self.sems = None, []

    def sem(self, name):
        s = Sem(self.ctx.enter_context(self.nc.semaphore(name)), name)
        self.sems.append(s)
        return s

    def raised(self, sem, inst, by=1):
        inst.then_inc(sem.handle, by)
        sem.count += by
        return Tok(sem, sem.count, self.loop)

    def now(self, sem):
        return Tok(sem, sem.count, self.loop)

    def value(self, tok):
        lp = tok.loop
        if lp is None:
            if self.loop is None:
                return tok.count
            return tok.count
        step = self.plan.get(lp.name, {}).get(tok.sem.name, 0)
        if lp.open:
            return lp.index * step + tok.count if step else tok.count
        return tok.count + (lp.trips - 1) * step

    @contextmanager
    def repeat(self, name, trips):
        with self.nc.Fori(0, trips) as i:
            lp = Loop(name, i, trips, {s.name: s.count for s in self.sems})
            self.loop = lp
            yield i
            adds = {s.name: s.count - lp.start[s.name] for s in self.sems}
            self.seen[name] = adds
            lp.open, self.loop = False, None
        for s in self.sems:
            s.count = lp.start[s.name] + trips * adds[s.name]


class Engine:

    def __init__(self, counters, queue, name):
        self.c, self.q = counters, queue
        self.sem = counters.sem("done_" + name)
        self.settled = counters.sem("settled_" + name)
        self.known = {}

    def after(self, *toks):
        best = {}
        for t in toks:
            if isinstance(t, (list, tuple)):
                self.after(*t)
            elif t is not None:
                if t.sem.name not in best or best[t.sem.name].count < t.count or best[t.sem.name].loop is not t.loop:
                    if t.sem.name in best and best[t.sem.name].loop is not t.loop:
                        self._wait(best[t.sem.name])
                    best[t.sem.name] = t
        for t in best.values():
            self._wait(t)

    def _wait(self, t):
        key = (t.sem.name, id(t.loop), id(self.c.loop))
        if self.known.get(key, -1) >= t.count:
            return
        self.known[key] = t.count
        self.q.wait_ge(t.sem.handle, self.c.value(t))

    def did(self, inst):
        return self.c.raised(self.sem, inst)

    def settle(self):
        self.q.sem_inc(self.settled.handle, 1)


class Ring:

    def __init__(self, c, ctx, nc, sync, pe):
        self.c, self.sync, self.pe = c, sync, pe
        self.slots = [ctx.enter_context(nc.sbuf_tensor(f"weights{i}", [P, CHUNK], F32)) for i in range(RING)]
        self.filled = [c.sem(f"filled{i}") for i in range(RING)]
        self.used = [c.sem(f"used{i}") for i in range(RING)]
        self.next = 0

    def align(self):
        self.next = 0

    def load(self, src, a, b):
        i = self.next
        self.next = (i + 1) % RING
        self.sync.after(self.c.now(self.used[i]))
        if self.c.loop is not None:
            self.sync.settle()
        view = self.slots[i][:, 0:a * b].rearrange("p (a b) -> p a b", a=a)
        arrived = self.c.raised(self.filled[i], self.sync.q.dma_start(view, src), 16)
        return i, view, arrived

    def release(self, i, inst):
        return self.c.raised(self.used[i], inst)


def write_program(nc, A, const_at, plan):
    ctx = ExitStack()
    c = Counters(nc, ctx, plan)
    with ctx:
        pe = Engine(c, nc.tensor, "pe")
        dve = Engine(c, nc.vector, "dve")
        act = Engine(c, nc.scalar, "act")
        pool = Engine(c, nc.gpsimd, "pool")
        sync = Engine(c, nc.sync, "sync")
        computing = (pe, dve, act, pool)
        V, G, SC, T = nc.vector, nc.gpsimd, nc.scalar, nc.tensor

        def sb(name, n, dt=F32, parts=P):
            return ctx.enter_context(nc.sbuf_tensor(name, [parts, n], dt))

        ring = Ring(c, ctx, nc, sync, pe)
        h = sb("h", TT * D)[:, :].rearrange("p (t d) -> p t d", t=TT)
        hT = sb("hT", KT * S)[:, :].rearrange("p (k s) -> p k s", k=KT)
        gains = sb("gains", 2 * D)[:, :].rearrange("p (i d) -> p i d", i=2)
        shared = sb("shared", A["const_shared"].shape[1])
        vecs = sb("vecs", A["vecs"].shape[1])
        stats = sb("stats", 64)
        tables = sb("tables", 64)
        arena = sb("arena", 30064)
        banks = [ctx.enter_context(nc.psum_tensor(f"bank{i}", [P, 512], F32)) for i in range(8)]
        bank_read = [None] * 8

        def shared_const(name):
            at, n = const_at["shared"][name]
            return shared[:, at:at + n]

        ident, ones = shared_const("ident"), shared_const("ones")

        class Area:

            def __init__(self, at=0):
                self.at = at

            def take(self, n, a=None, b=None):
                v = arena[:, self.at:self.at + n]
                self.at += n
                assert self.at <= 30064, self.at
                if b is not None:
                    return v.rearrange("p (a b c) -> p a b c", a=a, b=b)
                return v if a is None else v.rearrange("p (a b) -> p a b", a=a)

        def fence():
            toks = [c.now(e.sem) for e in computing] + [c.now(s) for s in ring.used]
            for e in computing:
                e.after(*toks)
                if c.loop is not None:
                    e.settle()
            for i in range(8):
                bank_read[i] = None

        def load_small(name, *pairs):
            arrived = c.sem("loaded_" + name)
            for dst, src in pairs:
                tok = c.raised(arrived, nc.scalar.dma_start(dst, src), 16)
            return tok

        def tile2(ap):
            return ap.rearrange("p (t n) -> p t n", t=2)


        def product(src, kt, n, act_in, ready, bank, rows):
            slot, w, arrived = ring.load(src, kt, n)
            pe.after(arrived, ready, bank_read[bank])
            out = tile2(banks[bank][:, :])
            for j in range(2):
                for k in range(kt):
                    if rows:
                        lhsT, rhs = act_in[:, k, j * P:(j + 1) * P], w[:, k, :]
                    else:
                        lhsT, rhs = w[:, k, j * P:(j + 1) * P], act_in[:, k, :]
                    mm = T.matmul(out[:, j, :], lhsT, rhs, start=(k == 0), stop=(k == kt - 1))
            return ring.release(slot, mm)

        def accumulate(w_rows, tiles, act_in, ready, first_bank):
            n = tiles // 2
            for i in range(n):
                slot, w, arrived = ring.load(
                    w_rows[i * 2 * P:(i + 1) * 2 * P, :].rearrange("(k p) n -> p k n", p=P), 2, D)
                pe.after(arrived, ready[i] if isinstance(ready, list) else ready)
                if i == 0:
                    pe.after(*[bank_read[first_bank + b] for b in range(4)])
                for k in range(2):
                    for t in range(TT):
                        for half in range(2):
                            mm = T.matmul(banks[first_bank + 2 * t + half][:, :],
                                          act_in[:, 2 * i + k, t * P:(t + 1) * P],
                                          w[:, k, half * 512:(half + 1) * 512],
                                          start=(i == 0 and k == 0), stop=(i == n - 1 and k == 1))
                done = ring.release(slot, mm)
            return done

        def transpose_rows(src, src_ready, dst, scales=None):
            last = []
            for t in range(TT):
                for g in range(KT // 4):
                    b = 2 * t + g
                    pe.after(src_ready[t], bank_read[b])
                    for k in range(4):
                        mm = T.transpose(banks[b][:, k * P:(k + 1) * P],
                                         src[:, t, (4 * g + k) * P:(4 * g + k + 1) * P], ident)
                    done = pe.did(mm)
                    out = dst[:, 4 * g:4 * g + 4, t * P:(t + 1) * P]
                    src4 = banks[b][:, :].rearrange("p (k s) -> p k s", k=4)
                    if scales is None:
                        e = dve if g else act
                        e.after(done)
                        bank_read[b] = e.did(V.tensor_copy(out, src4) if g else SC.copy(out, src4))
                    else:
                        dve.after(done)
                        bank_read[b] = dve.did(V.tensor_tensor(
                            out, src4, scales[:, 4 * g:4 * g + 4].to_broadcast((P, 4, P)) if False else
                            scales[:, 4 * g:4 * g + 4].unsqueeze(2).to_broadcast((P, 4, P)), ALU.mult))
                    last.append(bank_read[b])
            return last

        def inverse_root(x, ready):
            act.after(ready)
            a = act.did(SC.activation(x, x, ACT.Ln))
            act.after(a)
            return act.did(SC.activation(x, x, ACT.Exp, scale=-0.5))

        def layer_norm(x, t, dst, gains_ready, *ready):
            st = stats[:, 16 * t:16 * t + 12].rearrange("p (a b) -> p a b", a=2)
            mv = stats[:, 16 * t + 12:16 * t + 14]
            rstd = stats[:, 16 * t + 14:16 * t + 15]
            dve.after(*ready)
            for i in range(2):
                a = dve.did(V.bn_stats(st[:, i, :], x[:, t, i * 512:(i + 1) * 512]))
            dve.after(a)
            a = dve.did(V.bn_aggr(mv, st))
            dve.after(a)
            a = dve.did(V.tensor_scalar(rstd, mv[:, 1:2], LN_EPS, None, ALU.add))
            dve.after(inverse_root(rstd, a))
            a = dve.did(V.tensor_scalar(dst[:, t, :], x[:, t, :], mv[:, 0:1], rstd, ALU.subtract, ALU.mult))
            dve.after(a, gains_ready)
            a = dve.did(V.tensor_tensor(dst[:, t, :], dst[:, t, :], gains[:, 0, :], ALU.mult))
            dve.after(a)
            return dve.did(V.tensor_tensor(dst[:, t, :], dst[:, t, :], gains[:, 1, :], ALU.add))

        def rms_scale(x, t, scratch, *ready):
            ss, rstd = stats[:, 40 + 2 * t:41 + 2 * t], stats[:, 41 + 2 * t:42 + 2 * t]
            act.after(*ready)
            a = act.did(SC.activation(scratch, x[:, t, :], ACT.Square, accum_out=ss))
            dve.after(a)
            a = dve.did(V.tensor_scalar(rstd, ss, 1.0 / D, RMS_EPS, ALU.mult, ALU.add))
            return rstd, inverse_root(rstd, a)

        def residual_norm(first_bank, done, gains_ready):
            out = []
            for t in range(TT):
                dve.after(done)
                for half in range(2):
                    b = first_bank + 2 * t + half
                    cols = h[:, t, half * 512:(half + 1) * 512]
                    bank_read[b] = dve.did(V.scalar_tensor_tensor(
                        out=cols, in0=cols, scalar=ALPHA, in1=banks[b][:, :], op0=ALU.mult, op1=ALU.add))
                out.append(layer_norm(h, t, h, gains_ready, bank_read[b]))
            return out

        def load_gains(name, g, b, *free):
            act.after(*free)
            return load_small(name, (gains[:, 0, :], g.partition_broadcast(P)),
                              (gains[:, 1, :], b.partition_broadcast(P)))

        h_loaded = load_small("start", (h, A["x"].rearrange("a (t p) d -> p (a t) d", p=P)),
                              (shared[:, :], A["const_shared"]), (vecs[:, :], A["vecs"]),
                              (gains[:, 0, :], A["ln_in_g"].partition_broadcast(P)),
                              (gains[:, 1, :], A["ln_in_b"].partition_broadcast(P)))

        area = Area()
        first_const = area.take(A["const_first"].shape[1])
        const_loaded = load_small("const_first", (first_const, A["const_first"]))

        def fc(name):
            at, n = const_at["first"][name]
            return first_const[:, at:at + n]

        neg_ge, neg_ones, before, before_bias = fc("neg_ge"), fc("neg_ones"), fc("before"), fc("before_bias")
        upto, iota = fc("upto"), fc("iota")
        inv_count = fc("inv_count").rearrange("p (g s) -> p g s", g=4)
        mixer_start = area.at
        for e_ in computing:
            e_.after(h_loaded, const_loaded)

        def layer_vec(name, layer, n):
            at = const_at["vecs"][name] + layer * n
            return vecs[:, at:at + n]

        h_ready = [layer_norm(h, t, h, h_loaded, h_loaded) for t in range(TT)]

        def first_mixer(layer, h_ready):
            area = Area(mixer_start)
            uT, qT, kT = (area.take(4 * S, 4) for _ in range(3))
            v = area.take(TT * 512, TT)
            mixT = area.take(KT * S, KT)
            sums, lagged = area.take(4 * S, 4), area.take(4 * S, 4)
            pool_w = area.take(4 * P, 4)
            soft, expo, mag = (area.take(2 * 384, 2) for _ in range(3))
            soft2, expo2, mag2 = (area.take(2 * 384, 2) for _ in range(3))
            fence()
            pool_w_loaded = load_small(
                f"pool_w{layer}", (pool_w, A["pool_w"][layer].rearrange("g c d -> c g d")))
            gains_ready = load_gains(
                f"ln1_{layer}", A["ln1_g"][layer:layer + 1, :], A["ln1_b"][layer:layer + 1, :], h_ready)
            hT_ready = transpose_rows(h, h_ready, hT)
            w = A["w_in"][layer].rearrange("(k p) n -> p k n", p=P)

            def chunk(col):
                return w[:, :, col * 256:(col + 1) * 256]

            ready = {}
            for i, (name, dst, col) in enumerate((("q", qT, 2), ("q", qT, 3), ("k", kT, 4), ("k", kT, 5))):
                done = product(chunk(col), KT, 256, hT, hT_ready, i % 3, rows=False)
                j = 2 * (col % 2)
                act.after(done)
                out = dst[:, j:j + 2, :]
                bank_read[i % 3] = ready[name, j] = act.did(
                    SC.activation(out, tile2(banks[i % 3][:, :]), ACT.Copy, scale=0.125 if name == "q" else 1.0))
            for i in range(2):
                b = (4 + i) % 3
                done = product(chunk(6 + i), KT, 256, hT, hT_ready, b, rows=True)
                dve.after(done)
                bank_read[b] = ready["v", i] = dve.did(
                    V.tensor_copy(v[:, :, i * 256:(i + 1) * 256], tile2(banks[b][:, :])))

            def stick_breaking():
                y_read = None
                for pair in range(SB_HEADS // 2):
                    bufs = (soft, expo, mag) if pair % 2 == 0 else (soft2, expo2, mag2)
                    sp, ex, mg = bufs
                    zb = (4, 5) if pair % 2 == 0 else (6, 7)
                    pe.after(ready["q", 2 * (pair // 2)], ready["k", 2 * (pair // 2)], *[bank_read[b] for b in zb])
                    for e in range(2):
                        lo = SB_DIM * e
                        q_, k_ = qT[lo:lo + SB_DIM, pair, :], kT[lo:lo + SB_DIM, pair, :]
                        z = banks[zb[e]]
                        T.matmul(z[:, 0:256], k_[:, 0:P], q_, start=True, stop=True)
                        mm = T.matmul(z[:, 256:384], k_[:, P:S], q_[:, P:S], start=False, stop=True,
                                      skip_group_check=True)
                    scored = pe.did(mm)
                    yield
                    for e in range(2):
                        z = banks[zb[e]][:, 0:384]
                        act.after(scored)
                        a = act.did(SC.activation(mg[:, e, :], z, ACT.Abs))
                    act.after(a)
                    a = act.did(SC.activation(ex, mg, ACT.Exp, scale=-1.0))
                    act.after(a)
                    a = act.did(SC.activation(mg, ex, ACT.Ln, bias=1.0))
                    dve.after(a)
                    for e in range(2):
                        a = dve.did(V.scalar_tensor_tensor(out=sp[:, e, :], in0=banks[zb[e]][:, 0:384], scalar=0.0,
                                                           in1=mg[:, e, :], op0=ALU.max, op1=ALU.add))
                    dve.after(a)
                    two = before.unsqueeze(1).to_broadcast((P, 2, P))
                    dve.did(V.tensor_tensor(sp[:, :, 0:P], sp[:, :, 0:P], two, ALU.mult))
                    masked = dve.did(V.tensor_tensor(sp[:, :, 256:384], sp[:, :, 256:384], two, ALU.mult))
                    yield
                    pe.after(masked)
                    for e in range(2):
                        z = banks[zb[e]]
                        T.matmul(z[:, 0:256], neg_ge, sp[:, e, 0:256], start=False, stop=True, skip_group_check=True)
                        T.matmul(z[:, P:256], neg_ones, sp[:, e, 256:384], start=False, stop=True,
                                 skip_group_check=True)
                        mm = T.matmul(z[:, 256:384], neg_ge, sp[:, e, 256:384], start=False, stop=True,
                                      skip_group_check=True)
                    summed = pe.did(mm)
                    for e in range(2):
                        z = banks[zb[e]]
                        dve.after(summed)
                        dve.did(V.scalar_tensor_tensor(out=ex[:, e, 0:P], in0=z[:, 0:P], scalar=0.0, in1=before_bias,
                                                       op0=ALU.min, op1=ALU.add))
                        dve.did(V.scalar_tensor_tensor(out=ex[:, e, 256:384], in0=z[:, 256:384], scalar=0.0,
                                                       in1=before_bias, op0=ALU.min, op1=ALU.add))
                        a = dve.did(V.tensor_scalar(ex[:, e, P:256], z[:, P:256], 0.0, None, ALU.min))
                        bank_read[zb[e]] = a
                    act.after(a, summed)
                    att = act.did(SC.activation(mg, ex, ACT.Exp))
                    yield
                    pe.after(att, ready["v", pair // 2], y_read, bank_read[3])
                    for e in range(2):
                        lo, head = SB_DIM * e, 2 * pair + e
                        y = banks[3][lo:lo + SB_DIM, 0:256]
                        T.matmul(y, v[:, 0, head * SB_DIM:(head + 1) * SB_DIM], mg[:, e, 0:256], start=True, stop=True)
                        mm = T.matmul(y[:, P:S], v[:, 1, head * SB_DIM:(head + 1) * SB_DIM], mg[:, e, 256:384],
                                      start=False, stop=True, skip_group_check=True)
                    done = pe.did(mm)
                    act.after(done)
                    y_read = bank_read[3] = act.did(SC.copy(mixT[:, 4 + pair, :], banks[3][:, 0:256]))
                    ready["y", pair] = y_read
                    yield

            side = stick_breaking()
            for i in range(2):
                b = i
                done = product(chunk(i), KT, 256, hT, hT_ready, b, rows=False)
                act.after(done)
                bank_read[b] = ready["u", i] = act.did(SC.copy(uT[:, 2 * i:2 * i + 2, :], tile2(banks[b][:, :])))
                for _ in range(3):
                    next(side, None)
            u_ready = [ready["u", 0], ready["u", 1]]
            src, a = uT, u_ready
            for g, w_ in enumerate(POOL_WINDOWS):
                lag = w_ // 2
                dst = sums if g % 2 == 0 else lagged
                pool.after(a)
                a1 = pool.did(G.tensor_copy(dst[:, g:4, 0:lag], src[:, g:4, 0:lag]))
                a2 = pool.did(G.tensor_tensor(dst[:, g:4, lag:S], src[:, g:4, lag:S], src[:, g:4, 0:S - lag], ALU.add))
                a = [a1, a2]
                src = dst
            pool.after(a)
            for g in range(4):
                s_ = (sums if g % 2 == 0 else lagged)[:, g, :]
                a1 = pool.did(G.tensor_tensor(s_, s_, inv_count[:, g, :], ALU.mult))
                pool.after(a1)
                a1 = pool.did(G.tensor_tensor(s_, s_, uT[:, g, :], ALU.subtract))
            pooled = a1
            for g in range(4):
                b = g % 2
                pe.after(pooled, pool_w_loaded, bank_read[b])
                s_ = (sums if g % 2 == 0 else lagged)[:, g, :]
                mapped = pe.did(T.matmul(banks[b][:, 0:256], pool_w[:, g, :], s_, start=True, stop=True))
                act.after(mapped)
                bank_read[b] = act.did(SC.activation(mixT[:, g, :], banks[b][:, 0:256], ACT.Copy,
                                                     scale=layer_vec("pool_scale", layer, 4)[:, g:g + 1]))
            y_pool = bank_read[b]
            for _ in side:
                pass
            all_y = [ready["y", p_] for p_ in range(4)]
            done = accumulate(A["w_out"][layer], KT, mixT, [y_pool, y_pool, all_y, all_y], 4)
            return residual_norm(4, done, gains_ready)

        def dense_ffn(h_ready):
            area = Area(mixer_start)
            hid = area.take(FT * S, FT)
            gate = [area.take(512, 2) for _ in range(2)]
            fence()
            gains_ready = load_gains("ln2_0", A["ln2_g"][0:1, :], A["ln2_b"][0:1, :], h_ready)
            hT_ready = transpose_rows(h, h_ready, hT)
            wg = A["ffn_wg"][0].rearrange("(k p) n -> p k n", p=P)
            wu = A["ffn_wu"][0].rearrange("(k p) n -> p k n", p=P)
            hid_ready, gate_free = [], [None, None]
            for j in range(FT // 2):
                bg, bu = (0, 1) if j % 2 == 0 else (2, 3)
                cols = slice(j * 256, (j + 1) * 256)
                done = product(wg[:, :, cols], KT, 256, hT, hT_ready, bg, rows=False)
                act.after(done, gate_free[j % 2])
                bank_read[bg] = act.did(SC.activation(gate[j % 2], tile2(banks[bg][:, :]), ACT.Silu))
                done = product(wu[:, :, cols], KT, 256, hT, hT_ready, bu, rows=False)
                dve.after(done, bank_read[bg])
                bank_read[bu] = gate_free[j % 2] = dve.did(V.tensor_tensor(
                    hid[:, 2 * j:2 * j + 2, :], tile2(banks[bu][:, :]), gate[j % 2], ALU.mult))
                hid_ready.append(bank_read[bu])
            done = accumulate(A["ffn_wd"][0], FT, hid, hid_ready, 4)
            return residual_norm(4, done, gains_ready)

        def moe_ffn(h_ready):
            area = Area(mixer_start)
            router = area.take(KT * E, KT)
            names = ("logits", "top1", "first", "rest", "top2", "second", "sel", "gate", "rank", "t0", "t1")
            r = {n: area.take(TT * E, TT) for n in names}
            mx = area.take(8)
            base = area.take(2 * TT * E, 2, TT)
            table, table_i = tables[:, 0:32], tables[:, 32:64].bitcast(I32)
            pick, pickg = area.take(TT * P, TT), area.take(TT * P, TT)
            pickT = area.take(TT * P, TT)
            xsT = area.take(KT * SLOTS, KT)
            hidT = area.take(FT * SLOTS, FT)
            gate_s, hid_s = [area.take(256) for _ in range(2)], [area.take(256) for _ in range(2)]
            y = area.take(D)
            total = area.take(TT * D, TT)
            fence()
            gains_ready = load_gains("ln2_1", A["ln2_g"][1:2, :], A["ln2_b"][1:2, :], h_ready)
            router_ready = load_small("router", (router, A["moe_router"][0].rearrange("(k p) e -> p k e", p=P)))
            hT_ready = transpose_rows(h, h_ready, hT)
            zeroed = pool.did(G.memset(total, 0.0))
            pe.after(hT_ready, router_ready, bank_read[4])
            for t in range(TT):
                for k in range(KT):
                    mm = T.matmul(banks[4][:, t * E:(t + 1) * E], hT[:, k, t * P:(t + 1) * P], router[:, k, :],
                                  start=(k == 0), stop=(k == KT - 1))
            a = pe.did(mm)

            def vec(inst):
                t_ = dve.did(inst)
                dve.after(t_)
                return t_

            def bc(col):
                return col.unsqueeze(2).to_broadcast((P, TT, E))

            dve.after(a)
            vec(V.tensor_copy(r["logits"], banks[4][:, 0:TT * E].rearrange("p (t e) -> p t e", t=TT)))

            def choose(source, top, sel, col):
                vec(V.tensor_reduce(mx[:, col:col + 2], source, AX, ALU.max))
                vec(V.tensor_tensor(r["t0"], source, bc(mx[:, col:col + 2]), ALU.is_equal))
                for t in range(TT):
                    vec(V.tensor_tensor_scan(r["t1"][:, t, :], r["t0"][:, t, :], r["t0"][:, t, :], 0.0,
                                             ALU.bypass, ALU.add) if False else
                        V.tensor_tensor_scan(r["t1"][:, t, :], ones[:, 0:E], r["t0"][:, t, :], 0.0, ALU.mult, ALU.add))
                vec(V.tensor_scalar(r["t1"], r["t1"], 1.0, None, ALU.is_equal))
                vec(V.tensor_tensor(sel, r["t0"], r["t1"], ALU.mult))

            choose(r["logits"], None, r["first"], 0)
            vec(V.scalar_tensor_tensor(out=r["rest"], in0=r["first"], scalar=-3.0e38, in1=r["logits"],
                                       op0=ALU.mult, op1=ALU.add))
            choose(r["rest"], None, r["second"], 2)
            a = vec(V.tensor_tensor(mx[:, 4:6], mx[:, 2:4], mx[:, 0:2], ALU.subtract))
            act.after(a)
            a = act.did(SC.activation(mx[:, 4:6], mx[:, 4:6], ACT.Exp))
            dve.after(a)
            vec(V.tensor_scalar(mx[:, 6:8], mx[:, 4:6], 1.0, None, ALU.add))
            vec(V.reciprocal(mx[:, 6:8], mx[:, 6:8]))
            vec(V.tensor_tensor(mx[:, 4:6], mx[:, 4:6], mx[:, 6:8], ALU.mult))
            vec(V.tensor_tensor(r["t0"], r["first"], bc(mx[:, 6:8]), ALU.mult))
            vec(V.tensor_tensor(r["t1"], r["second"], bc(mx[:, 4:6]), ALU.mult))
            vec(V.tensor_tensor(r["gate"], r["t0"], r["t1"], ALU.add))
            a = vec(V.tensor_tensor(r["sel"], r["first"], r["second"], ALU.add))
            pe.after(a, const_loaded)
            T.matmul(banks[5][:, 0:E], upto, r["sel"][:, 0, :], start=True, stop=True)
            T.matmul(banks[5][:, E:2 * E], upto, r["sel"][:, 1, :], start=True, stop=False)
            T.matmul(banks[5][:, E:2 * E], ones, r["sel"][:, 0, :], start=False, stop=True)
            T.matmul(banks[5][:, 2 * E:3 * E], ones, r["sel"][:, 0, :], start=True, stop=False)
            a = pe.did(T.matmul(banks[5][:, 2 * E:3 * E], ones, r["sel"][:, 1, :], start=False, stop=True))
            dve.after(a)
            ranks = banks[5][:, 0:2 * E].rearrange("p (t e) -> p t e", t=TT)
            vec(V.tensor_scalar(base[:, 0, :, :], ranks, -1.0, None, ALU.add))
            vec(V.tensor_scalar(base[:, 1, :, :], ranks, -1.0 - SLOTS, None, ALU.add))
            over, order, hit = table[:, 0:8], table[:, 8:16], table[:, 24:32]
            vec(V.tensor_scalar(over, banks[5][:, 2 * E:3 * E], float(SLOTS), None, ALU.is_gt))
            vec(V.tensor_tensor_scan(order, ones[:, 0:E], over, 0.0, ALU.mult, ALU.add))
            for j in range(3):
                vec(V.tensor_scalar(hit, order, float(j + 1), None, ALU.is_equal))
                vec(V.tensor_tensor(hit, hit, over, ALU.mult))
                vec(V.tensor_reduce(table[:, 16 + 4 + j:17 + 4 + j], hit, AX, ALU.max))
                vec(V.tensor_tensor(hit, hit, iota[:, 0:E], ALU.mult))
                vec(V.tensor_reduce(table[:, 16 + j:17 + j], hit, AX, ALU.add))
            vec(V.memset(table[:, 19:20], 0.0))
            vec(V.memset(table[:, 23:24], 0.0))
            table_ready = vec(V.tensor_copy(table_i[:, 16:24], table[:, 16:24]))
            fence()

            wg, wu, wd = A["moe_wg"][0], A["moe_wu"][0], A["moe_wd"][0]

            def expert(e_sync, e_dve, block):
                for t in range(TT):
                    a = dve.did(V.tensor_scalar(pick[:, t, :], iota, base[:, block, t, bass.ds(e_dve, 1)],
                                                r["sel"][:, t, bass.ds(e_dve, 1)], ALU.is_equal, ALU.mult))
                picked = a
                dve.after(a)
                for t in range(TT):
                    pickg_ready = dve.did(V.tensor_scalar(pickg[:, t, :], pick[:, t, :],
                                                          r["gate"][:, t, bass.ds(e_dve, 1)], None, ALU.mult))
                pe.after(picked)
                xs_ready = []
                for g in range(2):
                    for k in range(4):
                        for t in range(TT):
                            kk = 4 * g + k
                            mm = T.matmul(banks[6 + g][:, k * P:(k + 1) * P], h[:, t, kk * P:(kk + 1) * P],
                                          pick[:, t, :], start=(t == 0), stop=(t == TT - 1))
                    a = pe.did(mm)
                    en = (act, dve)[g]
                    en.after(a)
                    dst = xsT[:, 4 * g:4 * g + 4, :]
                    src = banks[6 + g][:, :].rearrange("p (k s) -> p k s", k=4)
                    bank_read[6 + g] = en.did(SC.copy(dst, src) if g == 0 else V.tensor_copy(dst, src))
                    xs_ready.append(bank_read[6 + g])
                pe.after(pickg_ready, bank_read[2])
                for t in range(TT):
                    mm = T.transpose(banks[2][:, t * P:(t + 1) * P], pickg[:, t, :], ident)
                a = pe.did(mm)
                act.after(a)
                pickT_ready = bank_read[2] = act.did(SC.copy(pickT, tile2(banks[2][:, 0:2 * P])))
                hid_free, waiting, hidT_ready = [None, None], None, []

                def turn(j, hid_done):
                    b = 2 + j % 2
                    pe.after(hid_done, bank_read[b])
                    for i in range(2):
                        mm = T.transpose(banks[b][:, i * P:(i + 1) * P], hid_s[j % 2][:, i * P:(i + 1) * P], ident)
                    a = pe.did(mm)
                    hid_free[j % 2] = a
                    act.after(a)
                    bank_read[b] = act.did(SC.copy(hidT[:, 2 * j:2 * j + 2, :], tile2(banks[b][:, 0:2 * P])))
                    hidT_ready.append(bank_read[b])

                for j in range(FT // 2):
                    b = j % 2
                    for half, w in ((0, wg), (1, wu)):
                        src = w[bass.ds(e_sync, 1), :, j * 256:(j + 1) * 256].rearrange("e (k p) n -> p (e k) n", p=P)
                        slot, view, arrived = ring.load(src, KT, 256)
                        pe.after(arrived, xs_ready)
                        if half == 0:
                            pe.after(bank_read[b])
                        for k in range(KT):
                            mm = T.matmul(banks[b][:, half * 256:(half + 1) * 256], xsT[:, k, :], view[:, k, :],
                                          start=(k == 0), stop=(k == KT - 1))
                        done = ring.release(slot, mm)
                        if half == 0:
                            gate_done = done
                    if waiting:
                        turn(*waiting)
                    act.after(gate_done, done, hid_free[b])
                    a = act.did(SC.activation(gate_s[b], banks[b][:, 0:256], ACT.Silu))
                    dve.after(a, done, hid_free[b])
                    bank_read[b] = dve.did(V.tensor_tensor(hid_s[b], banks[b][:, 256:512], gate_s[b], ALU.mult))
                    waiting = (j, bank_read[b])
                turn(*waiting)
                for i in range(FT // 2):
                    src = wd[bass.ds(e_sync, 1), i * 2 * P:(i + 1) * 2 * P, :].rearrange("e (k p) n -> p (e k) n", p=P)
                    slot, view, arrived = ring.load(src, 2, D)
                    pe.after(arrived, hidT_ready[i], bank_read[4], bank_read[5])
                    for k in range(2):
                        for half in range(2):
                            mm = T.matmul(banks[4 + half][:, :], hidT[:, 2 * i + k, :],
                                          view[:, k, half * 512:(half + 1) * 512],
                                          start=(i == 0 and k == 0), stop=(i == FT // 2 - 1 and k == 1))
                    done = ring.release(slot, mm)
                act.after(done)
                bank_read[4] = act.did(SC.copy(y[:, 0:512], banks[4][:, :]))
                dve.after(done)
                bank_read[5] = dve.did(V.tensor_copy(y[:, 512:D], banks[5][:, :]))
                pe.after(bank_read[4], bank_read[5], pickT_ready)
                for t in range(TT):
                    for half in range(2):
                        b = (6 if t == 0 else 2) + half
                        pe.after(bank_read[b])
                        a = pe.did(T.matmul(banks[b][:, :], pickT[:, t, :], y[:, half * 512:(half + 1) * 512],
                                            start=True, stop=True))
                        cols = total[:, t, half * 512:(half + 1) * 512]
                        dve.after(a, zeroed)
                        bank_read[b] = dve.did(V.tensor_tensor(cols, cols, banks[b][:, :], ALU.add))

            ring.align()
            with c.repeat("experts", E) as e:
                expert(e, e, 0)
                fence()
            ring.align()
            meet = c.sem("meet")
            everyone = (*computing, sync)
            with c.repeat("overflow", 3) as j:
                toks = [c.now(e_.sem) for e_ in computing] + [c.now(s) for s in ring.used + ring.filled]
                for e_ in everyone:
                    e_.after(*toks)
                    e_.q.sem_inc(meet.handle, 1)
                meet.count += len(everyone)
                for e_ in everyone:
                    e_._wait(c.now(meet))
                    e_.settle()
                who = nc.values_load(table_i[0:1, bass.ds(j + 16, 1)], min_val=0, max_val=E - 1)
                there = nc.values_load(table_i[0:1, bass.ds(j + 20, 1)], min_val=0, max_val=1)
                before_pass = {s.name: s.count for s in c.sems}
                with nc.If(there):
                    expert(who, who, 1)
                    fence()
                with nc.Else():
                    for s, owner in [(e_.sem, e_) for e_ in computing] + [(s, pe) for s in ring.used] + [
                            (s, sync) for s in ring.filled]:
                        if s.count > before_pass[s.name]:
                            owner.q.sem_inc(s.handle, s.count - before_pass[s.name])
            ring.align()
            out = []
            fence()
            for t in range(TT):
                a = dve.did(V.scalar_tensor_tensor(out=h[:, t, :], in0=h[:, t, :], scalar=ALPHA,
                                                   in1=total[:, t, :], op0=ALU.mult, op1=ALU.add))
                out.append(layer_norm(h, t, h, gains_ready, a))
            return out

        def dump(name, ap, toks):
            if name in A.get("dumps", {}):
                sync.after(*toks)
                d_ = c.raised(dumped, nc.sync.dma_start(A["dumps"][name].rearrange("(t p) d -> p t d", p=P), ap), 16)
                for e_ in computing:
                    e_.after(d_)

        dumped = c.sem("dumped") if A.get("dumps") else None
        dump("ln_in", h, h_ready)
        h_ready = first_mixer(0, h_ready)
        dump("mix0", h, h_ready)
        h_ready = dense_ffn(h_ready)
        dump("ffn0", h, h_ready)
        h_ready = first_mixer(1, h_ready)
        dump("mix1", h, h_ready)
        h_ready = moe_ffn(h_ready)
        dump("moe", h, h_ready)

        area = Area()
        second_const = area.take(A["const_second"].shape[1])

        def sc_(name):
            at, n = const_at["second"][name]
            return second_const[:, at:at + n]

        fence()
        const2 = load_small("const_second", (second_const, A["const_second"]))
        own_mask = sc_("own_mask").rearrange("p (g s) -> p g s", g=3)
        prev_mask = sc_("prev_mask").rearrange("p (g s) -> p g s", g=3)
        hg_levels = sc_("hg_levels").rearrange("p (l s) -> p l s", l=len(HG_LEVELS) + 1)
        scan_keep = sc_("scan_keep")
        rope_cos, rope_sin, rope_swap = sc_("rope_cos"), sc_("rope_sin"), sc_("rope_swap")

        cur = area.take(28)
        lbs = area.take(48)
        W4 = HG_HEADS * S
        qkT = area.take(24 * S, 24)
        v_att = area.take(TT * 1536, TT)
        gate_ab = area.take(16 * S, 16)
        hg_mark = area.at
        q_hg, z_f, k_hg, v_hg, g_hg = (area.take(W4, 4) for _ in range(5))
        v_hg = v_hg.rearrange("p a s -> p (a s)").rearrange("p (t n) -> p t n", t=TT)
        decay = area.take(W4)
        hg_att = area.take(HG_HEADS * 3 * P, HG_HEADS, 3)
        w0, w1, w2 = (area.take(W4) for _ in range(3))
        o_hgT = area.take(W4, 4)
        o_attT = area.take(W4, 4)
        late = Area(hg_mark)
        masked_s = late.take(9 * P)
        probs_T = late.take(9 * P)
        rope_tmp = area.take(512)
        hid2 = Area(hg_mark - 16 * S - TT * 1536 - 24 * S).take(NT2 * S, NT2)
        yT = hT
        lb_at = const_at["vecs"]["hg_lb"]
        lb0, lb1 = vecs[:, lb_at:lb_at + 4], vecs[:, lb_at + 4:lb_at + 8]
        dve.after(h_loaded)
        x_, n_, l_ = lbs[:, 16:20], lbs[:, 20:24], lbs[:, 24:28]
        a = dve.did(V.tensor_tensor(x_, lb1, lb0, ALU.subtract))
        dve.did(V.memset(lbs[:, 0:4], -1.0e30))
        dve.did(V.memset(lbs[:, 8:12], 0.0))
        dve.after(a)
        act.after(a)
        a = act.did(SC.activation(n_, x_, ACT.Abs))
        act.after(a)
        a = act.did(SC.activation(l_, n_, ACT.Exp, scale=-1.0))
        act.after(a)
        a = act.did(SC.activation(l_, l_, ACT.Ln, bias=1.0))
        dve.after(a)
        a = dve.did(V.scalar_tensor_tensor(out=lbs[:, 4:8], in0=x_, scalar=0.0, in1=l_, op0=ALU.min, op1=ALU.subtract))
        dve.after(a)
        dve.did(V.tensor_tensor(lbs[:, 12:16], lbs[:, 4:8], x_, ALU.subtract))
        fence()

        def second_layer(layer):
            vat = const_at["vecs"]["second"]
            dve.did(V.tensor_copy(cur[:, 0:20], vecs[:, bass.ds(layer * 20 + vat, 20)]))
            dve.did(V.tensor_copy(cur[:, 20:24], lbs[:, bass.ds(layer * 4, 4)]))
            cur_ready = dve.did(V.tensor_copy(cur[:, 24:28], lbs[:, bass.ds(layer * 4 + 8, 4)]))
            dve.after(cur_ready)
            xn = gains

            def normed(scales):
                ready = []
                for t in range(TT):
                    rstd, a = rms_scale(h, t, xn[:, t, :])
                    dve.after(a)
                    ready.append(dve.did(V.tensor_scalar(xn[:, t, :], h[:, t, :], rstd, None, ALU.mult)))
                return transpose_rows(xn, ready, hT, scales)

            hT_ready = normed(cur[:, 0:8])
            w = A["w_in_2"][bass.ds(layer, 1), :, :].rearrange("l (k p) n -> p (l k) n", p=P)

            turn = [0]
            ready = {}

            def columns(col, rows, finish):
                b = turn[0] % 4
                turn[0] += 1
                done = product(w[:, :, col * 256:(col + 1) * 256], KT, 256, hT, hT_ready, b, rows)
                e_, inst = finish(tile2(banks[b][:, :]), done)
                bank_read[b] = e_.did(inst)
                return bank_read[b]

            def through(fn, dst):
                def finish(src, done):
                    act.after(done)
                    return act, SC.activation(dst, src, fn)
                return finish

            def copied(dst):
                def finish(src, done):
                    dve.after(done)
                    return dve, V.tensor_copy(dst, src)
                return finish

            for i in range(2):
                ready["zf", i] = columns(2 + i, False, copied(z_f[:, 2 * i:2 * i + 2, :]))
            for i in range(2):
                ready["q", i] = columns(i, False, through(ACT.Silu, q_hg[:, 2 * i:2 * i + 2, :]))
            for i in range(2):
                ready["v", i] = columns(4 + i, True, copied(v_hg[:, :, i * 256:(i + 1) * 256]))
            for i in range(2):
                ready["g", i] = columns(6 + i, False, through(ACT.Sigmoid, g_hg[:, 2 * i:2 * i + 2, :]))

            def flat(ap):
                return ap.rearrange("p a s -> p (a s)")

            def per_head(cols):
                return cols.unsqueeze(2).to_broadcast((P, HG_HEADS, S))

            def as4(ap):
                return ap.rearrange("p (a s) -> p a s", a=HG_HEADS)

            def recurrence():
                zf = flat(z_f)
                act.after(ready["zf", 0], ready["zf", 1])
                a = act.did(SC.activation(w0, zf, ACT.Abs))
                act.after(a)
                a = act.did(SC.activation(w0, w0, ACT.Exp, scale=-1.0))
                act.after(a)
                a = act.did(SC.activation(w0, w0, ACT.Ln, bias=1.0))
                dve.after(a)
                a = dve.did(V.scalar_tensor_tensor(out=w1, in0=zf, scalar=0.0, in1=w0, op0=ALU.min, op1=ALU.subtract))
                dve.after(a)
                a = dve.did(V.tensor_tensor(as4(w1), as4(w1), per_head(cur[:, 24:28]), ALU.add))
                dve.after(a)
                a = dve.did(V.tensor_tensor(w2, w1, zf, ALU.subtract))
                act.after(a)
                k_ready = act.did(SC.activation(flat(k_hg), w2, ACT.Exp))
                yield
                a = dve.did(V.tensor_tensor(as4(w0), as4(w1), per_head(cur[:, 20:24]), ALU.subtract))
                b_ = dve.did(V.tensor_tensor(as4(w1), as4(w1), per_head(cur[:, 20:24]), ALU.max))
                act.after(a)
                a = act.did(SC.activation(w0, w0, ACT.Abs))
                act.after(a)
                a = act.did(SC.activation(w0, w0, ACT.Exp, scale=-1.0))
                act.after(a)
                a = act.did(SC.activation(w0, w0, ACT.Ln, bias=1.0))
                dve.after(a, b_)
                a = dve.did(V.tensor_tensor(w1, w1, w0, ALU.add))
                dve.after(a)
                a = dve.did(V.tensor_tensor_scan(decay, scan_keep, w1, 0.0, ALU.mult, ALU.add))
                dve.after(a)
                yield
                dec4 = as4(decay)
                att = hg_att
                cleared = pool.did(G.memset(att[:, :, 0:2, :], 0.0))
                qf, kf = flat(q_hg), flat(k_hg)
                last = dec4[:, :, P - 1:P].to_broadcast((P, HG_HEADS, P))
                a = dve.did(V.tensor_tensor(as4(w0)[:, :, 0:P], last, dec4[:, :, 0:P], ALU.subtract))
                act.after(a)
                a1 = act.did(SC.activation(as4(w0)[:, :, 0:P], as4(w0)[:, :, 0:P], ACT.Exp))
                a2 = act.did(SC.activation(as4(w0)[:, :, P:S], dec4[:, :, P:S], ACT.Exp))
                dve.after(a1, a2, k_ready, ready["q", 0], ready["q", 1])
                dve.did(V.tensor_tensor(as4(w1)[:, :, 0:P], as4(w0)[:, :, 0:P], k_hg[:, :, 0:P], ALU.mult))
                a = dve.did(V.tensor_tensor(as4(w1)[:, :, P:S], as4(w0)[:, :, P:S], q_hg[:, :, P:S], ALU.mult))
                pe.after(a, bank_read[4])
                for hh in range(HG_HEADS):
                    mm = T.matmul(banks[4][:, hh * P:(hh + 1) * P], as4(w1)[:, hh, 0:P], as4(w1)[:, hh, P:S],
                                  start=True, stop=True)
                a = pe.did(mm)
                dve.after(a)
                bank_read[4] = dve.did(V.tensor_copy(att[:, :, 2, :], banks[4][:, :].rearrange("p (a s) -> p a s", a=4)))
                dve.after(bank_read[4])
                yield
                for li, m in enumerate(HG_LEVELS + (0,)):
                    if m:
                        blocks = decay.rearrange("p (n s) -> p n s", s=2 * m)
                        ref = blocks[:, :, m - 1:m].to_broadcast((P, W4 // (2 * m), 2 * m))
                        a = dve.did(V.tensor_tensor(w0.rearrange("p (n s) -> p n s", s=2 * m), blocks, ref,
                                                    ALU.subtract))
                        dve.after(a)
                        a = dve.did(V.scalar_tensor_tensor(out=w0, in0=w0, scalar=-1.0, in1=w0, op0=ALU.mult,
                                                           op1=ALU.min))
                        act.after(a)
                        a = act.did(SC.activation(w0, w0, ACT.Exp))
                        dve.after(a, k_ready)
                        qa = dve.did(V.tensor_tensor(w1, w0, qf, ALU.mult))
                        ka = dve.did(V.tensor_tensor(w2, w0, kf, ALU.mult))
                        qs, ks = as4(w1), as4(w2)
                        pe.after(qa, ka)
                    else:
                        qs, ks = q_hg, k_hg
                    b = 4 + 2 * (li % 2)
                    pe.after(bank_read[b], bank_read[b + 1])
                    for hh in range(HG_HEADS):
                        for n in range(2):
                            mm = T.matmul(banks[b + n][:, hh * P:(hh + 1) * P], ks[:, hh, n * P:(n + 1) * P],
                                          qs[:, hh, n * P:(n + 1) * P], start=True, stop=True)
                    a = pe.did(mm)
                    yield
                    dve.after(a, cleared)
                    mask = hg_levels[:, li, :].unsqueeze(1).to_broadcast((P, HG_HEADS, P)).bitcast(I32)
                    dve.settle()
                    for n in range(2):
                        bank_read[b + n] = dve.did(V.copy_predicated(
                            att[:, :, n, :], mask, banks[b + n][:, :].rearrange("p (a s) -> p a s", a=4)))
                    dve.after(bank_read[b + 1])
                pe.after(bank_read[b + 1], ready["v", 0], ready["v", 1], bank_read[4], bank_read[5])
                for hh in range(HG_HEADS):
                    o_ = banks[4 + hh // 2][:, (hh % 2) * S:(hh % 2) * S + S]
                    cols = slice(hh * P, (hh + 1) * P)
                    T.matmul(o_[:, 0:P], v_hg[:, 0, cols], att[:, hh, 0, :], start=True, stop=True)
                    T.matmul(o_[:, P:S], v_hg[:, 0, cols], att[:, hh, 2, :], start=True, stop=False)
                    mm = T.matmul(o_[:, P:S], v_hg[:, 1, cols], att[:, hh, 1, :], start=False, stop=True)
                a = pe.did(mm)
                yield
                for n in range(2):
                    act.after(a)
                    sq = act.did(SC.activation(w0[:, n * 512:(n + 1) * 512], banks[4 + n][:, :], ACT.Square))
                    pe.after(sq, bank_read[6 + n])
                    mm = pe.did(T.matmul(banks[6 + n][:, :], ones, w0[:, n * 512:(n + 1) * 512], start=True, stop=True))
                    dve.after(mm)
                    cols = w1[:, n * 512:(n + 1) * 512]
                    a_ = bank_read[6 + n] = dve.did(V.tensor_scalar(cols, banks[6 + n][:, :], 1.0 / P, RMS_EPS,
                                                                    ALU.mult, ALU.add))
                    dve.after(inverse_root(cols, a_))
                    a_ = bank_read[4 + n] = dve.did(V.tensor_tensor(cols, cols, banks[4 + n][:, :], ALU.mult))
                    dve.after(a_)
                dve.after(ready["g", 0], ready["g", 1])
                a_ = dve.did(V.tensor_tensor(as4(w1), as4(w1), per_head(cur[:, 16:20]), ALU.mult))
                dve.after(a_)
                ready["o_hg"] = dve.did(V.tensor_tensor(o_hgT, as4(w1), g_hg, ALU.mult))
                yield

            side = recurrence()

            def rope(j, copied_tok):
                b = 7 if False else 3
                pe.after(copied_tok, bank_read[b])
                part = qkT[0:ROPE_DIM, 2 * j:2 * j + 2, :]
                pe.settle()
                a = pe.did(T.matmul(banks[b][0:ROPE_DIM, :], rope_swap[0:ROPE_DIM, :], flat(part), start=True, stop=True))
                sin = rope_sin[0:ROPE_DIM, :].unsqueeze(1).to_broadcast((ROPE_DIM, 2, S))
                cos = rope_cos[0:ROPE_DIM, :].unsqueeze(1).to_broadcast((ROPE_DIM, 2, S))
                tmp = tile2(rope_tmp[0:ROPE_DIM, :])
                dve.after(a)
                a1 = bank_read[b] = dve.did(V.tensor_tensor(tmp, tile2(banks[b][0:ROPE_DIM, :]), sin, ALU.mult))
                a2 = dve.did(V.tensor_tensor(part, part, cos, ALU.mult))
                dve.after(a1, a2)
                a = dve.did(V.tensor_tensor(part, part, tmp, ALU.add))
                dve.after(a)
                return a

            def columns3(col, rows, finish):
                b = turn[0] % 3
                turn[0] += 1
                done = product(w[:, :, col * 256:(col + 1) * 256], KT, 256, hT, hT_ready, b, rows)
                e_, inst = finish(tile2(banks[b][:, :]), done)
                bank_read[b] = e_.did(inst)
                return bank_read[b]

            qk_ready, pending = [], None
            for j in range(12):
                tok = columns3(8 + j, False, through(ACT.Copy, qkT[:, 2 * j:2 * j + 2, :]))
                if pending:
                    qk_ready.append(rope(*pending))
                pending = (j, tok)
                next(side, None)
            qk_ready.append(rope(*pending))
            for j in range(6):
                ready["va", j] = columns3(20 + j, True, through(ACT.Copy, v_att[:, :, j * 256:(j + 1) * 256]))
                next(side, None)
            for _ in side:
                pass

            def attention():
                scale = float(P) ** -0.5
                dve.after(ready["o_hg"])
                act.after(ready["o_hg"])
                first, second = masked_s[:, 0:384], masked_s[:, 384:1152]
                sec4 = second.rearrange("p (g n s) -> p g n s", g=3, n=2)
                for hd in range(ATT_HEADS):
                    st = stats[:, 48:56]
                    pe.after(qk_ready, bank_read[4], bank_read[5], bank_read[6])
                    for g in range(ATT_GROUPS):
                        q_, k_ = qkT[:, g * 4 + hd, :], qkT[:, 12 + g * 4 + hd, :]
                        T.matmul(banks[4][:, g * P:(g + 1) * P], q_[:, 0:P], k_[:, 0:P], start=True, stop=True)
                        dst = banks[5 + g // 2][:, (g % 2) * S:(g % 2) * S + S]
                        mm = T.matmul(dst, q_[:, P:S], k_, start=True, stop=True)
                    a = pe.did(mm)
                    yield
                    dve.after(a)
                    bank_read[4] = dve.did(V.scalar_tensor_tensor(
                        out=first.rearrange("p (g s) -> p g s", g=3), in0=banks[4][:, 0:384].rearrange(
                            "p (g s) -> p g s", g=3), scalar=scale, in1=own_mask, op0=ALU.mult, op1=ALU.add))
                    for b, g0, ng in ((5, 0, 2), (6, 2, 1)):
                        src = banks[b][:, 0:ng * S].rearrange("p (g n s) -> p g n s", g=ng, n=2)
                        for n, mask in ((0, prev_mask), (1, own_mask)):
                            bank_read[b] = dve.did(V.scalar_tensor_tensor(
                                out=sec4[:, g0:g0 + ng, n, :], in0=src[:, :, n, :], scalar=scale,
                                in1=mask[:, g0:g0 + ng, :], op0=ALU.mult, op1=ALU.add))
                    dve.after(bank_read[6])
                    dve.did(V.tensor_reduce(st[:, 0:1], first, AX, ALU.max))
                    a = dve.did(V.tensor_reduce(st[:, 1:2], second, AX, ALU.max))
                    dve.after(a)
                    a = dve.did(V.tensor_scalar(st[:, 2:4], st[:, 0:2], -1.0, None, ALU.mult))
                    act.after(a)
                    act.did(SC.activation(first, first, ACT.Exp, bias=st[:, 2:3], accum_out=st[:, 4:5]))
                    a = act.did(SC.activation(second, second, ACT.Exp, bias=st[:, 3:4], accum_out=st[:, 5:6]))
                    dve.after(a)
                    a = dve.did(V.reciprocal(st[:, 6:8], st[:, 4:6]))
                    dve.after(a)
                    dve.did(V.tensor_scalar(first, first, st[:, 6:7], None, ALU.mult))
                    a = dve.did(V.tensor_scalar(second, second, st[:, 7:8], None, ALU.mult))
                    yield
                    pe.after(a)
                    for b in range(3):
                        pe.after(bank_read[4 + b])
                        for i in range(3):
                            mm = T.transpose(banks[4 + b][:, i * P:(i + 1) * P],
                                             masked_s[:, (3 * b + i) * P:(3 * b + i + 1) * P], ident)
                        a = pe.did(mm)
                        e_ = (act, dve, act)[b]
                        e_.after(a)
                        dst, src = probs_T[:, 3 * b * P:3 * (b + 1) * P], banks[4 + b][:, 0:384]
                        bank_read[4 + b] = e_.did(V.tensor_copy(dst, src) if b == 1 else SC.copy(dst, src))
                    yield
                    pe.after(bank_read[4], bank_read[5], bank_read[6], bank_read[7], *[ready["va", j] for j in range(6)])
                    for g in range(ATT_GROUPS):
                        cols = slice((g * 4 + hd) * P, (g * 4 + hd + 1) * P)
                        T.matmul(banks[7][:, 0:P], v_att[:, 0, cols], probs_T[:, g * P:(g + 1) * P],
                                 start=(g == 0), stop=(g == 2))
                    for g in range(ATT_GROUPS):
                        cols = slice((g * 4 + hd) * P, (g * 4 + hd + 1) * P)
                        for n in range(2):
                            at = (3 + 2 * g + n) * P
                            mm = T.matmul(banks[7][:, P:S], v_att[:, n, cols], probs_T[:, at:at + P],
                                          start=(g == 0 and n == 0), stop=(g == 2 and n == 1))
                    a = pe.did(mm)
                    act.after(a)
                    bank_read[7] = ready["o_att", hd] = act.did(SC.copy(o_attT[:, hd, :], banks[7][:, 0:S]))
                    dve.after(bank_read[7])
                    yield

            side = attention()
            for j in range(8):
                ready["ab", j] = columns(26 + j, False, through(ACT.Sigmoid, gate_ab[:, 2 * j:2 * j + 2, :]))
                for _ in range(2):
                    next(side, None)
            for _ in side:
                pass

            ab_ready = [ready["ab", j] for j in range(8)]
            for which, name, src, src_ready in ((0, "w_branch_a_2", o_hgT, ready["o_hg"]),
                                                (1, "w_branch_b_2", o_attT, ready["o_att", 3])):
                wv = A[name][bass.ds(layer, 1), :, :].rearrange("l (k p) n -> p (l k) n", p=P)
                for i in range(2):
                    slot, view, arrived = ring.load(wv[:, :, i * 512:(i + 1) * 512], 4, 512)
                    pe.after(arrived, src_ready)
                    for jj in range(2):
                        b = turn[0] % 4
                        turn[0] += 1
                        pe.after(bank_read[b])
                        for u in range(2):
                            for k in range(4):
                                cc = (2 * jj + u) * P
                                mm = T.matmul(banks[b][:, u * S:(u + 1) * S], view[:, k, cc:cc + P], src[:, k, :],
                                              start=(k == 0), stop=(k == 3))
                        a = ring.release(slot, mm) if jj == 1 else pe.did(mm)
                        tiles = slice(4 * i + 2 * jj, 4 * i + 2 * jj + 2)
                        gates = gate_ab[:, 8 * which + 4 * i + 2 * jj:8 * which + 4 * i + 2 * jj + 2, :]
                        dve.after(a, ab_ready)
                        bank_read[b] = dve.did(V.tensor_tensor(gates, tile2(banks[b][:, :]), gates, ALU.mult))
                        if which == 1:
                            dve.after(bank_read[b])
                            yT_ready = dve.did(V.tensor_tensor(yT[:, tiles, :], gates,
                                                               gate_ab[:, tiles, :], ALU.add))

            def add_to_residual(done):
                for t in range(TT):
                    for half in range(2):
                        b = 4 + 2 * t + half
                        cols = h[:, t, half * 512:(half + 1) * 512]
                        dve.after(done)
                        bank_read[b] = dve.did(V.tensor_tensor(cols, cols, banks[b][:, :], ALU.add))
                dve.after(bank_read[7])
                act.after(bank_read[7])

            w_rows = A["w_out_2"][bass.ds(layer, 1), :, :].rearrange("l r n -> (l r) n")
            add_to_residual(accumulate(w_rows, KT, yT, yT_ready, 4))

            fence()
            hT_ready = normed(cur[:, 8:16])
            wup = A["w_up_2"][bass.ds(layer, 1), :, :].rearrange("l (k p) n -> p (l k) n", p=P)
            hid_ready = []
            for j in range(NT2 // 2):
                b = j % 4
                done = product(wup[:, :, j * 256:(j + 1) * 256], KT, 256, hT, hT_ready, b, rows=False)
                out = hid2[:, 2 * j:2 * j + 2, :]
                act.after(done)
                a = act.did(SC.activation(out, tile2(banks[b][:, :]), ACT.Relu))
                bank_read[b] = a
                pool.after(a)
                hid_ready.append(pool.did(G.tensor_tensor(out, out, out, ALU.mult)))
            w_rows = A["w_down_2"][bass.ds(layer, 1), :, :].rearrange("l r n -> (l r) n")
            add_to_residual(accumulate(w_rows, NT2, hid2, hid_ready, 4))
            fence()

        act.after(const2)
        for e_ in (pe, dve, pool):
            e_.after(const2)
        ring.align()
        with c.repeat("layers", DEPTH) as layer:
            second_layer(layer)
            ring.align()

        fence()
        final = load_small("final", (gains[:, 0, :], A["final_norm_g_2"].partition_broadcast(P)))
        out_sem = c.sem("stored")
        for t in range(TT):
            rstd, a = rms_scale(h, t, gains[:, 1, :])
            dve.after(a, final)
            a = dve.did(V.scalar_tensor_tensor(out=h[:, t, :], in0=h[:, t, :], scalar=rstd, in1=gains[:, 0, :],
                                               op0=ALU.mult, op1=ALU.mult))
            sync.after(a)
            stored = c.raised(out_sem, nc.sync.dma_start(A["out"][0, t * P:(t + 1) * P, :], h[:, t, :]), 16)
            act.after(a)
        sync.after(stored)
    return c.seen


INPUTS = ("x", "ln_in_g", "ln_in_b", "w_in", "pool_w", "w_out", "ln1_g", "ln1_b", "ffn_wg", "ffn_wu", "ffn_wd",
          "moe_router", "moe_wg", "moe_wu", "moe_wd", "ln2_g", "ln2_b", "w_in_2", "w_branch_a_2", "w_branch_b_2",
          "w_out_2", "w_up_2", "w_down_2", "final_norm_g_2")


def lay_out(inputs):
    shared, first, second = shape_constants()
    arrays, at = {}, {}
    arrays["const_shared"], at["shared"] = packed(shared)
    arrays["const_first"], at["first"] = packed(first)
    arrays["const_second"], at["second"] = packed(second)

    def by_partition(a):
        return np.asarray(a).reshape(-1, P).T

    cols = [by_partition(inputs["pool_scale"]), by_partition(inputs["hg_lower_bounds_2"])]
    for layer in range(DEPTH):
        cols += [by_partition(inputs[n][layer]) for n in ("norm1_g_2", "norm2_g_2", "hg_norm_g_2")]
    arrays["vecs"] = np.ascontiguousarray(np.concatenate(cols, 1))
    at["vecs"] = {"pool_scale": 0, "hg_lb": 8, "second": 16}
    for n in INPUTS:
        a = np.ascontiguousarray(inputs[n])
        arrays[n] = a.reshape(1, -1) if a.ndim == 1 else a
    return arrays, at


def declare(nc, arrays):
    A = {}
    for n, a in arrays.items():
        A[n] = nc.dram_tensor("in_" + n, a.shape, F32, kind="ExternalInput").ap()
    A["out"] = nc.dram_tensor("out_0", (1, S, D), F32, kind="ExternalOutput").ap()
    return A


def kernel(**inputs):
    import concourse.bacc as bacc
    from concourse.bass_utils import run_bass_kernel_spmd

    arrays, at = lay_out(inputs)
    plan = {}
    for _ in range(2):
        nc = bacc.Bacc("TRN2", target_bir_lowering=False, num_devices=1)
        plan = write_program(nc, declare(nc, arrays), at, plan)
    got = run_bass_kernel_spmd(nc, [{"in_" + n: a for n, a in arrays.items()}], core_ids=[0])
    return got.results[0]["out_0"]
```

```python
from contextlib import ExitStack, contextmanager

import numpy as np

import concourse.bass as bass
from concourse import mybir

F32 = mybir.dt.float32
F32R = mybir.dt.float32r
I8 = mybir.dt.int8
I32 = mybir.dt.int32
ALU = mybir.AluOpType
ACT = mybir.ActivationFunctionType
AX = mybir.AxisListType.X

P = 128
D = 1024
S = 256
TT = S // P
KT = D // P
DEPTH = 2
ALPHA = (2 * DEPTH) ** 0.25
LN_EPS = 1e-5
RMS_EPS = 1e-6

POOL_W = 512
POOL_WINDOWS = (2, 4, 8, 16)
SB_HEADS = 8
SB_DIM = 64
FF = 2816
FT = FF // P
E = 8
SLOTS = 128

HG_HEADS = 4
ATT_HEADS = 4
ATT_GROUPS = 3
DILATIONS = (1, 4, 16)
ROPE_DIM = 32
ROPE_THETA = 500000.0
FF2 = 4096
NT2 = FF2 // P
BIG = 30000.0

CHUNK = 2048
RAW = 5
PIECE = CHUNK // 2
PAIRS = 4
AHEAD = PAIRS - 1

MIXER_STEPS = 3
LAYER_STEPS = 2

HG_LEVELS = (64, 32, 16, 8, 4, 2, 1)



def shape_constants():
    i = np.arange(P)
    part, free = i[:, None], i[None, :]
    f = np.float32
    c = {}
    c["ident"] = np.eye(P, dtype=f)
    c["ones"] = np.ones((P, P), f)
    c["neg_ge"] = -(part >= free).astype(f)
    c["neg_ones"] = -np.ones((P, P), f)
    c["before"] = (part < free).astype(f)
    c["before_bias"] = np.where(part < free, 0.0, -BIG).astype(f)
    c["upto"] = (part <= free).astype(f)
    c["iota"] = np.broadcast_to(free, (P, P)).astype(f)
    t = np.arange(S)
    c["inv_count"] = np.broadcast_to(
        np.concatenate([1.0 / np.minimum(t + 1, w) for w in POOL_WINDOWS])[None], (P, 4 * S)).astype(f)
    first = {k: v.copy() for k, v in c.items() if k not in ("ident", "ones")}
    shared = {k: c[k] for k in ("ident", "ones")}
    second = {}
    for name, gap in (("own_mask", 0), ("prev_mask", P)):
        delta = part + gap - free
        ok = [(delta >= 0) & (delta % dil == 0) & (delta <= P * dil) for dil in DILATIONS]
        second[name] = np.concatenate([np.where(o, 0.0, -BIG * 1e26) for o in ok], 1).astype(f)
    lv = [(part // (2 * m) == free // (2 * m)) & (part % (2 * m) < m) & (free % (2 * m) >= m) for m in HG_LEVELS]
    levels = np.concatenate(lv + [part == free], 1).astype(f)
    inv = ROPE_THETA ** (-np.arange(0, ROPE_DIM, 2, dtype=f) / f(ROPE_DIM))
    ang = np.arange(S, dtype=f)[None, :] * inv.astype(f)[:, None]
    pad = np.zeros((P - ROPE_DIM, S), f)
    second["rope_cos"] = np.concatenate([np.cos(ang), np.cos(ang), pad]).astype(f)
    second["rope_sin"] = np.concatenate([np.sin(ang), np.sin(ang), pad]).astype(f)
    half = ROPE_DIM // 2
    swap = np.zeros((P, ROPE_DIM), f)
    for m in range(half):
        swap[m + half, m] = -1.0
        swap[m, m + half] = 1.0
    second["rope_swap"] = swap
    return shared, first, second, levels


def packed(parts):
    where, at = {}, 0
    for k, v in parts.items():
        where[k] = (at, v.shape[1])
        at += v.shape[1]
    return np.ascontiguousarray(np.concatenate(list(parts.values()), 1)), where



class Sem:

    def __init__(self, handle, name):
        self.handle, self.name, self.count = handle, name, 0


class Tok:

    def __init__(self, sem, count, loop):
        self.sem, self.count, self.loop = sem, count, loop


class Loop:
    def __init__(self, name, index, trips, start):
        self.name, self.index, self.trips, self.start, self.open = name, index, trips, start, True


class Counters:

    def __init__(self, nc, ctx, plan):
        self.nc, self.ctx, self.plan, self.seen = nc, ctx, plan, {}
        self.loop, self.sems = None, []

    def sem(self, name):
        s = Sem(self.ctx.enter_context(self.nc.semaphore(name)), name)
        self.sems.append(s)
        return s

    def raised(self, sem, inst, by=1):
        inst.then_inc(sem.handle, by)
        sem.count += by
        return Tok(sem, sem.count, self.loop)

    def now(self, sem):
        return Tok(sem, sem.count, self.loop)

    def value(self, tok):
        lp = tok.loop
        if lp is None:
            if self.loop is None:
                return tok.count
            return tok.count
        step = self.plan.get(lp.name, {}).get(tok.sem.name, 0)
        if lp.open:
            return lp.index * step + tok.count if step else tok.count
        return tok.count + (lp.trips - 1) * step

    @contextmanager
    def repeat(self, name, trips):
        with self.nc.Fori(0, trips) as i:
            lp = Loop(name, i, trips, {s.name: s.count for s in self.sems})
            self.loop = lp
            yield i
            adds = {s.name: s.count - lp.start[s.name] for s in self.sems}
            self.seen[name] = adds
            lp.open, self.loop = False, None
        for s in self.sems:
            s.count = lp.start[s.name] + trips * adds[s.name]


class Engine:

    def __init__(self, counters, queue, name):
        self.c, self.q = counters, queue
        self.sem = counters.sem("done_" + name)
        self.settled = counters.sem("settled_" + name)
        self.known = {}

    def after(self, *toks):
        best = {}
        for t in toks:
            if isinstance(t, (list, tuple)):
                self.after(*t)
            elif t is not None:
                if t.sem.name not in best or best[t.sem.name].count < t.count or best[t.sem.name].loop is not t.loop:
                    if t.sem.name in best and best[t.sem.name].loop is not t.loop:
                        self._wait(best[t.sem.name])
                    best[t.sem.name] = t
        for t in best.values():
            self._wait(t)

    def _wait(self, t):
        key = (t.sem.name, id(t.loop), id(self.c.loop))
        if self.known.get(key, -1) >= t.count:
            return
        self.known[key] = t.count
        self.q.wait_ge(t.sem.handle, self.c.value(t))

    def did(self, inst):
        return self.c.raised(self.sem, inst)

    def settle(self):
        self.q.sem_inc(self.settled.handle, 1)


class Piece:

    def __init__(self, high, low, ready, pair):
        self.high, self.low, self.ready, self.pair = high, low, ready, pair


class Weights:

    def __init__(self, c, ctx, nc, sync, pe, act, dve):
        self.c, self.nc, self.sync, self.pe, self.act, self.dve = c, nc, sync, pe, act, dve

        def sb(name, n, dt):
            return ctx.enter_context(nc.sbuf_tensor(name, [P, n], dt))

        self.raw = [sb(f"raw{i}", CHUNK, F32) for i in range(RAW)]
        self.high = [sb(f"high{i}", PIECE, F32R) for i in range(PAIRS)]
        self.low = [sb(f"low{i}", PIECE, F32R) for i in range(PAIRS)]
        self.landed = [c.sem(f"landed{i}") for i in range(RAW)]
        self.first_half = [c.sem(f"first_half{i}") for i in range(RAW)]
        self.split = [c.sem(f"split{i}") for i in range(RAW)]
        self.used = [c.sem(f"used{i}") for i in range(PAIRS)]
        self.wanted, self.ready = [], []
        self.align()

    def align(self):
        assert not self.wanted and not self.ready
        self.slot = self.pair = 0

    def want(self, a, b, *loads):
        self.wanted += [(a, b, loads, 0), (a, b, loads, 1)]

    def _prepare(self):
        a, b, loads, half = self.wanted.pop(0)
        i, p = self.slot, self.pair
        raw = self.raw[i][:, :].rearrange("p (a b) -> p a b", a=a)
        if half == 0:
            self.sync.after(self.c.now(self.split[i]))
            if self.c.loop is not None:
                self.sync.settle()
            for lo, hi, src in loads:
                self.c.raised(self.landed[i], self.sync.q.dma_start(raw[:, :, lo:hi], src), 16)
        rows = a // 2
        src = raw[:, half * rows:(half + 1) * rows, :]
        high, low = (x[p][:, :].rearrange("p (a b) -> p a b", a=rows) for x in (self.high, self.low))
        self.act.after(self.c.now(self.landed[i]), self.c.now(self.used[p]))
        made = self.act.did(self.nc.scalar.copy(high, src))
        self.dve.after(made)
        inst = self.nc.vector.tensor_tensor(low, src, high.bitcast(F32), ALU.subtract)
        ready = self.c.raised((self.first_half, self.split)[half][i], inst)
        self.ready.append(Piece(high, low, ready, p))
        self.pair = (p + 1) % PAIRS
        if half:
            self.slot = (i + 1) % RAW

    def fetch(self):
        while self.wanted and len(self.ready) <= AHEAD:
            self._prepare()
        piece = self.ready.pop(0)
        self.pe.after(piece.ready)
        return piece

    def release(self, piece, inst):
        return self.c.raised(self.used[piece.pair], inst)


def write_program(nc, A, const_at, plan):
    ctx = ExitStack()
    c = Counters(nc, ctx, plan)
    with ctx:
        pe = Engine(c, nc.tensor, "pe")
        dve = Engine(c, nc.vector, "dve")
        act = Engine(c, nc.scalar, "act")
        pool = Engine(c, nc.gpsimd, "pool")
        sync = Engine(c, nc.sync, "sync")
        computing = (pe, dve, act, pool)
        V, G, SC, T = nc.vector, nc.gpsimd, nc.scalar, nc.tensor

        def sb(name, n, dt=F32, parts=P):
            return ctx.enter_context(nc.sbuf_tensor(name, [parts, n], dt))

        weights = Weights(c, ctx, nc, sync, pe, act, dve)
        h = sb("h", TT * D)[:, :].rearrange("p (t d) -> p t d", t=TT)
        xH = sb("x_high", KT * S, F32R)[:, :].rearrange("p (k s) -> p k s", k=KT)
        xL = sb("x_low", KT * S, F32R)[:, :].rearrange("p (k s) -> p k s", k=KT)
        gains = sb("gains", 2 * D)[:, :].rearrange("p (i d) -> p i d", i=2)
        shared = sb("shared", A["const_shared"].shape[1])
        vecs = sb("vecs", A["vecs"].shape[1])
        stats = sb("stats", 64)
        tables = sb("tables", 64)
        banks = [ctx.enter_context(nc.psum_tensor(f"bank{i}", [P, 512], F32)) for i in range(8)]
        bank_read = [None] * 8

        def shared_const(name):
            at, n = const_at["shared"][name]
            return shared[:, at:at + n]

        ident, ones = shared_const("ident"), shared_const("ones")

        class Area:

            def __init__(self, name):
                self.name, self.stack, self.n = name, ExitStack(), 0

            def take(self, n, a=None, b=None, dt=F32):
                self.n += 1
                v = self.stack.enter_context(nc.sbuf_tensor(f"{self.name}{self.n}", [P, n], dt))[:, :]
                if b is not None:
                    return v.rearrange("p (a b c) -> p a b c", a=a, b=b)
                return v if a is None else v.rearrange("p (a b) -> p a b", a=a)

            def take_split(self, n, a):
                return self.take(n, a, dt=F32R), self.take(n, a, dt=F32R)

            def close(self):
                self.stack.close()

        def fence():
            toks = [c.now(e.sem) for e in computing] + [
                c.now(s) for s in weights.used + weights.split + weights.first_half]
            for e in computing:
                e.after(*toks)
                if c.loop is not None:
                    e.settle()
            for i in range(8):
                bank_read[i] = None

        def load_small(name, *pairs):
            arrived = c.sem("loaded_" + name)
            for dst, src in pairs:
                tok = c.raised(arrived, nc.scalar.dma_start(dst, src), 16)
            return tok

        def tile2(ap):
            return ap.rearrange("p (t n) -> p t n", t=2)

        sides = []

        def side_steps(n):
            for _ in range(n):
                if sides:
                    g = sides.pop(0)
                    if next(g, "end") != "end":
                        sides.append(g)

        def finish_sides():
            while sides:
                side_steps(1)


        def split(src, dst, ready):
            act.after(ready)
            a = act.did(SC.copy(dst[0], src))
            dve.after(a, ready)
            return dve.did(V.tensor_tensor(dst[1], src, dst[0].bitcast(F32), ALU.subtract))

        def three(out, stationary, moving, start, stop):
            T.matmul(out, stationary[0], moving[0], start=start, stop=False, skip_group_check=True)
            T.matmul(out, stationary[0], moving[1], start=False, stop=False, skip_group_check=True)
            return T.matmul(out, stationary[1], moving[0], start=False, stop=stop, skip_group_check=True)

        def want_columns(w, n):
            weights.want(KT, 256, (0, 256, w[:, :, n * 256:(n + 1) * 256]))

        def want_rows(w, tiles):
            for i in range(tiles // 2):
                weights.want(2, D, (0, D, w[i * 2 * P:(i + 1) * 2 * P, :].rearrange("(k p) n -> p k n", p=P)))

        def product(x, ready, bank, rows, steps=0):
            pe.after(ready, bank_read[bank])
            out = tile2(banks[bank][:, :])
            for half in range(2):
                piece = weights.fetch()
                for j in range(2):
                    for kk in range(KT // 2):
                        k = half * (KT // 2) + kk
                        mine = [v[:, k, j * P:(j + 1) * P] if rows else v[:, k, :] for v in x]
                        w = [v[:, kk, :] if rows else v[:, kk, j * P:(j + 1) * P] for v in (piece.high, piece.low)]
                        mm = three(out[:, j, :], mine if rows else w, w if rows else mine,
                                   start=(k == 0 and j == 0), stop=(k == KT - 1))
                done = weights.release(piece, mm)
                side_steps(steps)
            return done

        def accumulate(tiles, x, ready, first_bank, steps=0):
            for i in range(tiles):
                piece = weights.fetch()
                pe.after(ready(i) if callable(ready) else ready[i // 2] if isinstance(ready, list) else ready)
                if i == 0:
                    pe.after(*[bank_read[first_bank + b] for b in range(4)])
                    for b in range(4):
                        bank_read[first_bank + b] = None
                for t in range(TT):
                    for half in range(2):
                        mm = three(banks[first_bank + 2 * t + half][:, :],
                                   [v[:, i, t * P:(t + 1) * P] for v in x],
                                   [v[:, 0, half * 512:(half + 1) * 512] for v in (piece.high, piece.low)],
                                   start=(i == 0), stop=(i == tiles - 1))
                done = weights.release(piece, mm)
                side_steps(steps)
            return done

        def transpose_rows(src, src_ready):
            last = []
            for t in range(TT):
                for g in range(KT // 4):
                    b = 2 * t + g
                    pe.after(src_ready[t], bank_read[b])
                    for k in range(4):
                        mm = T.transpose(banks[b][:, k * P:(k + 1) * P],
                                         src[:, t, (4 * g + k) * P:(4 * g + k + 1) * P], ident)
                    done = pe.did(mm)
                    dst = [v[:, 4 * g:4 * g + 4, t * P:(t + 1) * P] for v in (xH, xL)]
                    bank_read[b] = split(banks[b][:, :].rearrange("p (k s) -> p k s", k=4), dst, done)
                    last.append(bank_read[b])
            return last

        def inverse_root(x, ready):
            act.after(ready)
            a = act.did(SC.activation(x, x, ACT.Ln))
            act.after(a)
            return act.did(SC.activation(x, x, ACT.Exp, scale=-0.5))

        def layer_norm(x, t, dst, gains_ready, *ready):
            st = stats[:, 16 * t:16 * t + 12].rearrange("p (a b) -> p a b", a=2)
            mv = stats[:, 16 * t + 12:16 * t + 14]
            rstd = stats[:, 16 * t + 14:16 * t + 15]
            dve.after(*ready)
            for i in range(2):
                a = dve.did(V.bn_stats(st[:, i, :], x[:, t, i * 512:(i + 1) * 512]))
            dve.after(a)
            a = dve.did(V.bn_aggr(mv, st))
            dve.after(a)
            a = dve.did(V.tensor_scalar(rstd, mv[:, 1:2], LN_EPS, None, ALU.add))
            dve.after(inverse_root(rstd, a))
            a = dve.did(V.tensor_scalar(dst[:, t, :], x[:, t, :], mv[:, 0:1], rstd, ALU.subtract, ALU.mult))
            dve.after(a, gains_ready)
            a = dve.did(V.tensor_tensor(dst[:, t, :], dst[:, t, :], gains[:, 0, :], ALU.mult))
            dve.after(a)
            return dve.did(V.tensor_tensor(dst[:, t, :], dst[:, t, :], gains[:, 1, :], ALU.add))

        def rms_scale(x, t, scratch, *ready):
            ss, rstd = stats[:, 40 + 2 * t:41 + 2 * t], stats[:, 41 + 2 * t:42 + 2 * t]
            act.after(*ready)
            a = act.did(SC.activation(scratch, x[:, t, :], ACT.Square, accum_out=ss))
            dve.after(a)
            a = dve.did(V.tensor_scalar(rstd, ss, 1.0 / D, RMS_EPS, ALU.mult, ALU.add))
            return rstd, inverse_root(rstd, a)

        def residual_norm(first_bank, done, gains_ready):
            out = []
            for t in range(TT):
                dve.after(done)
                for half in range(2):
                    b = first_bank + 2 * t + half
                    cols = h[:, t, half * 512:(half + 1) * 512]
                    bank_read[b] = dve.did(V.scalar_tensor_tensor(
                        out=cols, in0=cols, scalar=ALPHA, in1=banks[b][:, :], op0=ALU.mult, op1=ALU.add))
                out.append(layer_norm(h, t, h, gains_ready, bank_read[b]))
            return out

        def load_gains(name, g, b, *free):
            act.after(*free)
            return load_small(name, (gains[:, 0, :], g.partition_broadcast(P)),
                              (gains[:, 1, :], b.partition_broadcast(P)))

        x_in = c.sem("loaded_x0"), c.sem("loaded_x1")
        h_loaded = [c.raised(x_in[t], nc.sync.dma_start(h[:, t, :], A["x"][0, t * P:(t + 1) * P, :]), 16)
                    for t in range(TT)]
        gains_loaded = load_small("start", (gains[:, 0, :], A["ln_in_g"].partition_broadcast(P)),
                                  (gains[:, 1, :], A["ln_in_b"].partition_broadcast(P)))
        second_area = Area("second_const")
        second_const = second_area.take(A["const_second"].shape[1])
        hg_levels = second_area.take(A["const_levels"].shape[1], len(HG_LEVELS) + 1, dt=I8)
        cur = second_area.take(28)
        lbs = second_area.take(48)

        first_area = Area("first_const")
        first_const = first_area.take(A["const_first"].shape[1])
        levels_area = Area("levels")
        levels_in = levels_area.take(A["const_levels"].shape[1])
        const_loaded = load_small("consts", (shared[:, :], A["const_shared"]), (first_const, A["const_first"]),
                                  (vecs[:, :], A["vecs"]), (second_const, A["const_second"]),
                                  (levels_in, A["const_levels"]))
        pool.after(const_loaded)
        pool.did(G.tensor_copy(hg_levels.rearrange("p l s -> p (l s)"), levels_in))
        levels_area.close()

        def fc(name):
            at, n = const_at["first"][name]
            return first_const[:, at:at + n]

        neg_ge, neg_ones, before, before_bias = fc("neg_ge"), fc("neg_ones"), fc("before"), fc("before_bias")
        upto, iota = fc("upto"), fc("iota")
        inv_count = fc("inv_count").rearrange("p (g s) -> p g s", g=4)

        def layer_vec(name, layer, n):
            at = const_at["vecs"][name] + layer * n
            return vecs[:, at:at + n]


        def first_mixer(layer, h_ready):
            area = Area(f"mixer{layer}_")
            uT, qT, kT = (area.take(4 * S, 4) for _ in range(3))
            v = area.take(TT * 512, TT)
            mix = area.take_split(KT * S, KT)
            sums, lagged = area.take(4 * S, 4), area.take(4 * S, 4)
            pool_w = area.take(4 * P, 4)
            soft, expo, mag = (area.take(2 * 384, 2) for _ in range(3))
            soft2, expo2, mag2 = (area.take(2 * 384, 2) for _ in range(3))
            fence()
            pool_w_loaded = load_small(
                f"pool_w{layer}", (pool_w, A["pool_w"][layer].rearrange("g c d -> c g d")))
            gains_ready = load_gains(
                f"ln1_{layer}", A["ln1_g"][layer:layer + 1, :], A["ln1_b"][layer:layer + 1, :], h_ready)
            x = (xH, xL)
            x_ready = transpose_rows(h, h_ready)

            ready = {}

            def next_chunk(i, name, j, steps):
                b = i % 3
                done = product(x, x_ready, b, rows=(name == "v"), steps=steps)
                src = tile2(banks[b][:, :])
                if name == "v":
                    act.after(done)
                    bank_read[b] = act.did(SC.copy(v[:, :, j * 256:(j + 1) * 256], src))
                else:
                    act.after(done)
                    dst = {"u": uT, "q": qT, "k": kT}[name][:, 2 * j:2 * j + 2, :]
                    bank_read[b] = act.did(SC.activation(dst, src, ACT.Copy, scale=0.125 if name == "q" else 1.0))
                ready[name, j] = bank_read[b]

            def stick_breaking(first_pair):
                sp, ex, mg = (soft, expo, mag) if first_pair == 0 else (soft2, expo2, mag2)
                zb = (4, 5) if first_pair == 0 else (6, 7)
                for pair in (first_pair, first_pair + 2):
                    j = pair // 2
                    while ("k", j) not in ready:
                        yield
                    pe.after(ready["q", j], ready["k", j], *[bank_read[b] for b in zb])
                    for e in range(2):
                        lo = SB_DIM * e
                        q_, k_ = qT[lo:lo + SB_DIM, pair, :], kT[lo:lo + SB_DIM, pair, :]
                        z = banks[zb[e]]
                        T.matmul(z[:, 0:256], k_[:, 0:P], q_, start=True, stop=True)
                        mm = T.matmul(z[:, 256:384], k_[:, P:S], q_[:, P:S], start=False, stop=True,
                                      skip_group_check=True)
                    scored = pe.did(mm)
                    yield
                    act.after(scored)
                    for e in range(2):
                        a = act.did(SC.activation(mg[:, e, :], banks[zb[e]][:, 0:384], ACT.Abs))
                    act.after(a)
                    a = act.did(SC.activation(ex, mg, ACT.Exp, scale=-1.0))
                    act.after(a)
                    a = act.did(SC.activation(mg, ex, ACT.Ln, bias=1.0))
                    yield
                    dve.after(a)
                    for e in range(2):
                        a = dve.did(V.scalar_tensor_tensor(out=sp[:, e, :], in0=banks[zb[e]][:, 0:384], scalar=0.0,
                                                           in1=mg[:, e, :], op0=ALU.max, op1=ALU.add))
                    dve.after(a)
                    two = before.unsqueeze(1).to_broadcast((P, 2, P))
                    dve.did(V.tensor_tensor(sp[:, :, 0:P], sp[:, :, 0:P], two, ALU.mult))
                    masked = dve.did(V.tensor_tensor(sp[:, :, 256:384], sp[:, :, 256:384], two, ALU.mult))
                    yield
                    pe.after(masked)
                    for e in range(2):
                        z = banks[zb[e]]
                        T.matmul(z[:, 0:256], neg_ge, sp[:, e, 0:256], start=False, stop=True, skip_group_check=True)
                        T.matmul(z[:, P:256], neg_ones, sp[:, e, 256:384], start=False, stop=True,
                                 skip_group_check=True)
                        mm = T.matmul(z[:, 256:384], neg_ge, sp[:, e, 256:384], start=False, stop=True,
                                      skip_group_check=True)
                    summed = pe.did(mm)
                    yield
                    dve.after(summed)
                    for e in range(2):
                        z = banks[zb[e]]
                        dve.did(V.scalar_tensor_tensor(out=ex[:, e, 0:P], in0=z[:, 0:P], scalar=0.0, in1=before_bias,
                                                       op0=ALU.min, op1=ALU.add))
                        dve.did(V.scalar_tensor_tensor(out=ex[:, e, 256:384], in0=z[:, 256:384], scalar=0.0,
                                                       in1=before_bias, op0=ALU.min, op1=ALU.add))
                        a = dve.did(V.tensor_scalar(ex[:, e, P:256], z[:, P:256], 0.0, None, ALU.min))
                        bank_read[zb[e]] = a
                    yield
                    act.after(a)
                    att = act.did(SC.activation(mg, ex, ACT.Exp))
                    yield
                    while ("v", j) not in ready:
                        yield
                    pe.after(att, ready["v", j], bank_read[zb[0]])
                    for e in range(2):
                        lo, head = SB_DIM * e, 2 * pair + e
                        y = banks[zb[0]][lo:lo + SB_DIM, 0:256]
                        T.matmul(y, v[:, 0, head * SB_DIM:(head + 1) * SB_DIM], mg[:, e, 0:256], start=True, stop=True)
                        mm = T.matmul(y[:, P:S], v[:, 1, head * SB_DIM:(head + 1) * SB_DIM], mg[:, e, 256:384],
                                      start=False, stop=True, skip_group_check=True)
                    done = pe.did(mm)
                    yield
                    ready["y", pair] = bank_read[zb[0]] = split(
                        banks[zb[0]][:, 0:256], [m[:, 4 + pair, :] for m in mix], done)
                    yield

            def pool_mixer():
                src, a = uT, [ready["u", 0], ready["u", 1]]
                for g, w_ in enumerate(POOL_WINDOWS):
                    lag = w_ // 2
                    dst = sums if g % 2 == 0 else lagged
                    pool.after(a)
                    a1 = pool.did(G.tensor_copy(dst[:, g:4, 0:lag], src[:, g:4, 0:lag]))
                    a2 = pool.did(G.tensor_tensor(dst[:, g:4, lag:S], src[:, g:4, lag:S], src[:, g:4, 0:S - lag],
                                                  ALU.add))
                    a = [a1, a2]
                    src = dst
                pooled = []
                for g in range(4):
                    s_ = (sums if g % 2 == 0 else lagged)[:, g, :]
                    pool.after(a)
                    a1 = pool.did(G.tensor_tensor(s_, s_, inv_count[:, g, :], ALU.mult))
                    pool.after(a1)
                    pooled.append(pool.did(G.tensor_tensor(s_, s_, uT[:, g, :], ALU.subtract)))
                for _ in range(3):
                    yield
                for g in range(4):
                    s_ = (sums if g % 2 == 0 else lagged)[:, g, :]
                    pe.after(pooled[g], pool_w_loaded, bank_read[3])
                    mapped = pe.did(T.matmul(banks[3][:, 0:256], pool_w[:, g, :], s_, start=True, stop=True))
                    yield
                    act.after(mapped)
                    bank_read[3] = act.did(SC.activation(s_, banks[3][:, 0:256], ACT.Copy,
                                                         scale=layer_vec("pool_scale", layer, 4)[:, g:g + 1]))
                    ready["pool", g] = split(s_, [m[:, g, :] for m in mix], bank_read[3])
                    yield

            next_chunk(0, "u", 0, 0)
            next_chunk(1, "u", 1, 0)
            sides.append(pool_mixer())
            next_chunk(2, "q", 0, 0)
            next_chunk(3, "k", 0, 0)
            sides.extend([stick_breaking(0), stick_breaking(1)])
            for i, (name, j) in enumerate((("v", 0), ("q", 1), ("k", 1), ("v", 1))):
                next_chunk(4 + i, name, j, MIXER_STEPS)

            def mix_ready(i):
                key = ("pool", i) if i < 4 else ("y", i - 4)
                while key not in ready:
                    side_steps(1)
                return ready[key]

            mix_ready(3)
            done = accumulate(KT, mix, mix_ready, 0, steps=MIXER_STEPS)
            finish_sides()
            area.close()
            return residual_norm(0, done, gains_ready)

        def dense_ffn(h_ready):
            area = Area("ffn_")
            hid = area.take_split(FT * S, FT)
            gate = [area.take(512, 2) for _ in range(2)]
            fence()
            gains_ready = load_gains("ln2_0", A["ln2_g"][0:1, :], A["ln2_b"][0:1, :], h_ready)
            x, x_ready = (xH, xL), transpose_rows(h, h_ready)
            hid_ready, gate_free = [], [None, None]
            for j in range(FT // 2):
                bg, bu = (0, 1) if j % 2 == 0 else (2, 3)
                done = product(x, x_ready, bg, rows=False)
                act.after(done, gate_free[j % 2])
                bank_read[bg] = act.did(SC.activation(gate[j % 2], tile2(banks[bg][:, :]), ACT.Silu))
                done = product(x, x_ready, bu, rows=False)
                dve.after(done, bank_read[bg])
                bank_read[bu] = dve.did(V.tensor_tensor(gate[j % 2], tile2(banks[bu][:, :]), gate[j % 2], ALU.mult))
                gate_free[j % 2] = split(gate[j % 2], [v[:, 2 * j:2 * j + 2, :] for v in hid], bank_read[bu])
                hid_ready.append(gate_free[j % 2])
            done = accumulate(FT, hid, hid_ready, 4)
            area.close()
            return residual_norm(4, done, gains_ready)

        def moe_ffn(h_ready):
            area = Area("moe_")
            router = area.take(KT * E, KT)
            router_split = area.take_split(KT * E, KT)
            r = {n: area.take(TT * E, TT) for n in ("logits", "first", "rest", "second", "t0", "t1")}
            r.update({n: area.take(TT * (E + 1), TT) for n in ("sel", "gate")})
            mx = area.take(8)
            base = area.take(2 * TT * (E + 1), 2, TT)
            table, table_i = tables[:, 0:32], tables[:, 32:64].bitcast(I32)
            pick, pickg = area.take(TT * P, TT), area.take(TT * P, TT)
            pickT = [area.take(TT * P, TT) for _ in range(2)]
            xs = [area.take_split(KT * SLOTS, KT) for _ in range(2)]
            y = [area.take(D) for _ in range(2)]
            hidT = area.take_split(FT * SLOTS, FT)
            gate_s, hid_s = [area.take(256) for _ in range(2)], [area.take(256) for _ in range(2)]
            total = area.take(TT * D, TT)
            fence()
            gains_ready = load_gains("ln2_1", A["ln2_g"][1:2, :], A["ln2_b"][1:2, :], h_ready)
            router_ready = load_small("router", (router, A["moe_router"][0].rearrange("(k p) e -> p k e", p=P)))
            x_ready = transpose_rows(h, h_ready)
            router_ready = split(router, router_split, router_ready)
            for v_ in (total, y[1], pickT[1], r["sel"], r["gate"], base):
                zeroed = pool.did(G.memset(v_, 0.0))
            pe.after(x_ready, router_ready, bank_read[4])
            for t in range(TT):
                for k in range(KT):
                    mm = three(banks[4][:, t * E:(t + 1) * E], [v[:, k, t * P:(t + 1) * P] for v in (xH, xL)],
                               [v[:, k, :] for v in router_split], start=(k == 0), stop=(k == KT - 1))
            a = pe.did(mm)

            def vec(inst):
                t_ = dve.did(inst)
                dve.after(t_)
                return t_

            def bc(col):
                return col.unsqueeze(2).to_broadcast((P, TT, E))

            dve.after(a)
            vec(V.tensor_copy(r["logits"], banks[4][:, 0:TT * E].rearrange("p (t e) -> p t e", t=TT)))

            def choose(source, sel, col):
                vec(V.tensor_reduce(mx[:, col:col + 2], source, AX, ALU.max))
                vec(V.tensor_tensor(r["t0"], source, bc(mx[:, col:col + 2]), ALU.is_equal))
                for t in range(TT):
                    vec(V.tensor_tensor_scan(r["t1"][:, t, :], ones[:, 0:E], r["t0"][:, t, :], 0.0,
                                             ALU.mult, ALU.add))
                vec(V.tensor_scalar(r["t1"], r["t1"], 1.0, None, ALU.is_equal))
                vec(V.tensor_tensor(sel, r["t0"], r["t1"], ALU.mult))

            choose(r["logits"], r["first"], 0)
            vec(V.scalar_tensor_tensor(out=r["rest"], in0=r["first"], scalar=-3.0e38, in1=r["logits"],
                                       op0=ALU.mult, op1=ALU.add))
            choose(r["rest"], r["second"], 2)
            a = vec(V.tensor_tensor(mx[:, 4:6], mx[:, 2:4], mx[:, 0:2], ALU.subtract))
            act.after(a)
            a = act.did(SC.activation(mx[:, 4:6], mx[:, 4:6], ACT.Exp))
            dve.after(a)
            vec(V.tensor_scalar(mx[:, 6:8], mx[:, 4:6], 1.0, None, ALU.add))
            vec(V.reciprocal(mx[:, 6:8], mx[:, 6:8]))
            vec(V.tensor_tensor(mx[:, 4:6], mx[:, 4:6], mx[:, 6:8], ALU.mult))
            vec(V.tensor_tensor(r["t0"], r["first"], bc(mx[:, 6:8]), ALU.mult))
            vec(V.tensor_tensor(r["t1"], r["second"], bc(mx[:, 4:6]), ALU.mult))
            dve.after(zeroed)
            vec(V.tensor_tensor(r["gate"][:, :, 0:E], r["t0"], r["t1"], ALU.add))
            a = vec(V.tensor_tensor(r["sel"][:, :, 0:E], r["first"], r["second"], ALU.add))
            pe.after(a, const_loaded)
            T.matmul(banks[5][:, 0:E], upto, r["sel"][:, 0, 0:E], start=True, stop=True)
            T.matmul(banks[5][:, E:2 * E], upto, r["sel"][:, 1, 0:E], start=True, stop=False)
            T.matmul(banks[5][:, E:2 * E], ones, r["sel"][:, 0, 0:E], start=False, stop=True)
            T.matmul(banks[5][:, 2 * E:3 * E], ones, r["sel"][:, 0, 0:E], start=True, stop=False)
            a = pe.did(T.matmul(banks[5][:, 2 * E:3 * E], ones, r["sel"][:, 1, 0:E], start=False, stop=True))
            dve.after(a)
            ranks = banks[5][:, 0:2 * E].rearrange("p (t e) -> p t e", t=TT)
            vec(V.tensor_scalar(base[:, 0, :, 0:E], ranks, -1.0, None, ALU.add))
            vec(V.tensor_scalar(base[:, 1, :, 0:E], ranks, -1.0 - SLOTS, None, ALU.add))
            over, order, hit = table[:, 0:8], table[:, 8:16], table[:, 24:32]
            vec(V.tensor_scalar(over, banks[5][:, 2 * E:3 * E], float(SLOTS), None, ALU.is_gt))
            vec(V.tensor_tensor_scan(order, ones[:, 0:E], over, 0.0, ALU.mult, ALU.add))
            for j in range(3):
                vec(V.tensor_scalar(hit, order, float(j + 1), None, ALU.is_equal))
                vec(V.tensor_tensor(hit, hit, over, ALU.mult))
                vec(V.tensor_reduce(table[:, 16 + 4 + j:17 + 4 + j], hit, AX, ALU.max))
                vec(V.tensor_tensor(hit, hit, iota[:, 0:E], ALU.mult))
                vec(V.tensor_reduce(table[:, 16 + j:17 + j], hit, AX, ALU.add))
            vec(V.tensor_copy(table[:, 19:20], table[:, 20:21]))
            vec(V.tensor_scalar(table[:, 20:23], table[:, 20:23], -float(E), float(E), ALU.mult, ALU.add))
            vec(V.tensor_tensor(table[:, 20:23], table[:, 20:23], table[:, 16:19], ALU.add))
            table_ready = vec(V.tensor_copy(table_i[:, 16:23], table[:, 16:23]))
            fence()

            wg, wu, wd = A["moe_wg"][0], A["moe_wu"][0], A["moe_wd"][0]

            def gather(e, block, buf):
                for t in range(TT):
                    picked = dve.did(V.tensor_scalar(pick[:, t, :], iota, base[:, block, t, bass.ds(e, 1)],
                                                     r["sel"][:, t, bass.ds(e, 1)], ALU.is_equal, ALU.mult))
                dve.after(picked)
                for t in range(TT):
                    pickg_ready = dve.did(V.tensor_scalar(pickg[:, t, :], pick[:, t, :],
                                                          r["gate"][:, t, bass.ds(e, 1)], None, ALU.mult))
                yield
                for g in range(2):
                    pe.after(picked, bank_read[6 + g])
                    for k in range(4):
                        for t in range(TT):
                            kk = 4 * g + k
                            mm = T.matmul(banks[6 + g][:, k * P:(k + 1) * P], h[:, t, kk * P:(kk + 1) * P],
                                          pick[:, t, :], start=(t == 0), stop=(t == TT - 1))
                    a = pe.did(mm)
                    yield
                    bank_read[6 + g] = split(banks[6 + g][:, :].rearrange("p (k s) -> p k s", k=4),
                                             [v[:, 4 * g:4 * g + 4, :] for v in xs[buf]], a)
                    yield
                xs_ready[buf] = bank_read[7]
                pe.after(pickg_ready, bank_read[6])
                for t in range(TT):
                    mm = T.transpose(banks[6][:, t * P:(t + 1) * P], pickg[:, t, :], ident)
                a = pe.did(mm)
                yield
                act.after(a)
                pickT_ready[buf] = bank_read[6] = act.did(SC.copy(pickT[buf], tile2(banks[6][:, 0:2 * P])))
                yield

            def scatter(buf):
                for t in range(TT):
                    for half in range(2):
                        b = 6 + half
                        pe.after(bank_read[b], y_ready[buf], pickT_ready[buf])
                        a = pe.did(T.matmul(banks[b][:, :], pickT[buf][:, t, :],
                                            y[buf][:, half * 512:(half + 1) * 512], start=True, stop=True))
                        yield
                        cols = total[:, t, half * 512:(half + 1) * 512]
                        dve.after(a)
                        bank_read[b] = dve.did(V.tensor_tensor(cols, cols, banks[b][:, :], ALU.add))
                yield

            xs_ready, pickT_ready, y_ready = [None, None], [None, None], [None, None]

            def want_expert(e):
                one = (bass.ds(e, 1), slice(None), slice(None))
                g_, u_ = (w[one].rearrange("e (k p) n -> p (e k) n", p=P) for w in (wg, wu))
                for j in range(FT // 2):
                    for ks in (slice(0, 4), slice(4, 8)):
                        cols = slice(j * 256, (j + 1) * 256)
                        weights.want(4, 512, (0, 256, g_[:, ks, cols]), (256, 512, u_[:, ks, cols]))
                want_rows(wd[one].rearrange("e r n -> (e r) n"), FT)

            def expert(buf):
                hid_free, waiting, hidT_ready = [None, None], None, []

                def turn(j, hid_done):
                    b = 2 + j % 2
                    pe.after(hid_done, bank_read[b])
                    for i in range(2):
                        mm = T.transpose(banks[b][:, i * P:(i + 1) * P], hid_s[j % 2][:, i * P:(i + 1) * P], ident)
                    a = pe.did(mm)
                    hid_free[j % 2] = a
                    bank_read[b] = split(tile2(banks[b][:, 0:2 * P]), [v[:, 2 * j:2 * j + 2, :] for v in hidT], a)
                    hidT_ready.append(bank_read[b])

                for j in range(FT // 2):
                    b = j % 2
                    pe.after(xs_ready[buf], bank_read[b])
                    for part in range(4):
                        piece = weights.fetch()
                        for kk in range(2):
                            k = 2 * part + kk
                            mm = three(banks[b][:, :], [v[:, k, :] for v in xs[buf]],
                                       [v[:, kk, :] for v in (piece.high, piece.low)],
                                       start=(k == 0), stop=(k == KT - 1))
                        done = weights.release(piece, mm)
                        side_steps(1)
                    if waiting:
                        turn(*waiting)
                    act.after(done, hid_free[b])
                    a = act.did(SC.activation(gate_s[b], banks[b][:, 0:256], ACT.Silu))
                    dve.after(a, done, hid_free[b])
                    bank_read[b] = dve.did(V.tensor_tensor(hid_s[b], banks[b][:, 256:512], gate_s[b], ALU.mult))
                    waiting = (j, bank_read[b])
                turn(*waiting)
                for i in range(FT):
                    piece = weights.fetch()
                    pe.after(hidT_ready[i // 2], bank_read[4], bank_read[5])
                    for half in range(2):
                        mm = three(banks[4 + half][:, :], [v[:, i, :] for v in hidT],
                                   [v[:, 0, half * 512:(half + 1) * 512] for v in (piece.high, piece.low)],
                                   start=(i == 0), stop=(i == FT - 1))
                    done = weights.release(piece, mm)
                act.after(done)
                bank_read[4] = act.did(SC.copy(y[buf][:, 0:512], banks[4][:, :]))
                dve.after(done)
                bank_read[5] = dve.did(V.tensor_copy(y[buf][:, 512:D], banks[5][:, :]))
                y_ready[buf] = [bank_read[4], bank_read[5]]

            def after_the_last(*work):
                for g in work:
                    yield from g

            sides.append(gather(0, 0, 0))
            finish_sides()
            fence()
            with c.repeat("experts", E // 2) as i:
                weights.align()
                want_expert(i * 2)
                want_expert(i * 2 + 1)
                for buf in range(2):
                    sides.append(after_the_last(scatter(1 - buf), gather(i * 2 + 1 + buf, 0, 1 - buf)))
                    expert(buf)
                fence()
            weights.align()
            sides.append(scatter(1))
            finish_sides()

            meet = c.sem("meet")
            everyone = (*computing, sync)
            toks = [c.now(e_.sem) for e_ in computing] + [
                c.now(s) for s in weights.used + weights.landed + weights.first_half + weights.split]
            for e_ in everyone:
                e_.after(*toks)
                e_.q.sem_inc(meet.handle, 1)
            meet.count += len(everyone)
            for e_ in everyone:
                e_.after(c.now(meet))
            for i in range(8):
                bank_read[i] = None
            any_over = nc.values_load(table_i[0:1, 19:20], min_val=0, max_val=1)
            before_passes = {s.name: s.count for s in c.sems}
            with nc.If(any_over):
                with c.repeat("overflow", 3) as j:
                    weights.align()
                    who = nc.values_load(table_i[0:1, bass.ds(j + 16, 1)], min_val=0, max_val=E - 1)
                    whose = nc.values_load(table_i[0:1, bass.ds(j + 20, 1)], min_val=0, max_val=E)
                    want_expert(who)
                    sides.append(gather(whose, 1, 0))
                    finish_sides()
                    expert(0)
                    sides.append(scatter(0))
                    finish_sides()
                    fence()
            with nc.Else():
                for s, owner in [(e_.sem, e_) for e_ in computing] + [(s, pe) for s in weights.used] + [
                        (s, sync) for s in weights.landed] + [
                        (s, dve) for s in weights.first_half + weights.split]:
                    if s.count > before_passes[s.name]:
                        owner.q.sem_inc(s.handle, s.count - before_passes[s.name])
            for e_ in everyone:
                e_.known = {}
            weights.align()
            out = []
            fence()
            area.close()
            for t in range(TT):
                a = dve.did(V.scalar_tensor_tensor(out=h[:, t, :], in0=h[:, t, :], scalar=ALPHA,
                                                   in1=total[:, t, :], op0=ALU.mult, op1=ALU.add))
                out.append(layer_norm(h, t, h, gains_ready, a))
            return out

        def dump(name, ap, toks):
            if name in A.get("dumps", {}):
                sync.after(*toks)
                d_ = c.raised(dumped, nc.sync.dma_start(A["dumps"][name].rearrange("(t p) d -> p t d", p=P), ap), 16)
                for e_ in computing:
                    e_.after(d_)

        dumped = c.sem("dumped") if A.get("dumps") else None
        def lower_bounds():
            lb_at = const_at["vecs"]["hg_lb"]
            lb0, lb1 = vecs[:, lb_at:lb_at + 4], vecs[:, lb_at + 4:lb_at + 8]
            x_, n_, l_ = lbs[:, 16:20], lbs[:, 20:24], lbs[:, 24:28]
            a = dve.did(V.tensor_tensor(x_, lb1, lb0, ALU.subtract))
            dve.did(V.memset(lbs[:, 0:4], -1.0e30))
            dve.did(V.memset(lbs[:, 8:12], 0.0))
            dve.after(a)
            act.after(a)
            a = act.did(SC.activation(n_, x_, ACT.Abs))
            act.after(a)
            a = act.did(SC.activation(l_, n_, ACT.Exp, scale=-1.0))
            act.after(a)
            a = act.did(SC.activation(l_, l_, ACT.Ln, bias=1.0))
            dve.after(a)
            a = dve.did(V.scalar_tensor_tensor(out=lbs[:, 4:8], in0=x_, scalar=0.0, in1=l_, op0=ALU.min, op1=ALU.subtract))
            dve.after(a)
            dve.did(V.tensor_tensor(lbs[:, 12:16], lbs[:, 4:8], x_, ALU.subtract))

        def want_mixer(layer):
            w = A["w_in"][layer].rearrange("(k p) n -> p k n", p=P)
            for col in (0, 1, 2, 4, 6, 3, 5, 7):
                want_columns(w, col)
            want_rows(A["w_out"][layer], KT)

        want_mixer(0)
        wg, wu = (A[n][0].rearrange("(k p) n -> p k n", p=P) for n in ("ffn_wg", "ffn_wu"))
        for j in range(FT // 2):
            want_columns(wg, j)
            want_columns(wu, j)
        want_rows(A["ffn_wd"][0], FT)
        want_mixer(1)

        h_ready = [layer_norm(h, t, h, gains_loaded, h_loaded[t]) for t in range(TT)]
        for e_ in computing:
            e_.after(const_loaded)
        lower_bounds()
        dump("ln_in", h, h_ready)
        h_ready = first_mixer(0, h_ready)
        dump("mix0", h, h_ready)
        h_ready = dense_ffn(h_ready)
        dump("ffn0", h, h_ready)
        h_ready = first_mixer(1, h_ready)
        dump("mix1", h, h_ready)
        h_ready = moe_ffn(h_ready)
        dump("moe", h, h_ready)

        first_area.close()
        def sc_(name):
            at, n = const_at["second"][name]
            return second_const[:, at:at + n]

        own_mask = sc_("own_mask").rearrange("p (g s) -> p g s", g=3)
        prev_mask = sc_("prev_mask").rearrange("p (g s) -> p g s", g=3)
        rope_cos, rope_sin, rope_swap = sc_("rope_cos"), sc_("rope_sin"), sc_("rope_swap")
        W4 = HG_HEADS * S
        fence()

        def second_layer(layer):
            area = Area("layer_")
            qkT = area.take(24 * S, 24)
            v_att = area.take(TT * 1536, TT)
            o_hg = area.take_split(W4, 4)
            o_att = area.take_split(W4, 4)
            rope_tmp = area.take(512)
            hg_area = Area("hg_")
            q_hg, z_f, v_hg, g_hg = (hg_area.take(W4, 4) for _ in range(4))
            k_hg = z_f
            v_hg = v_hg.rearrange("p a s -> p (a s)").rearrange("p (t n) -> p t n", t=TT)
            decay = hg_area.take(W4)
            hg_att = hg_area.take(HG_HEADS * 3 * P, HG_HEADS, 3)
            work = hg_area.take(3 * W4)
            w0, w1, w2 = (work[:, i * W4:(i + 1) * W4] for i in range(3))
            norms_loaded = None
            for i, name in enumerate(("norm1_g_2", "norm2_g_2")):
                norms_loaded = c.raised(norm_loads, nc.scalar.dma_start(
                    gains[:, i, :], A[name][bass.ds(layer, 1), :].partition_broadcast(P)), 16)
            w = A["w_in_2"][bass.ds(layer, 1), :, :].rearrange("l (k p) n -> p (l k) n", p=P)
            for col in [2, 3, 0, 1, 4, 5, 6, 7] + list(range(8, 34)):
                want_columns(w, col)
            for name in ("w_branch_a_2", "w_branch_b_2"):
                wv = A[name][bass.ds(layer, 1), :, :].rearrange("l (k p) n -> p (l k) n", p=P)
                for i in range(2):
                    weights.want(4, 512, (0, 512, wv[:, :, i * 512:(i + 1) * 512]))
            want_rows(A["w_out_2"][bass.ds(layer, 1), :, :].rearrange("l r n -> (l r) n"), KT)
            w = A["w_up_2"][bass.ds(layer, 1), :, :].rearrange("l (k p) n -> p (l k) n", p=P)
            for j in range(NT2 // 2):
                want_columns(w, j)
            want_rows(A["w_down_2"][bass.ds(layer, 1), :, :].rearrange("l r n -> (l r) n"), NT2)
            vat = const_at["vecs"]["second"]
            dve.did(V.tensor_copy(cur[:, 0:4], vecs[:, bass.ds(layer * 4 + vat, 4)]))
            dve.did(V.tensor_copy(cur[:, 4:8], lbs[:, bass.ds(layer * 4, 4)]))
            cur_ready = dve.did(V.tensor_copy(cur[:, 8:12], lbs[:, bass.ds(layer * 4 + 8, 4)]))
            dve.after(cur_ready)

            def normed(which, xn):
                ready = []
                for t in range(TT):
                    rstd, a = rms_scale(h, t, xn[:, t, :])
                    dve.after(a, norms_loaded)
                    ready.append(dve.did(V.scalar_tensor_tensor(
                        out=xn[:, t, :], in0=h[:, t, :], scalar=rstd, in1=gains[:, which, :],
                        op0=ALU.mult, op1=ALU.mult)))
                return transpose_rows(xn, ready)

            x = (xH, xL)
            x_ready = normed(0, work[:, 0:TT * D].rearrange("p (t d) -> p t d", t=TT))

            turn = [0]
            ready = {}

            def columns(col, rows, finish):
                b = turn[0] % 4
                turn[0] += 1
                done = product(x, x_ready, b, rows, steps=LAYER_STEPS)
                e_, inst = finish(tile2(banks[b][:, :]), done)
                bank_read[b] = e_.did(inst)
                return bank_read[b]

            def through(fn, dst):
                def finish(src, done):
                    act.after(done)
                    return act, SC.activation(dst, src, fn)
                return finish

            def copied(dst):
                def finish(src, done):
                    dve.after(done)
                    return dve, V.tensor_copy(dst, src)
                return finish

            def columns3(col, rows, finish):
                b = turn[0] % 3
                turn[0] += 1
                done = product(x, x_ready, b, rows, steps=LAYER_STEPS)
                e_, inst = finish(tile2(banks[b][:, :]), done)
                bank_read[b] = e_.did(inst)
                return bank_read[b]

            for i in range(2):
                ready["zf", i] = columns(2 + i, False, copied(z_f[:, 2 * i:2 * i + 2, :]))
            def flat(ap):
                return ap.rearrange("p a s -> p (a s)")

            def per_head(cols):
                return cols.unsqueeze(2).to_broadcast((P, HG_HEADS, S))

            def as4(ap):
                return ap.rearrange("p (a s) -> p a s", a=HG_HEADS)

            def recurrence():
                zf = flat(z_f)
                act.after(ready["zf", 0], ready["zf", 1])
                a = act.did(SC.activation(w0, zf, ACT.Abs))
                act.after(a)
                a = act.did(SC.activation(w0, w0, ACT.Exp, scale=-1.0))
                act.after(a)
                a = act.did(SC.activation(w0, w0, ACT.Ln, bias=1.0))
                yield
                dve.after(a)
                a = dve.did(V.scalar_tensor_tensor(out=w1, in0=zf, scalar=0.0, in1=w0, op0=ALU.min, op1=ALU.subtract))
                dve.after(a)
                a = dve.did(V.tensor_tensor(as4(w1), as4(w1), per_head(cur[:, 8:12]), ALU.add))
                dve.after(a)
                a = dve.did(V.tensor_tensor(w2, w1, zf, ALU.subtract))
                yield
                act.after(a)
                k_ready = act.did(SC.activation(flat(k_hg), w2, ACT.Exp))
                yield
                a = dve.did(V.tensor_tensor(as4(w0), as4(w1), per_head(cur[:, 4:8]), ALU.subtract))
                b_ = dve.did(V.tensor_tensor(as4(w1), as4(w1), per_head(cur[:, 4:8]), ALU.max))
                yield
                act.after(a)
                a = act.did(SC.activation(w0, w0, ACT.Abs))
                act.after(a)
                a = act.did(SC.activation(w0, w0, ACT.Exp, scale=-1.0))
                act.after(a)
                a = act.did(SC.activation(w0, w0, ACT.Ln, bias=1.0))
                yield
                dve.after(a, b_)
                a = dve.did(V.tensor_tensor(w1, w1, w0, ALU.add))
                dve.after(a)
                for n in range(W4 // P):
                    cols = slice(n * P, (n + 1) * P)
                    a = dve.did(V.tensor_tensor_scan(decay[:, cols], ones, w1[:, cols], 0.0, ALU.mult, ALU.add))
                dve.after(a)
                yield
                dec4 = as4(decay)
                att = hg_att
                cleared = pool.did(G.memset(att[:, :, 0:2, :], 0.0))
                qf, kf = flat(q_hg), flat(k_hg)
                last = dec4[:, :, P - 1:P].to_broadcast((P, HG_HEADS, P))
                a = dve.did(V.tensor_tensor(as4(w0)[:, :, 0:P], last, dec4[:, :, 0:P], ALU.subtract))
                yield
                act.after(a)
                a1 = act.did(SC.activation(as4(w0)[:, :, 0:P], as4(w0)[:, :, 0:P], ACT.Exp))
                a2 = act.did(SC.activation(as4(w0)[:, :, P:S], dec4[:, :, P:S], ACT.Exp))
                yield
                while ("q", 1) not in ready:
                    yield
                dve.after(a1, a2, k_ready, ready["q", 0], ready["q", 1])
                dve.did(V.tensor_tensor(as4(w1)[:, :, 0:P], as4(w0)[:, :, 0:P], k_hg[:, :, 0:P], ALU.mult))
                a = dve.did(V.tensor_tensor(as4(w1)[:, :, P:S], as4(w0)[:, :, P:S], q_hg[:, :, P:S], ALU.mult))
                yield
                pe.after(a, bank_read[4])
                for hh in range(HG_HEADS):
                    mm = T.matmul(banks[4][:, hh * P:(hh + 1) * P], as4(w1)[:, hh, 0:P], as4(w1)[:, hh, P:S],
                                  start=True, stop=True)
                a = pe.did(mm)
                yield
                dve.after(a)
                bank_read[4] = dve.did(V.tensor_copy(att[:, :, 2, :], banks[4][:, :].rearrange("p (a s) -> p a s", a=4)))
                dve.after(bank_read[4])
                yield
                for li, m in enumerate(HG_LEVELS + (0,)):
                    if m:
                        blocks = decay.rearrange("p (n s) -> p n s", s=2 * m)
                        ref = blocks[:, :, m - 1:m].to_broadcast((P, W4 // (2 * m), 2 * m))
                        a = dve.did(V.tensor_tensor(w0.rearrange("p (n s) -> p n s", s=2 * m), blocks, ref,
                                                    ALU.subtract))
                        dve.after(a)
                        a = dve.did(V.scalar_tensor_tensor(out=w0, in0=w0, scalar=-1.0, in1=w0, op0=ALU.mult,
                                                           op1=ALU.min))
                        yield
                        act.after(a)
                        a = act.did(SC.activation(w0, w0, ACT.Exp))
                        yield
                        dve.after(a, k_ready)
                        qa = dve.did(V.tensor_tensor(w1, w0, qf, ALU.mult))
                        ka = dve.did(V.tensor_tensor(w2, w0, kf, ALU.mult))
                        qs, ks = as4(w1), as4(w2)
                        yield
                        pe.after(qa, ka)
                    else:
                        qs, ks = q_hg, k_hg
                    b = 4 + 2 * (li % 2)
                    pe.after(bank_read[b], bank_read[b + 1])
                    for hh in range(HG_HEADS):
                        for n in range(2):
                            mm = T.matmul(banks[b + n][:, hh * P:(hh + 1) * P], ks[:, hh, n * P:(n + 1) * P],
                                          qs[:, hh, n * P:(n + 1) * P], start=True, stop=True)
                    a = pe.did(mm)
                    yield
                    dve.after(a, cleared)
                    mask = hg_levels[:, li, :].unsqueeze(1).to_broadcast((P, HG_HEADS, P))
                    dve.settle()
                    for n in range(2):
                        bank_read[b + n] = dve.did(V.copy_predicated(
                            att[:, :, n, :], mask, banks[b + n][:, :].rearrange("p (a s) -> p a s", a=4)))
                    dve.after(bank_read[b + 1])
                while ("g", 1) not in ready:
                    yield
                pe.after(bank_read[b + 1], ready["v", 0], ready["v", 1], bank_read[4], bank_read[5])
                for hh in range(HG_HEADS):
                    o_ = banks[4 + hh // 2][:, (hh % 2) * S:(hh % 2) * S + S]
                    cols = slice(hh * P, (hh + 1) * P)
                    T.matmul(o_[:, 0:P], v_hg[:, 0, cols], att[:, hh, 0, :], start=True, stop=True)
                    T.matmul(o_[:, P:S], v_hg[:, 0, cols], att[:, hh, 2, :], start=True, stop=False)
                    mm = T.matmul(o_[:, P:S], v_hg[:, 1, cols], att[:, hh, 1, :], start=False, stop=True)
                a = pe.did(mm)
                yield
                for n in range(2):
                    yield
                    act.after(a)
                    sq = act.did(SC.activation(w0[:, n * 512:(n + 1) * 512], banks[4 + n][:, :], ACT.Square))
                    yield
                    pe.after(sq, bank_read[6 + n])
                    mm = pe.did(T.matmul(banks[6 + n][:, :], ones, w0[:, n * 512:(n + 1) * 512], start=True, stop=True))
                    yield
                    dve.after(mm)
                    cols = w1[:, n * 512:(n + 1) * 512]
                    a_ = bank_read[6 + n] = dve.did(V.tensor_scalar(cols, banks[6 + n][:, :], 1.0 / P, RMS_EPS,
                                                                    ALU.mult, ALU.add))
                    yield
                    a_ = inverse_root(cols, a_)
                    yield
                    dve.after(a_)
                    a_ = bank_read[4 + n] = dve.did(V.tensor_tensor(cols, cols, banks[4 + n][:, :], ALU.mult))
                    dve.after(a_)
                dve.after(ready["g", 0], ready["g", 1])
                a_ = dve.did(V.tensor_tensor(as4(w1), as4(w1), per_head(cur[:, 0:4]), ALU.mult))
                dve.after(a_)
                a_ = dve.did(V.tensor_tensor(as4(w1), as4(w1), g_hg, ALU.mult))
                ready["o_hg"] = split(as4(w1), o_hg, a_)
                yield

            sides.append(recurrence())
            for i in range(2):
                ready["q", i] = columns3(i, False, through(ACT.Silu, q_hg[:, 2 * i:2 * i + 2, :]))
            for i in range(2):
                ready["v", i] = columns3(4 + i, True, copied(v_hg[:, :, i * 256:(i + 1) * 256]))
            for i in range(2):
                ready["g", i] = columns3(6 + i, False, through(ACT.Sigmoid, g_hg[:, 2 * i:2 * i + 2, :]))

            def rope(j, copied_tok):
                b = 3
                pe.after(copied_tok, bank_read[b])
                part = qkT[0:ROPE_DIM, 2 * j:2 * j + 2, :]
                pe.settle()
                a = pe.did(T.matmul(banks[b][0:ROPE_DIM, :], rope_swap[0:ROPE_DIM, :], flat(part), start=True, stop=True))
                sin = rope_sin[0:ROPE_DIM, :].unsqueeze(1).to_broadcast((ROPE_DIM, 2, S))
                cos = rope_cos[0:ROPE_DIM, :].unsqueeze(1).to_broadcast((ROPE_DIM, 2, S))
                tmp = tile2(rope_tmp[0:ROPE_DIM, :])
                yield
                dve.after(a, ready.get("rope_tmp free"))
                a1 = bank_read[b] = dve.did(V.tensor_tensor(tmp, tile2(banks[b][0:ROPE_DIM, :]), sin, ALU.mult))
                a2 = dve.did(V.tensor_tensor(part, part, cos, ALU.mult))
                dve.after(a1, a2)
                ready["qk", j] = ready["rope_tmp free"] = dve.did(V.tensor_tensor(part, part, tmp, ALU.add))
                yield

            for j in range(12):
                tok = columns3(8 + j, False, through(ACT.Copy, qkT[:, 2 * j:2 * j + 2, :]))
                sides.append(rope(j, tok))
            for j in range(6):
                ready["va", j] = columns3(20 + j, True, through(ACT.Copy, v_att[:, :, j * 256:(j + 1) * 256]))
            finish_sides()
            qk_ready = [ready["qk", j] for j in range(12)]

            def attention():
                scale = float(P) ** -0.5
                dve.after(ready["o_hg"])
                act.after(ready["o_hg"])
                masked_s, probs_T = late.take(9 * P), late.take(9 * P)
                first, second = masked_s[:, 0:384], masked_s[:, 384:1152]
                sec4 = second.rearrange("p (g n s) -> p g n s", g=3, n=2)
                for hd in range(ATT_HEADS):
                    st = stats[:, 48:56]
                    pe.after(qk_ready, bank_read[4], bank_read[5], bank_read[6])
                    for g in range(ATT_GROUPS):
                        q_, k_ = qkT[:, g * 4 + hd, :], qkT[:, 12 + g * 4 + hd, :]
                        T.matmul(banks[4][:, g * P:(g + 1) * P], q_[:, 0:P], k_[:, 0:P], start=True, stop=True)
                        dst = banks[5 + g // 2][:, (g % 2) * S:(g % 2) * S + S]
                        mm = T.matmul(dst, q_[:, P:S], k_, start=True, stop=True)
                    a = pe.did(mm)
                    yield
                    dve.after(a)
                    bank_read[4] = dve.did(V.scalar_tensor_tensor(
                        out=first.rearrange("p (g s) -> p g s", g=3), in0=banks[4][:, 0:384].rearrange(
                            "p (g s) -> p g s", g=3), scalar=scale, in1=own_mask, op0=ALU.mult, op1=ALU.add))
                    for b, g0, ng in ((5, 0, 2), (6, 2, 1)):
                        src = banks[b][:, 0:ng * S].rearrange("p (g n s) -> p g n s", g=ng, n=2)
                        for n, mask in ((0, prev_mask), (1, own_mask)):
                            bank_read[b] = dve.did(V.scalar_tensor_tensor(
                                out=sec4[:, g0:g0 + ng, n, :], in0=src[:, :, n, :], scalar=scale,
                                in1=mask[:, g0:g0 + ng, :], op0=ALU.mult, op1=ALU.add))
                    dve.after(bank_read[6])
                    dve.did(V.tensor_reduce(st[:, 0:1], first, AX, ALU.max))
                    a = dve.did(V.tensor_reduce(st[:, 1:2], second, AX, ALU.max))
                    dve.after(a)
                    a = dve.did(V.tensor_scalar(st[:, 2:4], st[:, 0:2], -1.0, None, ALU.mult))
                    yield
                    act.after(a)
                    act.did(SC.activation(first, first, ACT.Exp, bias=st[:, 2:3], accum_out=st[:, 4:5]))
                    a = act.did(SC.activation(second, second, ACT.Exp, bias=st[:, 3:4], accum_out=st[:, 5:6]))
                    yield
                    dve.after(a)
                    a = dve.did(V.reciprocal(st[:, 6:8], st[:, 4:6]))
                    dve.after(a)
                    dve.did(V.tensor_scalar(first, first, st[:, 6:7], None, ALU.mult))
                    a = dve.did(V.tensor_scalar(second, second, st[:, 7:8], None, ALU.mult))
                    yield
                    pe.after(a)
                    turned = []
                    for b in range(3):
                        pe.after(bank_read[4 + b])
                        for i in range(3):
                            mm = T.transpose(banks[4 + b][:, i * P:(i + 1) * P],
                                             masked_s[:, (3 * b + i) * P:(3 * b + i + 1) * P], ident)
                        turned.append(pe.did(mm))
                    yield
                    for b, a in enumerate(turned):
                        e_ = (act, dve, act)[b]
                        e_.after(a)
                        dst, src = probs_T[:, 3 * b * P:3 * (b + 1) * P], banks[4 + b][:, 0:384]
                        bank_read[4 + b] = e_.did(V.tensor_copy(dst, src) if b == 1 else SC.copy(dst, src))
                    yield
                    pe.after(bank_read[4], bank_read[5], bank_read[6], bank_read[7], *[ready["va", j] for j in range(6)])
                    for g in range(ATT_GROUPS):
                        cols = slice((g * 4 + hd) * P, (g * 4 + hd + 1) * P)
                        T.matmul(banks[7][:, 0:P], v_att[:, 0, cols], probs_T[:, g * P:(g + 1) * P],
                                 start=(g == 0), stop=(g == 2))
                    for g in range(ATT_GROUPS):
                        cols = slice((g * 4 + hd) * P, (g * 4 + hd + 1) * P)
                        for n in range(2):
                            at = (3 + 2 * g + n) * P
                            mm = T.matmul(banks[7][:, P:S], v_att[:, n, cols], probs_T[:, at:at + P],
                                          start=(g == 0 and n == 0), stop=(g == 2 and n == 1))
                    a = pe.did(mm)
                    yield
                    bank_read[7] = ready["o_att", hd] = split(banks[7][:, 0:S], [v[:, hd, :] for v in o_att], a)
                    dve.after(bank_read[7])
                    yield

            hg_area.close()
            late = Area("att_")
            gate_ab = late.take(16 * S, 16)
            for e_ in (act, dve):
                e_.after(ready["o_hg"])
            sides.append(attention())
            for j in range(8):
                ready["ab", j] = columns(26 + j, False, through(ACT.Sigmoid, gate_ab[:, 2 * j:2 * j + 2, :]))

            y_ready = []
            ab_ready = [ready["ab", j] for j in range(8)]
            for which, src in ((0, o_hg), (1, o_att)):
                if which == 1:
                    finish_sides()
                src_ready = ready["o_att", 3] if which else ready["o_hg"]
                for i in range(2):
                    b0 = 2 * i
                    pe.after(src_ready, bank_read[b0], bank_read[b0 + 1])
                    for part in range(2):
                        piece = weights.fetch()
                        for u in range(4):
                            for kk in range(2):
                                k = 2 * part + kk
                                mm = three(banks[b0 + u // 2][:, (u % 2) * S:(u % 2) * S + S],
                                           [v[:, kk, u * P:(u + 1) * P] for v in (piece.high, piece.low)],
                                           [v[:, k, :] for v in src], start=(k == 0 and u % 2 == 0), stop=(k == 3))
                        a = weights.release(piece, mm)
                        side_steps(LAYER_STEPS)
                    for jj in range(2):
                        b = b0 + jj
                        tiles = slice(4 * i + 2 * jj, 4 * i + 2 * jj + 2)
                        gates = gate_ab[:, 8 * which + 4 * i + 2 * jj:8 * which + 4 * i + 2 * jj + 2, :]
                        dve.after(a, ab_ready)
                        bank_read[b] = dve.did(V.tensor_tensor(gates, tile2(banks[b][:, :]), gates, ALU.mult))
                        if which == 1:
                            dve.after(bank_read[b])
                            a_ = dve.did(V.tensor_tensor(gates, gates, gate_ab[:, tiles, :], ALU.add))
                            y_ready.append(split(gates, [v[:, tiles, :] for v in x], a_))

            def add_to_residual(done):
                for t in range(TT):
                    for half in range(2):
                        b = 4 + 2 * t + half
                        cols = h[:, t, half * 512:(half + 1) * 512]
                        dve.after(done)
                        bank_read[b] = dve.did(V.tensor_tensor(cols, cols, banks[b][:, :], ALU.add))
                dve.after(bank_read[7])
                act.after(bank_read[7])

            add_to_residual(accumulate(KT, x, y_ready, 4))
            late.close()
            area.close()

            area = Area("mlp_")
            hid = area.take_split(NT2 * S, NT2)
            work = area.take(TT * D, TT)
            relu = [area.take(512, 2) for _ in range(2)]
            relu_free = [None, None]
            fence()
            x_ready = normed(1, work)
            hid_ready = []
            for j in range(NT2 // 2):
                b = j % 4
                done = product(x, x_ready, b, rows=False)
                act.after(done, relu_free[j % 2])
                a = act.did(SC.activation(relu[j % 2], tile2(banks[b][:, :]), ACT.Relu))
                bank_read[b] = a
                pool.after(a)
                a = pool.did(G.tensor_tensor(relu[j % 2], relu[j % 2], relu[j % 2], ALU.mult))
                relu_free[j % 2] = split(relu[j % 2], [v[:, 2 * j:2 * j + 2, :] for v in hid], a)
                hid_ready.append(relu_free[j % 2])
            add_to_residual(accumulate(NT2, hid, hid_ready, 4))
            area.close()
            fence()

        norm_loads = c.sem("loaded_norms")
        with c.repeat("layers", DEPTH) as layer:
            weights.align()
            second_layer(layer)

        fence()
        final = load_small("final", (gains[:, 0, :], A["final_norm_g_2"].partition_broadcast(P)))
        out_sem = c.sem("stored")
        for t in range(TT):
            rstd, a = rms_scale(h, t, gains[:, 1, :])
            dve.after(a, final)
            a = dve.did(V.scalar_tensor_tensor(out=h[:, t, :], in0=h[:, t, :], scalar=rstd, in1=gains[:, 0, :],
                                               op0=ALU.mult, op1=ALU.mult))
            sync.after(a)
            stored = c.raised(out_sem, nc.sync.dma_start(A["out"][0, t * P:(t + 1) * P, :], h[:, t, :]), 16)
            act.after(a)
        sync.after(stored)
        second_area.close()
    return c.seen


INPUTS = ("x", "ln_in_g", "ln_in_b", "w_in", "pool_w", "w_out", "ln1_g", "ln1_b", "ffn_wg", "ffn_wu", "ffn_wd",
          "moe_router", "moe_wg", "moe_wu", "moe_wd", "ln2_g", "ln2_b", "w_in_2", "w_branch_a_2", "w_branch_b_2",
          "w_out_2", "w_up_2", "w_down_2", "final_norm_g_2", "norm1_g_2", "norm2_g_2")


def lay_out(inputs):
    shared, first, second, levels = shape_constants()
    arrays, at = {}, {}
    arrays["const_shared"], at["shared"] = packed(shared)
    arrays["const_first"], at["first"] = packed(first)
    arrays["const_second"], at["second"] = packed(second)

    arrays["const_levels"] = levels

    def by_partition(a):
        return np.asarray(a).reshape(-1, P).T

    cols = [by_partition(inputs["pool_scale"]), by_partition(inputs["hg_lower_bounds_2"])]
    for layer in range(DEPTH):
        cols.append(by_partition(inputs["hg_norm_g_2"][layer]))
    arrays["vecs"] = np.ascontiguousarray(np.concatenate(cols, 1))
    at["vecs"] = {"pool_scale": 0, "hg_lb": 8, "second": 16}
    for n in INPUTS:
        a = np.ascontiguousarray(inputs[n])
        arrays[n] = a.reshape(1, -1) if a.ndim == 1 else a
    return arrays, at


def declare(nc, arrays):
    A = {}
    for n, a in arrays.items():
        A[n] = nc.dram_tensor("in_" + n, a.shape, mybir.dt.from_np(a.dtype), kind="ExternalInput").ap()
    A["out"] = nc.dram_tensor("out_0", (1, S, D), F32, kind="ExternalOutput").ap()
    return A


def kernel(**inputs):
    import concourse.bacc as bacc
    from concourse.bass_utils import run_bass_kernel_spmd

    arrays, at = lay_out(inputs)
    plan = {}
    for _ in range(2):
        nc = bacc.Bacc("TRN2", target_bir_lowering=False, num_devices=1)
        plan = write_program(nc, declare(nc, arrays), at, plan)
    got = run_bass_kernel_spmd(nc, [{"in_" + n: a for n, a in arrays.items()}], core_ids=[0])
    return got.results[0]["out_0"]
```

```python
from contextlib import ExitStack, contextmanager

import numpy as np

import concourse.bass as bass
from concourse import mybir

F32 = mybir.dt.float32
F32R = mybir.dt.float32r
I8 = mybir.dt.int8
I32 = mybir.dt.int32
ALU = mybir.AluOpType
ACT = mybir.ActivationFunctionType
AX = mybir.AxisListType.X

P = 128
D = 1024
S = 256
TT = S // P
KT = D // P
DEPTH = 2
ALPHA = (2 * DEPTH) ** 0.25
LN_EPS = 1e-5
RMS_EPS = 1e-6

POOL_W = 512
POOL_WINDOWS = (2, 4, 8, 16)
SB_HEADS = 8
SB_DIM = 64
FF = 2816
FT = FF // P
E = 8
SLOTS = 128

HG_HEADS = 4
ATT_HEADS = 4
ATT_GROUPS = 3
DILATIONS = (1, 4, 16)
ROPE_DIM = 32
ROPE_THETA = 500000.0
FF2 = 4096
NT2 = FF2 // P
BIG = 30000.0
MASKED = -3.0e30

CHUNK = 2048
RAW = 5
PIECE = CHUNK // 2
PAIRS = 4
TAIL = 3
POOL_PAIRS = (3,)

PIECE_US = 2.56
STEP_US = 2.5

HG_LEVELS = (64, 32, 16, 8, 4, 2, 1)



def shape_constants():
    i = np.arange(P)
    part, free = i[:, None], i[None, :]
    f = np.float32
    c = {}
    c["ident"] = np.eye(P, dtype=f)
    c["ones"] = np.ones((P, P), f)
    c["neg_ge"] = -(part >= free).astype(f)
    c["neg_ones"] = -np.ones((P, P), f)
    c["before"] = (part < free).astype(f)
    c["before_bias"] = np.where(part < free, 0.0, -BIG).astype(f)
    c["upto"] = (part <= free).astype(f)
    c["iota"] = np.broadcast_to(free, (P, P)).astype(f)
    t = np.arange(S)
    c["inv_count"] = np.broadcast_to(
        np.concatenate([1.0 / np.minimum(t + 1, w) for w in POOL_WINDOWS])[None], (P, 4 * S)).astype(f)
    first = {k: v.copy() for k, v in c.items() if k not in ("ident", "ones")}
    shared = {k: c[k] for k in ("ident", "ones")}
    second = {}
    for name, gap in (("own_mask", 0), ("prev_mask", P)):
        delta = part + gap - free
        ok = [(delta >= 0) & (delta % dil == 0) & (delta <= P * dil) for dil in DILATIONS]
        second[name] = np.concatenate([np.where(o, 0.0, MASKED) for o in ok], 1).astype(f)
    lv = [(part // (2 * m) == free // (2 * m)) & (part % (2 * m) < m) & (free % (2 * m) >= m) for m in HG_LEVELS]
    levels = np.concatenate(lv + [part == free], 1).astype(f)
    inv = ROPE_THETA ** (-np.arange(0, ROPE_DIM, 2, dtype=f) / f(ROPE_DIM))
    ang = np.arange(S, dtype=f)[None, :] * inv.astype(f)[:, None]
    pad = np.zeros((P - ROPE_DIM, S), f)
    second["rope_cos"] = np.concatenate([np.cos(ang), np.cos(ang), pad]).astype(f)
    second["rope_sin"] = np.concatenate([np.sin(ang), np.sin(ang), pad]).astype(f)
    half = ROPE_DIM // 2
    swap = np.zeros((P, ROPE_DIM), f)
    for m in range(half):
        swap[m + half, m] = -1.0
        swap[m, m + half] = 1.0
    second["rope_swap"] = swap
    return shared, first, second, levels


def packed(parts):
    where, at = {}, 0
    for k, v in parts.items():
        where[k] = (at, v.shape[1])
        at += v.shape[1]
    return np.ascontiguousarray(np.concatenate(list(parts.values()), 1)), where



class Sem:

    def __init__(self, handle, name):
        self.handle, self.name, self.count = handle, name, 0


class Tok:

    def __init__(self, sem, count, loop):
        self.sem, self.count, self.loop = sem, count, loop


class Loop:
    def __init__(self, name, index, trips, start):
        self.name, self.index, self.trips, self.start, self.open = name, index, trips, start, True


class Counters:

    def __init__(self, nc, ctx, plan):
        self.nc, self.ctx, self.plan, self.seen = nc, ctx, plan, {}
        self.loop, self.sems = None, []

    def sem(self, name):
        s = Sem(self.ctx.enter_context(self.nc.semaphore(name)), name)
        self.sems.append(s)
        return s

    def raised(self, sem, inst, by=1):
        inst.then_inc(sem.handle, by)
        sem.count += by
        return Tok(sem, sem.count, self.loop)

    def now(self, sem):
        return Tok(sem, sem.count, self.loop)

    def value(self, tok):
        lp = tok.loop
        if lp is None:
            return tok.count
        step = self.plan.get(lp.name, {}).get(tok.sem.name, 0)
        if lp.open:
            return lp.index * step + tok.count if step else tok.count
        return tok.count + (lp.trips - 1) * step

    @contextmanager
    def repeat(self, name, trips):
        with self.nc.Fori(0, trips) as i:
            lp = Loop(name, i, trips, {s.name: s.count for s in self.sems})
            self.loop = lp
            yield i
            adds = {s.name: s.count - lp.start[s.name] for s in self.sems}
            self.seen[name] = adds
            lp.open, self.loop = False, None
        for s in self.sems:
            s.count = lp.start[s.name] + trips * adds[s.name]


class Engine:

    def __init__(self, counters, queue, name):
        self.c, self.q = counters, queue
        self.sem = counters.sem("done_" + name)
        self.settled = counters.sem("settled_" + name)
        self.known = {}

    def after(self, *toks):
        best = {}
        for t in toks:
            if isinstance(t, (list, tuple)):
                self.after(*t)
            elif t is not None:
                if t.sem.name not in best or best[t.sem.name].count < t.count or best[t.sem.name].loop is not t.loop:
                    if t.sem.name in best and best[t.sem.name].loop is not t.loop:
                        self._wait(best[t.sem.name])
                    best[t.sem.name] = t
        for t in best.values():
            self._wait(t)

    def _wait(self, t):
        assert t.count > 0 or t.loop is None
        key = (t.sem.name, id(t.loop), id(self.c.loop))
        if self.known.get(key, -1) >= t.count:
            return
        self.known[key] = t.count
        self.q.wait_ge(t.sem.handle, self.c.value(t))

    def did(self, inst):
        return self.c.raised(self.sem, inst)

    def settle(self):
        self.q.sem_inc(self.settled.handle, 1)


class Piece:

    def __init__(self, high, low, ready, pair):
        self.high, self.low, self.ready, self.pair = high, low, ready, pair


class Weights:

    def __init__(self, c, ctx, nc, sync, pe, act, dve, pool):
        self.c, self.nc, self.sync, self.pe, self.act, self.dve, self.pool = c, nc, sync, pe, act, dve, pool

        def sb(name, n, dt):
            return ctx.enter_context(nc.sbuf_tensor(name, [P, n], dt))

        self.raw = [sb(f"raw{i}", CHUNK, F32) for i in range(RAW)]
        self.high = [sb(f"high{i}", PIECE, F32R) for i in range(PAIRS)]
        self.low = [sb(f"low{i}", PIECE, F32R) for i in range(PAIRS)]
        self.landed = [c.sem(f"landed{i}") for i in range(RAW)]
        self.dve_split = [c.sem(f"dve_split{i}") for i in range(RAW)]
        self.pool_split = [c.sem(f"pool_split{i}") for i in range(RAW)]
        self.used = [c.sem(f"used{i}") for i in range(PAIRS)]
        self.wanted, self.ready, self.held = [], [], 0
        self.pool_helps = True
        self.align()

    def align(self):
        assert not self.wanted and not self.ready
        self.slot = self.pair = 0

    def want(self, a, b, *loads):
        self.wanted += [(a, b, loads, 0), (a, b, loads, 1)]

    def _prepare(self, spread):
        a, b, loads, half = self.wanted.pop(0)
        i, p = self.slot, self.pair
        raw = self.raw[i][:, :].rearrange("p (a b) -> p a b", a=a)
        if half == 0:
            self.sync.after(self.c.now(self.dve_split[i]))
            if self.c.loop is not None:
                self.sync.settle()
            self.sync.after(self.c.now(self.pool_split[i]))
            if self.c.loop is not None:
                self.sync.settle()
            for lo, hi, src in loads:
                self.c.raised(self.landed[i], self.sync.q.dma_start(raw[:, :, lo:hi], src), 16)
        rows = a // 2
        src = raw[:, half * rows:(half + 1) * rows, :]
        high, low = (x[p][:, :].rearrange("p (a b) -> p a b", a=rows) for x in (self.high, self.low))
        self.act.after(self.c.now(self.landed[i]), self.c.now(self.used[p]))
        made = self.act.did(self.nc.scalar.copy(high, src))
        if (self.pool_helps and p in POOL_PAIRS) or (spread and p % 2):
            self.pool.after(made)
            inst = self.nc.gpsimd.tensor_tensor(low, src, high.bitcast(F32), ALU.subtract)
            ready = self.c.raised(self.pool_split[i], inst)
        else:
            self.dve.after(made)
            inst = self.nc.vector.tensor_tensor(low, src, high.bitcast(F32), ALU.subtract)
            ready = self.c.raised(self.dve_split[i], inst)
        self.ready.append(Piece(high, low, ready, p))
        self.pair = (p + 1) % PAIRS
        if half:
            self.slot = (i + 1) % RAW

    def fill(self, spread=False):
        while self.wanted and len(self.ready) + self.held < PAIRS:
            self._prepare(spread)

    def fetch(self):
        self.fill()
        piece = self.ready.pop(0)
        self.held += 1
        self.pe.after(piece.ready)
        return piece

    def release(self, piece, inst):
        self.held -= 1
        return self.c.raised(self.used[piece.pair], inst)


def write_program(nc, A, const_at, plan):
    ctx = ExitStack()
    c = Counters(nc, ctx, plan)
    with ctx:
        pe = Engine(c, nc.tensor, "pe")
        dve = Engine(c, nc.vector, "dve")
        act = Engine(c, nc.scalar, "act")
        pool = Engine(c, nc.gpsimd, "pool")
        sync = Engine(c, nc.sync, "sync")
        computing = (pe, dve, act, pool)
        V, G, SC, T = nc.vector, nc.gpsimd, nc.scalar, nc.tensor

        def sb(name, n, dt=F32, parts=P):
            return ctx.enter_context(nc.sbuf_tensor(name, [parts, n], dt))

        weights = Weights(c, ctx, nc, sync, pe, act, dve, pool)
        h = sb("h", TT * D)[:, :].rearrange("p (t d) -> p t d", t=TT)
        xH = sb("x_high", KT * S, F32R)[:, :].rearrange("p (k s) -> p k s", k=KT)
        xL = sb("x_low", KT * S, F32R)[:, :].rearrange("p (k s) -> p k s", k=KT)
        gains = sb("gains", 2 * D)[:, :].rearrange("p (i d) -> p i d", i=2)
        shared = sb("shared", A["const_shared"].shape[1])
        vecs = sb("vecs", A["vecs"].shape[1])
        stats = sb("stats", 64)
        tables = sb("tables", 64)
        banks = [ctx.enter_context(nc.psum_tensor(f"bank{i}", [P, 512], F32)) for i in range(8)]
        bank_read = [None] * 8

        def shared_const(name):
            at, n = const_at["shared"][name]
            return shared[:, at:at + n]

        ident, ones = shared_const("ident"), shared_const("ones")

        class Area:

            def __init__(self, name):
                self.name, self.stack, self.n = name, ExitStack(), 0

            def take(self, n, a=None, b=None, dt=F32):
                self.n += 1
                v = self.stack.enter_context(nc.sbuf_tensor(f"{self.name}{self.n}", [P, n], dt))[:, :]
                if b is not None:
                    return v.rearrange("p (a b c) -> p a b c", a=a, b=b)
                return v if a is None else v.rearrange("p (a b) -> p a b", a=a)

            def take_split(self, n, a):
                return self.take(n, a, dt=F32R), self.take(n, a, dt=F32R)

            def close(self):
                self.stack.close()

        def fence():
            toks = [c.now(e.sem) for e in computing] + [
                c.now(s) for s in weights.used + weights.dve_split + weights.pool_split]
            for e in computing:
                e.after(*toks)
                if c.loop is not None:
                    e.settle()
            for i in range(8):
                bank_read[i] = None

        def load_small(name, *pairs):
            arrived = c.sem("loaded_" + name)
            for dst, src in pairs:
                tok = c.raised(arrived, nc.scalar.dma_start(dst, src), 16)
            return tok

        def tile2(ap):
            return ap.rearrange("p (t n) -> p t n", t=2)

        sides, clock = [], [0.0]

        def add_side(*work):
            sides.extend([g, clock[0]] for g in work)

        def next_step(side):
            took = next(side[0], "end")
            if took == "end":
                sides.remove(side)
            else:
                side[1] = clock[0] + (STEP_US if took is None else took)

        def run_sides(us):
            clock[0] += us
            for side in list(sides):
                if side[1] <= clock[0]:
                    next_step(side)

        def push_sides():
            clock[0] = max([clock[0]] + [side[1] for side in sides])
            for side in list(sides):
                next_step(side)

        def finish_sides():
            while sides:
                push_sides()


        def split(src, dst, ready):
            act.after(ready)
            a = act.did(SC.copy(dst[0], src))
            dve.after(a, ready)
            return dve.did(V.tensor_tensor(dst[1], src, dst[0].bitcast(F32), ALU.subtract))

        def three(out, stationary, moving, start, stop):
            T.matmul(out, stationary[0], moving[0], start=start, stop=False, skip_group_check=True)
            T.matmul(out, stationary[0], moving[1], start=False, stop=False, skip_group_check=True)
            return T.matmul(out, stationary[1], moving[0], start=False, stop=stop, skip_group_check=True)

        def want_columns(w, n):
            weights.want(KT, 256, (0, 256, w[:, :, n * 256:(n + 1) * 256]))

        def want_rows(w, tiles):
            for i in range(tiles // 2):
                weights.want(2, D, (0, D, w[i * 2 * P:(i + 1) * 2 * P, :].rearrange("(k p) n -> p k n", p=P)))

        def product(x, ready, bank, rows):
            pe.after(bank_read[bank])
            out = tile2(banks[bank][:, :])
            for half in range(2):
                piece = weights.fetch()
                pe.after(ready[half::2])
                for j in range(2):
                    for kk in range(KT // 2):
                        k = half * (KT // 2) + kk
                        mine = [v[:, k, j * P:(j + 1) * P] if rows else v[:, k, :] for v in x]
                        w = [v[:, kk, :] if rows else v[:, kk, j * P:(j + 1) * P] for v in (piece.high, piece.low)]
                        mm = three(out[:, j, :], mine if rows else w, w if rows else mine,
                                   start=(k == 0 and j == 0), stop=(k == KT - 1))
                done = weights.release(piece, mm)
                run_sides(PIECE_US)
            return done

        def accumulate(tiles, x, ready, first_bank):
            def step(i, t, piece):
                for half in range(2):
                    mm = three(banks[first_bank + 2 * t + half][:, :],
                               [v[:, i, t * P:(t + 1) * P] for v in x],
                               [v[:, 0, half * 512:(half + 1) * 512] for v in (piece.high, piece.low)],
                               start=(i == 0), stop=(i == tiles - 1))
                return mm

            def get(i):
                piece = weights.fetch()
                pe.after(ready(i) if callable(ready) else ready[i // 2])
                return piece

            for i in range(tiles - TAIL):
                piece = get(i)
                if i == 0:
                    pe.after(*[bank_read[first_bank + b] for b in range(4)])
                    for b in range(4):
                        bank_read[first_bank + b] = None
                for t in range(TT):
                    mm = step(i, t, piece)
                weights.release(piece, mm)
                run_sides(PIECE_US)
            tail = [(i, get(i)) for i in range(tiles - TAIL, tiles)]
            for i, piece in tail:
                mm = step(i, 0, piece)
            done = [pe.did(mm)]
            root_ahead()
            for i, piece in tail:
                last = weights.release(piece, step(i, 1, piece))
            return done + [last]

        def transpose_rows(src, src_ready):
            last = []
            for t in range(TT):
                for g in range(2):
                    b = 2 * t + g
                    pe.after(src_ready[t], bank_read[b])
                    for k in range(4):
                        mm = T.transpose(banks[b][:, k * P:(k + 1) * P],
                                         src[:, t, (4 * g + k) * P:(4 * g + k + 1) * P], ident)
                    done = pe.did(mm)
                    dst = [v[:, 4 * g:4 * g + 4, t * P:(t + 1) * P] for v in (xH, xL)]
                    bank_read[b] = split(banks[b][:, :].rearrange("p (k s) -> p k s", k=4), dst, done)
                    last.append(bank_read[b])
            return last

        def inverse_root(x, ready):
            act.after(ready)
            a = act.did(SC.activation(x, x, ACT.Ln))
            act.after(a)
            return act.did(SC.activation(x, x, ACT.Exp, scale=-0.5))

        def root_ahead():
            act.did(SC.activation(stats[:, 56:57], ones[:, 0:1], ACT.Sqrt))

        def inverse_root_column(v, r, ready):
            act.after(ready)
            dve.after(act.did(SC.activation(r, v, ACT.Sqrt)))
            dve.after(dve.did(V.reciprocal(r, r)))
            step = stats[:, 57:58]
            dve.after(dve.did(V.scalar_tensor_tensor(out=step, in0=r, scalar=v, in1=r, op0=ALU.mult, op1=ALU.mult)))
            dve.after(dve.did(V.tensor_scalar(step, step, -0.5, 1.5, ALU.mult, ALU.add)))
            return dve.did(V.tensor_tensor(r, r, step, ALU.mult))

        def layer_norm(x, t, dst, gains_ready, *ready):
            st = stats[:, 16 * t:16 * t + 12].rearrange("p (a b) -> p a b", a=2)
            mv = stats[:, 16 * t + 12:16 * t + 14]
            rstd, var = stats[:, 16 * t + 14:16 * t + 15], stats[:, 16 * t + 15:16 * t + 16]
            dve.after(*ready)
            for i in range(2):
                a = dve.did(V.bn_stats(st[:, i, :], x[:, t, i * 512:(i + 1) * 512]))
            dve.after(a)
            a = dve.did(V.bn_aggr(mv, st))
            dve.after(a)
            a = dve.did(V.tensor_scalar(var, mv[:, 1:2], LN_EPS, None, ALU.add))
            dve.after(gains_ready)
            centred = dve.did(V.scalar_tensor_tensor(out=dst[:, t, :], in0=x[:, t, :], scalar=mv[:, 0:1],
                                               in1=gains[:, 0, :], op0=ALU.subtract, op1=ALU.mult))
            dve.after(centred, inverse_root_column(var, rstd, a))
            return dve.did(V.scalar_tensor_tensor(out=dst[:, t, :], in0=dst[:, t, :], scalar=rstd,
                                                  in1=gains[:, 1, :], op0=ALU.mult, op1=ALU.add))

        def rms_scale(x, t, scratch, *ready):
            ss, rstd = stats[:, 40 + 2 * t:41 + 2 * t], stats[:, 41 + 2 * t:42 + 2 * t]
            act.after(*ready)
            a = act.did(SC.activation(scratch, x[:, t, :], ACT.Square, accum_out=ss))
            dve.after(a)
            a = dve.did(V.tensor_scalar(ss, ss, 1.0 / D, RMS_EPS, ALU.mult, ALU.add))
            return rstd, inverse_root_column(ss, rstd, a)

        def residual_norm(first_bank, done, gains_ready):
            out = []
            for t in range(TT):
                dve.after(done[t])
                for half in range(2):
                    b = first_bank + 2 * t + half
                    cols = h[:, t, half * 512:(half + 1) * 512]
                    bank_read[b] = dve.did(V.scalar_tensor_tensor(
                        out=cols, in0=cols, scalar=ALPHA, in1=banks[b][:, :], op0=ALU.mult, op1=ALU.add))
                out.append(layer_norm(h, t, h, gains_ready, bank_read[b]))
                weights.fill(spread=True)
            return out

        def load_gains(name, g, b, *free):
            act.after(*free)
            return load_small(name, (gains[:, 0, :], g.partition_broadcast(P)),
                              (gains[:, 1, :], b.partition_broadcast(P)))

        x_in = c.sem("loaded_x0"), c.sem("loaded_x1")
        h_loaded = [c.raised(x_in[t], nc.sync.dma_start(h[:, t, :], A["x"][0, t * P:(t + 1) * P, :]), 16)
                    for t in range(TT)]
        gains_loaded = load_small("start", (gains[:, 0, :], A["ln_in_g"].partition_broadcast(P)),
                                  (gains[:, 1, :], A["ln_in_b"].partition_broadcast(P)))
        second_area = Area("second_const")
        second_const = second_area.take(A["const_second"].shape[1])
        hg_levels = second_area.take(A["const_levels"].shape[1], len(HG_LEVELS) + 1, dt=I8)
        cur = second_area.take(28)
        lbs = second_area.take(48)

        first_area = Area("first_const")
        first_const = first_area.take(A["const_first"].shape[1])
        ident_loaded = load_small("shared", (shared[:, :], A["const_shared"]))
        const_loaded = load_small("consts", (first_const, A["const_first"]), (vecs[:, :], A["vecs"]))

        def fc(name):
            at, n = const_at["first"][name]
            return first_const[:, at:at + n]

        neg_ge, neg_ones, before, before_bias = fc("neg_ge"), fc("neg_ones"), fc("before"), fc("before_bias")
        upto, iota = fc("upto"), fc("iota")
        inv_count = fc("inv_count").rearrange("p (g s) -> p g s", g=4)

        def layer_vec(name, layer, n):
            at = const_at["vecs"][name] + layer * n
            return vecs[:, at:at + n]

        def first_mixer(layer, h_ready):
            area = Area(f"mixer{layer}_")
            uT, qT, kT = (area.take(4 * S, 4) for _ in range(3))
            v = area.take(TT * 512, TT)
            mix = area.take_split(KT * S, KT)
            sums, lagged = area.take(4 * S, 4), area.take(4 * S, 4)
            pool_w = area.take(4 * P, 4)
            soft, expo, mag = (area.take(2 * 384, 2) for _ in range(3))
            soft2, expo2, mag2 = (area.take(2 * 384, 2) for _ in range(3))
            fence()
            pool_w_loaded = load_small(
                f"pool_w{layer}", (pool_w, A["pool_w"][layer].rearrange("g c d -> c g d")))
            gains_ready = load_gains(
                f"ln1_{layer}", A["ln1_g"][layer:layer + 1, :], A["ln1_b"][layer:layer + 1, :], h_ready)
            x = (xH, xL)
            x_ready = transpose_rows(h, h_ready)

            ready = {}

            def next_chunk(i, name, j):
                b = i % 3
                done = product(x, x_ready, b, rows=(name == "v"))
                src = tile2(banks[b][:, :])
                if name == "v":
                    act.after(done)
                    bank_read[b] = act.did(SC.copy(v[:, :, j * 256:(j + 1) * 256], src))
                else:
                    act.after(done)
                    dst = {"u": uT, "q": qT, "k": kT}[name][:, 2 * j:2 * j + 2, :]
                    bank_read[b] = act.did(SC.activation(dst, src, ACT.Copy, scale=0.125 if name == "q" else 1.0))
                ready[name, j] = bank_read[b]

            def stick_breaking(first_pair):
                sp, ex, mg = (soft, expo, mag) if first_pair == 0 else (soft2, expo2, mag2)
                zb = (4, 5) if first_pair == 0 else (6, 7)
                for pair in (first_pair, first_pair + 2):
                    j = pair // 2
                    while ("k", j) not in ready:
                        yield
                    pe.after(ready["q", j], ready["k", j], *[bank_read[b] for b in zb])
                    for e in range(2):
                        lo = SB_DIM * e
                        q_, k_ = qT[lo:lo + SB_DIM, pair, :], kT[lo:lo + SB_DIM, pair, :]
                        z = banks[zb[e]]
                        T.matmul(z[:, 0:256], k_[:, 0:P], q_, start=True, stop=True)
                        mm = T.matmul(z[:, 256:384], k_[:, P:S], q_[:, P:S], start=False, stop=True,
                                      skip_group_check=True)
                    scored = pe.did(mm)
                    yield
                    act.after(scored)
                    for e in range(2):
                        a = act.did(SC.activation(mg[:, e, :], banks[zb[e]][:, 0:384], ACT.Abs))
                    act.after(a)
                    a = act.did(SC.activation(ex, mg, ACT.Exp, scale=-1.0))
                    act.after(a)
                    a = act.did(SC.activation(mg, ex, ACT.Ln, bias=1.0))
                    yield
                    dve.after(a)
                    for e in range(2):
                        a = dve.did(V.scalar_tensor_tensor(out=sp[:, e, :], in0=banks[zb[e]][:, 0:384], scalar=0.0,
                                                           in1=mg[:, e, :], op0=ALU.max, op1=ALU.add))
                    dve.after(a)
                    two = before.unsqueeze(1).to_broadcast((P, 2, P))
                    dve.did(V.tensor_tensor(sp[:, :, 0:P], sp[:, :, 0:P], two, ALU.mult))
                    masked = dve.did(V.tensor_tensor(sp[:, :, 256:384], sp[:, :, 256:384], two, ALU.mult))
                    yield
                    pe.after(masked, const_loaded)
                    for e in range(2):
                        z = banks[zb[e]]
                        T.matmul(z[:, 0:256], neg_ge, sp[:, e, 0:256], start=False, stop=True, skip_group_check=True)
                        T.matmul(z[:, P:256], neg_ones, sp[:, e, 256:384], start=False, stop=True,
                                 skip_group_check=True)
                        mm = T.matmul(z[:, 256:384], neg_ge, sp[:, e, 256:384], start=False, stop=True,
                                      skip_group_check=True)
                    summed = pe.did(mm)
                    yield
                    dve.after(summed)
                    for e in range(2):
                        z = banks[zb[e]]
                        dve.did(V.scalar_tensor_tensor(out=ex[:, e, 0:P], in0=z[:, 0:P], scalar=0.0, in1=before_bias,
                                                       op0=ALU.min, op1=ALU.add))
                        dve.did(V.scalar_tensor_tensor(out=ex[:, e, 256:384], in0=z[:, 256:384], scalar=0.0,
                                                       in1=before_bias, op0=ALU.min, op1=ALU.add))
                        a = dve.did(V.tensor_scalar(ex[:, e, P:256], z[:, P:256], 0.0, None, ALU.min))
                        bank_read[zb[e]] = a
                    yield
                    act.after(a)
                    att = act.did(SC.activation(mg, ex, ACT.Exp))
                    yield
                    while ("v", j) not in ready:
                        yield
                    pe.after(att, ready["v", j], bank_read[zb[0]])
                    for e in range(2):
                        lo, head = SB_DIM * e, 2 * pair + e
                        y = banks[zb[0]][lo:lo + SB_DIM, 0:256]
                        T.matmul(y, v[:, 0, head * SB_DIM:(head + 1) * SB_DIM], mg[:, e, 0:256], start=True, stop=True)
                        mm = T.matmul(y[:, P:S], v[:, 1, head * SB_DIM:(head + 1) * SB_DIM], mg[:, e, 256:384],
                                      start=False, stop=True, skip_group_check=True)
                    done = pe.did(mm)
                    yield
                    ready["y", pair] = bank_read[zb[0]] = split(
                        banks[zb[0]][:, 0:256], [m[:, 4 + pair, :] for m in mix], done)
                    yield

            def pool_mixer():
                src, a = uT, [ready["u", 0], ready["u", 1]]
                for g, w_ in enumerate(POOL_WINDOWS):
                    lag = w_ // 2
                    dst = sums if g % 2 == 0 else lagged
                    pool.after(a)
                    a1 = pool.did(G.tensor_copy(dst[:, g:4, 0:lag], src[:, g:4, 0:lag]))
                    a2 = pool.did(G.tensor_tensor(dst[:, g:4, lag:S], src[:, g:4, lag:S], src[:, g:4, 0:S - lag],
                                                  ALU.add))
                    a = [a1, a2]
                    src = dst
                pooled = []
                for g in range(4):
                    s_ = (sums if g % 2 == 0 else lagged)[:, g, :]
                    pool.after(a)
                    a1 = pool.did(G.tensor_tensor(s_, s_, inv_count[:, g, :], ALU.mult))
                    pool.after(a1)
                    pooled.append(pool.did(G.tensor_tensor(s_, s_, uT[:, g, :], ALU.subtract)))
                for _ in range(3):
                    yield
                for g in range(4):
                    s_ = (sums if g % 2 == 0 else lagged)[:, g, :]
                    pe.after(pooled[g], pool_w_loaded, bank_read[3])
                    mapped = pe.did(T.matmul(banks[3][:, 0:256], pool_w[:, g, :], s_, start=True, stop=True))
                    yield
                    act.after(mapped)
                    bank_read[3] = act.did(SC.activation(s_, banks[3][:, 0:256], ACT.Copy,
                                                         scale=layer_vec("pool_scale", layer, 4)[:, g:g + 1]))
                    ready["pool", g] = split(s_, [m[:, g, :] for m in mix], bank_read[3])
                    yield

            for e_ in (act, dve, pool):
                e_.after(const_loaded)
            next_chunk(0, "u", 0)
            next_chunk(1, "u", 1)
            if layer == 1:
                lower_bounds()
            add_side(pool_mixer())
            next_chunk(2, "q", 0)
            next_chunk(3, "k", 0)
            add_side(stick_breaking(0), stick_breaking(1))
            for i, (name, j) in enumerate((("v", 0), ("q", 1), ("k", 1), ("v", 1))):
                next_chunk(4 + i, name, j)

            def mix_ready(i):
                key = ("pool", i) if i < 4 else ("y", i - 4)
                while key not in ready:
                    push_sides()
                return ready[key]

            mix_ready(3)
            done = accumulate(KT, mix, mix_ready, 0)
            finish_sides()
            area.close()
            return residual_norm(0, done, gains_ready)

        def dense_ffn(h_ready):
            area = Area("ffn_")
            levels_in = area.take(A["const_levels"].shape[1])
            hid = area.take_split(FT * S, FT)
            gate = [area.take(512, 2) for _ in range(2)]
            fence()
            levels_loaded = load_small("second", (second_const, A["const_second"]), (levels_in, A["const_levels"]))
            pool.after(levels_loaded)
            pool.did(G.tensor_copy(hg_levels.rearrange("p l s -> p (l s)"), levels_in))
            gains_ready = load_gains("ln2_0", A["ln2_g"][0:1, :], A["ln2_b"][0:1, :], h_ready)
            x, x_ready = (xH, xL), transpose_rows(h, h_ready)
            hid_ready, gate_free = [], [None, None]
            for j in range(FT // 2):
                bg, bu = (0, 1) if j % 2 == 0 else (2, 3)
                done = product(x, x_ready, bg, rows=False)
                act.after(done, gate_free[j % 2])
                bank_read[bg] = act.did(SC.activation(gate[j % 2], tile2(banks[bg][:, :]), ACT.Silu))
                done = product(x, x_ready, bu, rows=False)
                dve.after(done, bank_read[bg])
                bank_read[bu] = dve.did(V.tensor_tensor(gate[j % 2], tile2(banks[bu][:, :]), gate[j % 2], ALU.mult))
                gate_free[j % 2] = split(gate[j % 2], [v[:, 2 * j:2 * j + 2, :] for v in hid], bank_read[bu])
                hid_ready.append(gate_free[j % 2])
            done = accumulate(FT, hid, hid_ready, 4)
            area.close()
            return residual_norm(4, done, gains_ready)

        def moe_ffn(h_ready):
            weights.pool_helps = False
            area = Area("moe_")
            router = area.take(KT * E, KT)
            router_split = area.take(KT * 2 * E, KT, dt=F32R)
            logits_T = area.take(S)
            r = {n: area.take(TT * E, TT) for n in ("logits", "first", "rest", "second", "t0", "t1")}
            r.update({n: area.take(TT * (E + 1), TT) for n in ("sel", "gate")})
            mx = area.take(8)
            base = area.take(2 * TT * (E + 1), 2, TT)
            table, table_i = tables[:, 0:32], tables[:, 32:64].bitcast(I32)
            pick, pickg = area.take(TT * P, TT), area.take(TT * P, TT)
            pickT = [area.take(TT * P, TT) for _ in range(2)]
            xs = [area.take_split(KT * SLOTS, KT) for _ in range(2)]
            y = [area.take(D) for _ in range(2)]
            hidT = area.take_split(FT * SLOTS, FT)
            gate_s, hid_s = [area.take(256) for _ in range(2)], [area.take(256) for _ in range(2)]
            total = area.take(TT * D, TT)
            fence()
            gains_ready = load_gains("ln2_1", A["ln2_g"][1:2, :], A["ln2_b"][1:2, :], h_ready)
            router_ready = load_small("router", (router, A["moe_router"][0].rearrange("(k p) e -> p k e", p=P)))
            x_ready = transpose_rows(h, h_ready)
            router_ready = split(router, [router_split[:, :, i * E:(i + 1) * E] for i in range(2)], router_ready)
            for v_ in (total, y[1], pickT[1], r["sel"], r["gate"], base):
                zeroed = pool.did(G.memset(v_, 0.0))
            pe.after(x_ready, router_ready, bank_read[4])
            for k in range(KT):
                for v_ in (xH, xL):
                    mm = T.matmul(banks[4][0:2 * E, 0:S], router_split[:, k, :], v_[:, k, :],
                                  start=(k == 0 and v_ is xH), stop=(k == KT - 1 and v_ is xL))
            act.after(pe.did(mm))
            a = act.did(SC.copy(logits_T[0:2 * E, :], banks[4][0:2 * E, 0:S]))
            pe.after(a)
            for t in range(TT):
                mm = T.transpose(banks[5][:, t * 2 * E:(t + 1) * 2 * E], logits_T[0:2 * E, t * P:(t + 1) * P],
                                 ident[0:2 * E, 0:2 * E])
            a = pe.did(mm)

            def vec(inst):
                t_ = dve.did(inst)
                dve.after(t_)
                return t_

            def bc(col):
                return col.unsqueeze(2).to_broadcast((P, TT, E))

            dve.after(a)
            parts = banks[5][:, 0:TT * 2 * E].rearrange("p (t i e) -> p t i e", t=TT, i=2)
            vec(V.tensor_copy(r["logits"], parts[:, :, 0, :]))
            a = vec(V.tensor_tensor(r["logits"], r["logits"], parts[:, :, 1, :], ALU.add))
            bank_read[5] = a

            def choose(source, sel, col):
                vec(V.tensor_reduce(mx[:, col:col + 2], source, AX, ALU.max))
                vec(V.tensor_tensor(r["t0"], source, bc(mx[:, col:col + 2]), ALU.is_equal))
                for t in range(TT):
                    vec(V.tensor_tensor_scan(r["t1"][:, t, :], ones[:, 0:E], r["t0"][:, t, :], 0.0,
                                             ALU.mult, ALU.add))
                vec(V.tensor_scalar(r["t1"], r["t1"], 1.0, None, ALU.is_equal))
                vec(V.tensor_tensor(sel, r["t0"], r["t1"], ALU.mult))

            choose(r["logits"], r["first"], 0)
            vec(V.scalar_tensor_tensor(out=r["rest"], in0=r["first"], scalar=-3.0e38, in1=r["logits"],
                                       op0=ALU.mult, op1=ALU.add))
            choose(r["rest"], r["second"], 2)
            a = vec(V.tensor_tensor(mx[:, 4:6], mx[:, 2:4], mx[:, 0:2], ALU.subtract))
            act.after(a)
            a = act.did(SC.activation(mx[:, 4:6], mx[:, 4:6], ACT.Exp))
            dve.after(a)
            vec(V.tensor_scalar(mx[:, 6:8], mx[:, 4:6], 1.0, None, ALU.add))
            vec(V.reciprocal(mx[:, 6:8], mx[:, 6:8]))
            vec(V.tensor_tensor(mx[:, 4:6], mx[:, 4:6], mx[:, 6:8], ALU.mult))
            vec(V.tensor_tensor(r["t0"], r["first"], bc(mx[:, 6:8]), ALU.mult))
            vec(V.tensor_tensor(r["t1"], r["second"], bc(mx[:, 4:6]), ALU.mult))
            dve.after(zeroed)
            vec(V.tensor_tensor(r["gate"][:, :, 0:E], r["t0"], r["t1"], ALU.add))
            a = vec(V.tensor_tensor(r["sel"][:, :, 0:E], r["first"], r["second"], ALU.add))
            pe.after(a)
            T.matmul(banks[5][:, 0:E], upto, r["sel"][:, 0, 0:E], start=True, stop=True)
            T.matmul(banks[5][:, E:2 * E], upto, r["sel"][:, 1, 0:E], start=True, stop=False)
            T.matmul(banks[5][:, E:2 * E], ones, r["sel"][:, 0, 0:E], start=False, stop=True)
            T.matmul(banks[5][:, 2 * E:3 * E], ones, r["sel"][:, 0, 0:E], start=True, stop=False)
            a = pe.did(T.matmul(banks[5][:, 2 * E:3 * E], ones, r["sel"][:, 1, 0:E], start=False, stop=True))
            dve.after(a)
            ranks = banks[5][:, 0:2 * E].rearrange("p (t e) -> p t e", t=TT)
            vec(V.tensor_scalar(base[:, 0, :, 0:E], ranks, -1.0, None, ALU.add))
            vec(V.tensor_scalar(base[:, 1, :, 0:E], ranks, -1.0 - SLOTS, None, ALU.add))
            wg, wu, wd = A["moe_wg"][0], A["moe_wu"][0], A["moe_wd"][0]

            def gather(e, block, buf):
                for t in range(TT):
                    picked = dve.did(V.tensor_scalar(pick[:, t, :], iota, base[:, block, t, bass.ds(e, 1)],
                                                     r["sel"][:, t, bass.ds(e, 1)], ALU.is_equal, ALU.mult))
                dve.after(picked)
                for t in range(TT):
                    pickg_ready = dve.did(V.tensor_scalar(pickg[:, t, :], pick[:, t, :],
                                                          r["gate"][:, t, bass.ds(e, 1)], None, ALU.mult))
                yield
                for g in range(2):
                    pe.after(picked, bank_read[6 + g])
                    for k in range(4):
                        for t in range(TT):
                            kk = 4 * g + k
                            mm = T.matmul(banks[6 + g][:, k * P:(k + 1) * P], h[:, t, kk * P:(kk + 1) * P],
                                          pick[:, t, :], start=(t == 0), stop=(t == TT - 1))
                    a = pe.did(mm)
                    yield
                    bank_read[6 + g] = split(banks[6 + g][:, :].rearrange("p (k s) -> p k s", k=4),
                                             [v[:, 4 * g:4 * g + 4, :] for v in xs[buf]], a)
                    yield
                xs_ready[buf] = bank_read[7]
                pe.after(pickg_ready, bank_read[6])
                for t in range(TT):
                    mm = T.transpose(banks[6][:, t * P:(t + 1) * P], pickg[:, t, :], ident)
                a = pe.did(mm)
                yield
                act.after(a)
                pickT_ready[buf] = bank_read[6] = act.did(SC.copy(pickT[buf], tile2(banks[6][:, 0:2 * P])))
                yield

            def scatter(buf):
                for t in range(TT):
                    for half in range(2):
                        b = 6 + half
                        pe.after(bank_read[b], y_ready[buf], pickT_ready[buf])
                        a = pe.did(T.matmul(banks[b][:, :], pickT[buf][:, t, :],
                                            y[buf][:, half * 512:(half + 1) * 512], start=True, stop=True))
                        yield
                        cols = total[:, t, half * 512:(half + 1) * 512]
                        dve.after(a)
                        bank_read[b] = dve.did(V.tensor_tensor(cols, cols, banks[b][:, :], ALU.add))
                yield

            xs_ready, pickT_ready, y_ready = [None, None], [None, None], [None, None]

            def want_expert(e):
                one = (bass.ds(e, 1), slice(None), slice(None))
                g_, u_ = (w[one].rearrange("e (k p) n -> p (e k) n", p=P) for w in (wg, wu))
                for j in range(FT // 2):
                    for ks in (slice(0, 4), slice(4, 8)):
                        cols = slice(j * 256, (j + 1) * 256)
                        weights.want(4, 512, (0, 256, g_[:, ks, cols]), (256, 512, u_[:, ks, cols]))
                want_rows(wd[one].rearrange("e r n -> (e r) n"), FT)

            def expert(buf):
                hid_free, waiting, hidT_ready = [None, None], None, []

                def turn(j, hid_done):
                    b = 2 + j % 2
                    pe.after(hid_done, bank_read[b])
                    for i in range(2):
                        mm = T.transpose(banks[b][:, i * P:(i + 1) * P], hid_s[j % 2][:, i * P:(i + 1) * P], ident)
                    a = pe.did(mm)
                    hid_free[j % 2] = a
                    bank_read[b] = split(tile2(banks[b][:, 0:2 * P]), [v[:, 2 * j:2 * j + 2, :] for v in hidT], a)
                    hidT_ready.append(bank_read[b])

                for j in range(FT // 2):
                    b = j % 2
                    pe.after(xs_ready[buf], bank_read[b])
                    for part in range(4):
                        piece = weights.fetch()
                        for kk in range(2):
                            k = 2 * part + kk
                            mm = three(banks[b][:, :], [v[:, k, :] for v in xs[buf]],
                                       [v[:, kk, :] for v in (piece.high, piece.low)],
                                       start=(k == 0), stop=(k == KT - 1))
                        done = weights.release(piece, mm)
                        run_sides(PIECE_US / 2)
                    if waiting:
                        turn(*waiting)
                    act.after(done, hid_free[b])
                    a = act.did(SC.activation(gate_s[b], banks[b][:, 0:256], ACT.Silu))
                    dve.after(a, done, hid_free[b])
                    bank_read[b] = dve.did(V.tensor_tensor(hid_s[b], banks[b][:, 256:512], gate_s[b], ALU.mult))
                    waiting = (j, bank_read[b])
                turn(*waiting)
                for i in range(FT):
                    piece = weights.fetch()
                    pe.after(hidT_ready[i // 2], bank_read[4], bank_read[5])
                    for half in range(2):
                        mm = three(banks[4 + half][:, :], [v[:, i, :] for v in hidT],
                                   [v[:, 0, half * 512:(half + 1) * 512] for v in (piece.high, piece.low)],
                                   start=(i == 0), stop=(i == FT - 1))
                    done = weights.release(piece, mm)
                act.after(done)
                bank_read[4] = act.did(SC.copy(y[buf][:, 0:512], banks[4][:, :]))
                dve.after(done)
                bank_read[5] = dve.did(V.tensor_copy(y[buf][:, 512:D], banks[5][:, :]))
                y_ready[buf] = [bank_read[4], bank_read[5]]

            def after_the_last(*work):
                for g in work:
                    yield from g

            add_side(gather(0, 0, 0))
            for _ in range(4):
                push_sides()
            over, order, hit = table[:, 0:8], table[:, 8:16], table[:, 24:32]
            vec(V.tensor_scalar(over, banks[5][:, 2 * E:3 * E], float(SLOTS), None, ALU.is_gt))
            vec(V.tensor_tensor_scan(order, ones[:, 0:E], over, 0.0, ALU.mult, ALU.add))
            for j in range(3):
                vec(V.tensor_scalar(hit, order, float(j + 1), None, ALU.is_equal))
                vec(V.tensor_tensor(hit, hit, over, ALU.mult))
                vec(V.tensor_reduce(table[:, 16 + 4 + j:17 + 4 + j], hit, AX, ALU.max))
                vec(V.tensor_tensor(hit, hit, iota[:, 0:E], ALU.mult))
                vec(V.tensor_reduce(table[:, 16 + j:17 + j], hit, AX, ALU.add))
            vec(V.tensor_copy(table[:, 19:20], table[:, 20:21]))
            vec(V.tensor_scalar(table[:, 20:23], table[:, 20:23], -float(E), float(E), ALU.mult, ALU.add))
            vec(V.tensor_tensor(table[:, 20:23], table[:, 20:23], table[:, 16:19], ALU.add))
            vec(V.tensor_copy(table_i[:, 16:23], table[:, 16:23]))
            finish_sides()
            fence()
            with c.repeat("experts", E // 4) as i:
                weights.align()
                for n in range(4):
                    want_expert(i * 4 + n)
                for n in range(4):
                    add_side(after_the_last(scatter(1 - n % 2), gather(i * 4 + 1 + n, 0, 1 - n % 2)))
                    expert(n % 2)
                fence()
            weights.align()
            add_side(scatter(1))
            finish_sides()

            meet = c.sem("meet")
            everyone = (*computing, sync)
            toks = [c.now(e_.sem) for e_ in computing] + [
                c.now(s) for s in weights.used + weights.landed + weights.dve_split + weights.pool_split]
            for e_ in everyone:
                e_.after(*toks)
                e_.q.sem_inc(meet.handle, 1)
            meet.count += len(everyone)
            for e_ in everyone:
                e_.after(c.now(meet))
            for i in range(8):
                bank_read[i] = None
            any_over = nc.values_load(table_i[0:1, 19:20], min_val=0, max_val=1)
            before_passes = {s.name: s.count for s in c.sems}
            with nc.If(any_over):
                with c.repeat("overflow", 3) as j:
                    weights.align()
                    who = nc.values_load(table_i[0:1, bass.ds(j + 16, 1)], min_val=0, max_val=E - 1)
                    whose = nc.values_load(table_i[0:1, bass.ds(j + 20, 1)], min_val=0, max_val=E)
                    want_expert(who)
                    add_side(gather(whose, 1, 0))
                    finish_sides()
                    expert(0)
                    add_side(scatter(0))
                    finish_sides()
                    fence()
            with nc.Else():
                for s, owner in [(e_.sem, e_) for e_ in computing] + [(s, pe) for s in weights.used] + [
                        (s, sync) for s in weights.landed] + [
                        (s, dve) for s in weights.dve_split] + [(s, pool) for s in weights.pool_split]:
                    if s.count > before_passes[s.name]:
                        owner.q.sem_inc(s.handle, s.count - before_passes[s.name])
            for e_ in everyone:
                e_.known = {}
            weights.align()
            out = []
            fence()
            area.close()
            for t in range(TT):
                a = dve.did(V.scalar_tensor_tensor(out=h[:, t, :], in0=h[:, t, :], scalar=ALPHA,
                                                   in1=total[:, t, :], op0=ALU.mult, op1=ALU.add))
                out.append(layer_norm(h, t, h, gains_ready, a))
            return out

        def lower_bounds():
            lb_at = const_at["vecs"]["hg_lb"]
            lb0, lb1 = vecs[:, lb_at:lb_at + 4], vecs[:, lb_at + 4:lb_at + 8]
            x_, n_, l_ = lbs[:, 16:20], lbs[:, 20:24], lbs[:, 24:28]
            a = dve.did(V.tensor_tensor(x_, lb1, lb0, ALU.subtract))
            dve.did(V.memset(lbs[:, 0:4], -1.0e30))
            dve.did(V.memset(lbs[:, 8:12], 0.0))
            dve.after(a)
            act.after(a)
            a = act.did(SC.activation(n_, x_, ACT.Abs))
            act.after(a)
            a = act.did(SC.activation(l_, n_, ACT.Exp, scale=-1.0))
            act.after(a)
            a = act.did(SC.activation(l_, l_, ACT.Ln, bias=1.0))
            dve.after(a)
            a = dve.did(V.scalar_tensor_tensor(out=lbs[:, 4:8], in0=x_, scalar=0.0, in1=l_, op0=ALU.min, op1=ALU.subtract))
            dve.after(a)
            dve.did(V.tensor_tensor(lbs[:, 12:16], lbs[:, 4:8], x_, ALU.subtract))

        def want_mixer(layer):
            w = A["w_in"][layer].rearrange("(k p) n -> p k n", p=P)
            for col in (0, 1, 2, 4, 6, 3, 5, 7):
                want_columns(w, col)
            want_rows(A["w_out"][layer], KT)

        want_mixer(0)
        wg, wu = (A[n][0].rearrange("(k p) n -> p k n", p=P) for n in ("ffn_wg", "ffn_wu"))
        for j in range(FT // 2):
            want_columns(wg, j)
            want_columns(wu, j)
        want_rows(A["ffn_wd"][0], FT)
        want_mixer(1)

        h_ready = [layer_norm(h, t, h, gains_loaded, h_loaded[t]) for t in range(TT)]
        pe.after(ident_loaded)
        h_ready = first_mixer(0, h_ready)
        h_ready = dense_ffn(h_ready)
        h_ready = first_mixer(1, h_ready)
        h_ready = moe_ffn(h_ready)

        weights.pool_helps = False
        first_area.close()
        def sc_(name):
            at, n = const_at["second"][name]
            return second_const[:, at:at + n]

        own_mask = sc_("own_mask").rearrange("p (g s) -> p g s", g=3)
        prev_mask = sc_("prev_mask").rearrange("p (g s) -> p g s", g=3)
        rope_cos, rope_sin, rope_swap = sc_("rope_cos"), sc_("rope_sin"), sc_("rope_swap")
        W4 = HG_HEADS * S
        fence()

        def second_layer(layer):
            area = Area("layer_")
            qkT = area.take(24 * S, 24)
            v_att = area.take(TT * 1536, TT)
            o_hg = area.take_split(W4, 4)
            o_att = area.take_split(W4, 4)
            rope_tmp = area.take(512)
            hg_area = Area("hg_")
            q_hg, z_f, v_hg, g_hg = (hg_area.take(W4, 4) for _ in range(4))
            k_hg = z_f
            v_hg = v_hg.rearrange("p a s -> p (a s)").rearrange("p (t n) -> p t n", t=TT)
            decay = hg_area.take(W4)
            hg_att = hg_area.take(HG_HEADS * 3 * P, HG_HEADS, 3)
            work = hg_area.take(3 * W4)
            w0, w1, w2 = (work[:, i * W4:(i + 1) * W4] for i in range(3))
            norms_loaded = None
            for i, name in enumerate(("norm1_g_2", "norm2_g_2")):
                norms_loaded = c.raised(norm_loads, nc.scalar.dma_start(
                    gains[:, i, :], A[name][bass.ds(layer, 1), :].partition_broadcast(P)), 16)
            w = A["w_in_2"][bass.ds(layer, 1), :, :].rearrange("l (k p) n -> p (l k) n", p=P)
            for col in [2, 3, 0, 1, 4, 5, 6, 7] + list(range(8, 34)):
                want_columns(w, col)
            for name in ("w_branch_a_2", "w_branch_b_2"):
                wv = A[name][bass.ds(layer, 1), :, :].rearrange("l (k p) n -> p (l k) n", p=P)
                for i in range(2):
                    weights.want(4, 512, (0, 512, wv[:, :, i * 512:(i + 1) * 512]))
            want_rows(A["w_out_2"][bass.ds(layer, 1), :, :].rearrange("l r n -> (l r) n"), KT)
            w = A["w_up_2"][bass.ds(layer, 1), :, :].rearrange("l (k p) n -> p (l k) n", p=P)
            for j in range(NT2 // 2):
                want_columns(w, j)
            want_rows(A["w_down_2"][bass.ds(layer, 1), :, :].rearrange("l r n -> (l r) n"), NT2)
            vat = const_at["vecs"]["second"]
            dve.did(V.tensor_copy(cur[:, 0:4], vecs[:, bass.ds(layer * 4 + vat, 4)]))
            dve.did(V.tensor_copy(cur[:, 4:8], lbs[:, bass.ds(layer * 4, 4)]))
            cur_ready = dve.did(V.tensor_copy(cur[:, 8:12], lbs[:, bass.ds(layer * 4 + 8, 4)]))
            dve.after(cur_ready)

            def normed(which, xn):
                ready = []
                for t in range(TT):
                    rstd, a = rms_scale(h, t, xn[:, t, :])
                    dve.after(a, norms_loaded)
                    ready.append(dve.did(V.scalar_tensor_tensor(
                        out=xn[:, t, :], in0=h[:, t, :], scalar=rstd, in1=gains[:, which, :],
                        op0=ALU.mult, op1=ALU.mult)))
                return transpose_rows(xn, ready)

            x = (xH, xL)
            x_ready = normed(0, work[:, 0:TT * D].rearrange("p (t d) -> p t d", t=TT))

            turn = [0]
            ready = {}

            def columns(in_turn, col, rows, finish):
                b = turn[0] % in_turn
                turn[0] += 1
                done = product(x, x_ready, b, rows)
                e_, inst = finish(tile2(banks[b][:, :]), done)
                bank_read[b] = e_.did(inst)
                return bank_read[b]

            def through(fn, dst):
                def finish(src, done):
                    act.after(done)
                    return act, SC.activation(dst, src, fn)
                return finish

            def copied(dst):
                def finish(src, done):
                    dve.after(done)
                    return dve, V.tensor_copy(dst, src)
                return finish

            for i in range(2):
                ready["zf", i] = columns(4, 2 + i, False, copied(z_f[:, 2 * i:2 * i + 2, :]))
            def flat(ap):
                return ap.rearrange("p a s -> p (a s)")

            def per_head(cols):
                return cols.unsqueeze(2).to_broadcast((P, HG_HEADS, S))

            def as4(ap):
                return ap.rearrange("p (a s) -> p a s", a=HG_HEADS)

            def recurrence():
                zf = flat(z_f)
                act.after(ready["zf", 0], ready["zf", 1])
                a = act.did(SC.activation(w0, zf, ACT.Abs))
                act.after(a)
                a = act.did(SC.activation(w0, w0, ACT.Exp, scale=-1.0))
                act.after(a)
                a = act.did(SC.activation(w0, w0, ACT.Ln, bias=1.0))
                yield
                dve.after(a)
                a = dve.did(V.scalar_tensor_tensor(out=w1, in0=zf, scalar=0.0, in1=w0, op0=ALU.min, op1=ALU.subtract))
                dve.after(a)
                a = dve.did(V.tensor_tensor(as4(w1), as4(w1), per_head(cur[:, 8:12]), ALU.add))
                dve.after(a)
                a = dve.did(V.tensor_tensor(w2, w1, zf, ALU.subtract))
                yield
                act.after(a)
                k_ready = act.did(SC.activation(flat(k_hg), w2, ACT.Exp))
                yield
                a = dve.did(V.tensor_tensor(as4(w0), as4(w1), per_head(cur[:, 4:8]), ALU.subtract))
                b_ = dve.did(V.tensor_tensor(as4(w1), as4(w1), per_head(cur[:, 4:8]), ALU.max))
                yield
                act.after(a)
                a = act.did(SC.activation(w0, w0, ACT.Abs))
                act.after(a)
                a = act.did(SC.activation(w0, w0, ACT.Exp, scale=-1.0))
                act.after(a)
                a = act.did(SC.activation(w0, w0, ACT.Ln, bias=1.0))
                yield
                dve.after(a, b_)
                a = dve.did(V.tensor_tensor(w1, w1, w0, ALU.add))
                dve.after(a)
                for n in range(W4 // P):
                    cols = slice(n * P, (n + 1) * P)
                    a = dve.did(V.tensor_tensor_scan(decay[:, cols], ones, w1[:, cols], 0.0, ALU.mult, ALU.add))
                dve.after(a)
                yield
                dec4 = as4(decay)
                att = hg_att
                cleared = pool.did(G.memset(att[:, :, 0:2, :], 0.0))
                qf, kf = flat(q_hg), flat(k_hg)
                last = dec4[:, :, P - 1:P].to_broadcast((P, HG_HEADS, P))
                a = dve.did(V.tensor_tensor(as4(w0)[:, :, 0:P], last, dec4[:, :, 0:P], ALU.subtract))
                yield
                act.after(a)
                a1 = act.did(SC.activation(as4(w0)[:, :, 0:P], as4(w0)[:, :, 0:P], ACT.Exp))
                a2 = act.did(SC.activation(as4(w0)[:, :, P:S], dec4[:, :, P:S], ACT.Exp))
                yield
                while ("q", 1) not in ready:
                    yield
                dve.after(a1, a2, k_ready, ready["q", 0], ready["q", 1])
                dve.did(V.tensor_tensor(as4(w1)[:, :, 0:P], as4(w0)[:, :, 0:P], k_hg[:, :, 0:P], ALU.mult))
                a = dve.did(V.tensor_tensor(as4(w1)[:, :, P:S], as4(w0)[:, :, P:S], q_hg[:, :, P:S], ALU.mult))
                yield
                pe.after(a, bank_read[4])
                for hh in range(HG_HEADS):
                    mm = T.matmul(banks[4][:, hh * P:(hh + 1) * P], as4(w1)[:, hh, 0:P], as4(w1)[:, hh, P:S],
                                  start=True, stop=True)
                a = pe.did(mm)
                yield
                dve.after(a)
                bank_read[4] = dve.did(V.tensor_copy(att[:, :, 2, :], banks[4][:, :].rearrange("p (a s) -> p a s", a=4)))
                dve.after(bank_read[4])
                yield
                for li, m in enumerate(HG_LEVELS + (0,)):
                    if m:
                        blocks = decay.rearrange("p (n s) -> p n s", s=2 * m)
                        ref = blocks[:, :, m - 1:m].to_broadcast((P, W4 // (2 * m), 2 * m))
                        a = dve.did(V.tensor_tensor(w0.rearrange("p (n s) -> p n s", s=2 * m), blocks, ref,
                                                    ALU.subtract))
                        dve.after(a)
                        a = dve.did(V.scalar_tensor_tensor(out=w0, in0=w0, scalar=-1.0, in1=w0, op0=ALU.mult,
                                                           op1=ALU.min))
                        yield
                        act.after(a)
                        a = act.did(SC.activation(w0, w0, ACT.Exp))
                        yield
                        dve.after(a, k_ready)
                        qa = dve.did(V.tensor_tensor(w1, w0, qf, ALU.mult))
                        ka = dve.did(V.tensor_tensor(w2, w0, kf, ALU.mult))
                        qs, ks = as4(w1), as4(w2)
                        yield
                        pe.after(qa, ka)
                    else:
                        qs, ks = q_hg, k_hg
                    b = 4 + 2 * (li % 2)
                    pe.after(bank_read[b], bank_read[b + 1])
                    for hh in range(HG_HEADS):
                        for n in range(2):
                            mm = T.matmul(banks[b + n][:, hh * P:(hh + 1) * P], ks[:, hh, n * P:(n + 1) * P],
                                          qs[:, hh, n * P:(n + 1) * P], start=True, stop=True)
                    a = pe.did(mm)
                    yield
                    dve.after(a, cleared)
                    mask = hg_levels[:, li, :].unsqueeze(1).to_broadcast((P, HG_HEADS, P))
                    dve.settle()
                    for n in range(2):
                        bank_read[b + n] = dve.did(V.copy_predicated(
                            att[:, :, n, :], mask, banks[b + n][:, :].rearrange("p (a s) -> p a s", a=4)))
                    dve.after(bank_read[b + 1])
                while ("g", 1) not in ready:
                    yield
                pe.after(bank_read[b + 1], ready["v", 0], ready["v", 1], bank_read[4], bank_read[5])
                for hh in range(HG_HEADS):
                    o_ = banks[4 + hh // 2][:, (hh % 2) * S:(hh % 2) * S + S]
                    cols = slice(hh * P, (hh + 1) * P)
                    T.matmul(o_[:, 0:P], v_hg[:, 0, cols], att[:, hh, 0, :], start=True, stop=True)
                    T.matmul(o_[:, P:S], v_hg[:, 0, cols], att[:, hh, 2, :], start=True, stop=False)
                    mm = T.matmul(o_[:, P:S], v_hg[:, 1, cols], att[:, hh, 1, :], start=False, stop=True)
                a = pe.did(mm)
                yield
                for n in range(2):
                    yield
                    act.after(a)
                    sq = act.did(SC.activation(w0[:, n * 512:(n + 1) * 512], banks[4 + n][:, :], ACT.Square))
                    yield
                    pe.after(sq, bank_read[6 + n])
                    mm = pe.did(T.matmul(banks[6 + n][:, :], ones, w0[:, n * 512:(n + 1) * 512], start=True, stop=True))
                    yield
                    dve.after(mm)
                    cols = w1[:, n * 512:(n + 1) * 512]
                    a_ = bank_read[6 + n] = dve.did(V.tensor_scalar(cols, banks[6 + n][:, :], 1.0 / P, RMS_EPS,
                                                                    ALU.mult, ALU.add))
                    yield
                    a_ = inverse_root(cols, a_)
                    yield
                    dve.after(a_)
                    a_ = bank_read[4 + n] = dve.did(V.tensor_tensor(cols, cols, banks[4 + n][:, :], ALU.mult))
                    dve.after(a_)
                dve.after(ready["g", 0], ready["g", 1])
                a_ = dve.did(V.tensor_tensor(as4(w1), as4(w1), per_head(cur[:, 0:4]), ALU.mult))
                dve.after(a_)
                a_ = dve.did(V.tensor_tensor(as4(w1), as4(w1), g_hg, ALU.mult))
                ready["o_hg"] = split(as4(w1), o_hg, a_)
                yield

            add_side(recurrence())
            for i in range(2):
                ready["q", i] = columns(3, i, False, through(ACT.Silu, q_hg[:, 2 * i:2 * i + 2, :]))
            for i in range(2):
                ready["v", i] = columns(3, 4 + i, True, copied(v_hg[:, :, i * 256:(i + 1) * 256]))
            for i in range(2):
                ready["g", i] = columns(3, 6 + i, False, through(ACT.Sigmoid, g_hg[:, 2 * i:2 * i + 2, :]))

            def rope():
                sin = rope_sin[0:ROPE_DIM, :].unsqueeze(1).to_broadcast((ROPE_DIM, 2, S))
                cos = rope_cos[0:ROPE_DIM, :].unsqueeze(1).to_broadcast((ROPE_DIM, 2, S))
                tmp = tile2(rope_tmp[0:ROPE_DIM, :])
                rotated = None
                for j in range(12):
                    while ("raw qk", j) not in ready:
                        yield
                    part = qkT[0:ROPE_DIM, 2 * j:2 * j + 2, :]
                    pe.after(ready["raw qk", j], bank_read[3])
                    pe.settle()
                    a = pe.did(T.matmul(banks[3][0:ROPE_DIM, :], rope_swap[0:ROPE_DIM, :], flat(part), start=True,
                                        stop=True))
                    yield
                    dve.after(a, rotated)
                    a1 = bank_read[3] = dve.did(V.tensor_tensor(tmp, tile2(banks[3][0:ROPE_DIM, :]), sin, ALU.mult))
                    a2 = dve.did(V.tensor_tensor(part, part, cos, ALU.mult))
                    dve.after(a1, a2)
                    ready["qk", j] = rotated = dve.did(V.tensor_tensor(part, part, tmp, ALU.add))
                    yield

            add_side(rope())
            for j in range(12):
                ready["raw qk", j] = columns(3, 8 + j, False, through(ACT.Copy, qkT[:, 2 * j:2 * j + 2, :]))
            for j in range(6):
                ready["va", j] = columns(3, 20 + j, True, through(ACT.Copy, v_att[:, :, j * 256:(j + 1) * 256]))
            finish_sides()
            qk_ready = [ready["qk", j] for j in range(12)]

            def attention(worker):
                scale = float(P) ** -0.5
                masked_s, probs_T = scratch[worker]
                b0 = 2 + 3 * worker
                first, second = masked_s[:, 0:384], masked_s[:, 384:1152]
                sec4 = second.rearrange("p (g n s) -> p g n s", g=3, n=2)
                for hd in range(worker, ATT_HEADS, 2):
                    st = stats[:, 48 + 8 * worker:56 + 8 * worker]
                    pe.after(qk_ready, *[bank_read[b0 + b] for b in range(3)])
                    for g in range(ATT_GROUPS):
                        q_, k_ = qkT[:, g * 4 + hd, :], qkT[:, 12 + g * 4 + hd, :]
                        T.matmul(banks[b0][:, g * P:(g + 1) * P], q_[:, 0:P], k_[:, 0:P], start=True, stop=True)
                        dst = banks[b0 + 1 + g // 2][:, (g % 2) * S:(g % 2) * S + S]
                        mm = T.matmul(dst, q_[:, P:S], k_, start=True, stop=True)
                    a = pe.did(mm)
                    yield
                    dve.after(a)
                    bank_read[b0] = dve.did(V.scalar_tensor_tensor(
                        out=first.rearrange("p (g s) -> p g s", g=3), in0=banks[b0][:, 0:384].rearrange(
                            "p (g s) -> p g s", g=3), scalar=scale, in1=own_mask, op0=ALU.mult, op1=ALU.add))
                    for b, g0, ng in ((b0 + 1, 0, 2), (b0 + 2, 2, 1)):
                        src = banks[b][:, 0:ng * S].rearrange("p (g n s) -> p g n s", g=ng, n=2)
                        for n, mask in ((0, prev_mask), (1, own_mask)):
                            bank_read[b] = dve.did(V.scalar_tensor_tensor(
                                out=sec4[:, g0:g0 + ng, n, :], in0=src[:, :, n, :], scalar=scale,
                                in1=mask[:, g0:g0 + ng, :], op0=ALU.mult, op1=ALU.add))
                    dve.after(bank_read[b0 + 2])
                    dve.did(V.tensor_reduce(st[:, 0:1], first, AX, ALU.max))
                    a = dve.did(V.tensor_reduce(st[:, 1:2], second, AX, ALU.max))
                    dve.after(a)
                    a = dve.did(V.tensor_scalar(st[:, 2:4], st[:, 0:2], -1.0, None, ALU.mult))
                    yield
                    act.after(a)
                    act.did(SC.activation(first, first, ACT.Exp, bias=st[:, 2:3], accum_out=st[:, 4:5]))
                    a = act.did(SC.activation(second, second, ACT.Exp, bias=st[:, 3:4], accum_out=st[:, 5:6]))
                    yield
                    dve.after(a)
                    a = dve.did(V.reciprocal(st[:, 6:8], st[:, 4:6]))
                    dve.after(a)
                    dve.did(V.tensor_scalar(first, first, st[:, 6:7], None, ALU.mult))
                    a = dve.did(V.tensor_scalar(second, second, st[:, 7:8], None, ALU.mult))
                    yield
                    pe.after(a)
                    turned = []
                    for b in range(3):
                        pe.after(bank_read[b0 + b])
                        for i in range(3):
                            mm = T.transpose(banks[b0 + b][:, i * P:(i + 1) * P],
                                             masked_s[:, (3 * b + i) * P:(3 * b + i + 1) * P], ident)
                        turned.append(pe.did(mm))
                    yield
                    for b, a in enumerate(turned):
                        e_ = (act, dve, act)[b]
                        e_.after(a)
                        dst, src = probs_T[:, 3 * b * P:3 * (b + 1) * P], banks[b0 + b][:, 0:384]
                        bank_read[b0 + b] = e_.did(V.tensor_copy(dst, src) if b == 1 else SC.copy(dst, src))
                    yield
                    pe.after(*[bank_read[b0 + b] for b in range(3)], *[ready["va", j] for j in range(6)])
                    for g in range(ATT_GROUPS):
                        cols = slice((g * 4 + hd) * P, (g * 4 + hd + 1) * P)
                        T.matmul(banks[b0][:, 0:P], v_att[:, 0, cols], probs_T[:, g * P:(g + 1) * P],
                                 start=(g == 0), stop=(g == 2))
                    for g in range(ATT_GROUPS):
                        cols = slice((g * 4 + hd) * P, (g * 4 + hd + 1) * P)
                        for n in range(2):
                            at = (3 + 2 * g + n) * P
                            mm = T.matmul(banks[b0][:, P:S], v_att[:, n, cols], probs_T[:, at:at + P],
                                          start=(g == 0 and n == 0), stop=(g == 2 and n == 1))
                    a = pe.did(mm)
                    yield
                    bank_read[b0] = ready["o_att", hd] = split(banks[b0][:, 0:S], [v[:, hd, :] for v in o_att], a)
                    dve.after(bank_read[b0])
                    yield

            hg_area.close()
            late = Area("att_")
            gate_ab = late.take(16 * S, 16)
            for e_ in (act, dve):
                e_.after(ready["o_hg"])
            scratch = [(late.take(9 * P), late.take(9 * P)) for _ in range(2)]
            add_side(attention(0), attention(1))
            for j in range(8):
                ready["ab", j] = columns(2, 26 + j, False, through(ACT.Sigmoid, gate_ab[:, 2 * j:2 * j + 2, :]))

            y_ready = []
            ab_ready = [ready["ab", j] for j in range(8)]
            for which, src in ((0, o_hg), (1, o_att)):
                if which == 1:
                    finish_sides()
                src_ready = ready["o_att", 3] if which else ready["o_hg"]
                for i in range(2):
                    b0 = 0
                    pe.after(src_ready, bank_read[b0], bank_read[b0 + 1])
                    for part in range(2):
                        piece = weights.fetch()
                        for u in range(4):
                            for kk in range(2):
                                k = 2 * part + kk
                                mm = three(banks[b0 + u // 2][:, (u % 2) * S:(u % 2) * S + S],
                                           [v[:, kk, u * P:(u + 1) * P] for v in (piece.high, piece.low)],
                                           [v[:, k, :] for v in src], start=(k == 0 and u % 2 == 0), stop=(k == 3))
                        a = weights.release(piece, mm)
                        run_sides(PIECE_US)
                    for jj in range(2):
                        b = b0 + jj
                        tiles = slice(4 * i + 2 * jj, 4 * i + 2 * jj + 2)
                        gates = gate_ab[:, 8 * which + 4 * i + 2 * jj:8 * which + 4 * i + 2 * jj + 2, :]
                        dve.after(a, ab_ready)
                        bank_read[b] = dve.did(V.tensor_tensor(gates, tile2(banks[b][:, :]), gates, ALU.mult))
                        if which == 1:
                            dve.after(bank_read[b])
                            a_ = dve.did(V.tensor_tensor(gates, gates, gate_ab[:, tiles, :], ALU.add))
                            y_ready.append(split(gates, [v[:, tiles, :] for v in x], a_))

            def add_to_residual(done):
                for t in range(TT):
                    for half in range(2):
                        b = 4 + 2 * t + half
                        cols = h[:, t, half * 512:(half + 1) * 512]
                        dve.after(done[t])
                        bank_read[b] = dve.did(V.tensor_tensor(cols, cols, banks[b][:, :], ALU.add))
                dve.after(bank_read[7])
                act.after(bank_read[7])

            add_to_residual(accumulate(KT, x, y_ready, 4))
            late.close()
            area.close()

            area = Area("mlp_")
            hid = area.take_split(NT2 * S, NT2)
            work = area.take(TT * D, TT)
            relu = [area.take(512, 2) for _ in range(2)]
            relu_free = [None, None]
            fence()
            x_ready = normed(1, work)
            hid_ready = []
            for j in range(NT2 // 2):
                b = j % 4
                done = product(x, x_ready, b, rows=False)
                act.after(done, relu_free[j % 2])
                a = act.did(SC.activation(relu[j % 2], tile2(banks[b][:, :]), ACT.Relu))
                bank_read[b] = a
                pool.after(a)
                a = pool.did(G.tensor_tensor(relu[j % 2], relu[j % 2], relu[j % 2], ALU.mult))
                relu_free[j % 2] = split(relu[j % 2], [v[:, 2 * j:2 * j + 2, :] for v in hid], a)
                hid_ready.append(relu_free[j % 2])
            add_to_residual(accumulate(NT2, hid, hid_ready, 4))
            area.close()
            fence()

        norm_loads = c.sem("loaded_norms")
        with c.repeat("layers", DEPTH) as layer:
            weights.align()
            second_layer(layer)

        fence()
        final = load_small("final", (gains[:, 0, :], A["final_norm_g_2"].partition_broadcast(P)))
        out_sem = c.sem("stored")
        for t in range(TT):
            rstd, a = rms_scale(h, t, gains[:, 1, :])
            dve.after(a, final)
            a = dve.did(V.scalar_tensor_tensor(out=h[:, t, :], in0=h[:, t, :], scalar=rstd, in1=gains[:, 0, :],
                                               op0=ALU.mult, op1=ALU.mult))
            sync.after(a)
            stored = c.raised(out_sem, nc.sync.dma_start(A["out"][0, t * P:(t + 1) * P, :], h[:, t, :]), 16)
            act.after(a)
        sync.after(stored)
        second_area.close()
    return c.seen


INPUTS = ("x", "ln_in_g", "ln_in_b", "w_in", "pool_w", "w_out", "ln1_g", "ln1_b", "ffn_wg", "ffn_wu", "ffn_wd",
          "moe_router", "moe_wg", "moe_wu", "moe_wd", "ln2_g", "ln2_b", "w_in_2", "w_branch_a_2", "w_branch_b_2",
          "w_out_2", "w_up_2", "w_down_2", "final_norm_g_2", "norm1_g_2", "norm2_g_2")


def lay_out(inputs):
    shared, first, second, levels = shape_constants()
    arrays, at = {}, {}
    arrays["const_shared"], at["shared"] = packed(shared)
    arrays["const_first"], at["first"] = packed(first)
    arrays["const_second"], at["second"] = packed(second)

    arrays["const_levels"] = levels

    def by_partition(a):
        return np.asarray(a).reshape(-1, P).T

    cols = [by_partition(inputs["pool_scale"]), by_partition(inputs["hg_lower_bounds_2"])]
    for layer in range(DEPTH):
        cols.append(by_partition(inputs["hg_norm_g_2"][layer]))
    arrays["vecs"] = np.ascontiguousarray(np.concatenate(cols, 1))
    at["vecs"] = {"pool_scale": 0, "hg_lb": 8, "second": 16}
    for n in INPUTS:
        a = np.ascontiguousarray(inputs[n])
        arrays[n] = a.reshape(1, -1) if a.ndim == 1 else a
    return arrays, at


def declare(nc, arrays):
    A = {}
    for n, a in arrays.items():
        A[n] = nc.dram_tensor("in_" + n, a.shape, mybir.dt.from_np(a.dtype), kind="ExternalInput").ap()
    A["out"] = nc.dram_tensor("out_0", (1, S, D), F32, kind="ExternalOutput").ap()
    return A


def kernel(**inputs):
    import concourse.bacc as bacc
    from concourse.bass_utils import run_bass_kernel_spmd

    arrays, at = lay_out(inputs)
    plan = {}
    for _ in range(2):
        nc = bacc.Bacc("TRN2", target_bir_lowering=False, num_devices=1)
        plan = write_program(nc, declare(nc, arrays), at, plan)
    got = run_bass_kernel_spmd(nc, [{"in_" + n: a for n, a in arrays.items()}], core_ids=[0])
    return got.results[0]["out_0"]
```
